# Optimizing a Trainium2 kernel written in Bass

```python
import math
import jax, jax.numpy as jnp
from jax import lax
import numpy as np

D_MODEL = 1024
BATCH = 1
SEQ = 256
DEPTH = 2

HEAD_DIM = 64
MIX_WIDTH = D_MODEL
DIFF_WIDTH = MIX_WIDTH // 2
MOBA_WIDTH = MIX_WIDTH - DIFF_WIDTH
DIFF_HEADS = DIFF_WIDTH // (2 * HEAD_DIM)
DIFF_V_DIM = 2 * HEAD_DIM
MOBA_HEADS = MOBA_WIDTH // HEAD_DIM
PROJ_WIDTH = 3 * DIFF_WIDTH + 3 * MOBA_WIDTH
N_BIAS_HEADS = DIFF_HEADS + MOBA_HEADS
D_FF = ((8 * D_MODEL // 3 + 127) // 128) * 128
CONV_WIDTH = 3
DIFF_Q_BLOCK = 128
MOBA_BLOCK = 256
MOBA_TOPK = 3
MOBA_Q_CHUNK = 64
REL_BUCKETS = 32
REL_MAX_EXACT = REL_BUCKETS // 2
REL_MAX_DISTANCE = 1024
NORM_EPS = 1e-6


def rms_norm(x, g):
    xf = x.astype(jnp.float32)
    y = xf * lax.rsqrt(jnp.mean(xf * xf, axis=-1, keepdims=True) + NORM_EPS)
    return (y * g).astype(x.dtype)

def rel_bucket(dist):
    n = jnp.maximum(dist, 0)
    nf = jnp.maximum(n, REL_MAX_EXACT).astype(jnp.float32)
    large = REL_MAX_EXACT + (jnp.log(nf / REL_MAX_EXACT) / math.log(REL_MAX_DISTANCE / REL_MAX_EXACT)
                             * (REL_BUCKETS - REL_MAX_EXACT)).astype(jnp.int32)
    large = jnp.minimum(large, REL_BUCKETS - 1)
    return jnp.where(n < REL_MAX_EXACT, n, large)

def diff_attention(q, k, v, lam, lam_init, sub_g, bias_tab):
    B, S, H = q.shape[:3]
    nqb = S // DIFF_Q_BLOCK
    qb = q.reshape(B, nqb, DIFF_Q_BLOCK, H, 2, HEAD_DIM).transpose(1, 0, 2, 3, 4, 5)
    kpos = jnp.arange(S)
    scale = HEAD_DIM ** -0.5

    def block(args):
        qblk, i = args
        qpos = i * DIFF_Q_BLOCK + jnp.arange(DIFF_Q_BLOCK)
        dist = qpos[:, None] - kpos[None, :]
        bias = jnp.moveaxis(bias_tab[rel_bucket(dist)], -1, 0)
        logits = jnp.einsum('bqhmd,bkhmd->bmhqk', qblk, k).astype(jnp.float32) * scale + bias
        logits = jnp.where(dist >= 0, logits, -jnp.inf)
        p = jax.nn.softmax(logits, axis=-1)
        a = p[:, 0] - lam * p[:, 1]
        return jnp.einsum('bhqk,bkhe->bqhe', a.astype(v.dtype), v)

    out = lax.map(block, (qb, jnp.arange(nqb)))
    out = out.transpose(1, 0, 2, 3, 4).reshape(B, S, H, DIFF_V_DIM)
    out = rms_norm(out, sub_g) * (1.0 - lam_init)
    return out.reshape(B, S, H * DIFF_V_DIM)

def moba_attention(q, k, v, bias_tab):
    B, S, H, D = q.shape
    nb = -(-S // MOBA_BLOCK)
    pad = nb * MOBA_BLOCK - S
    padw = ((0, 0), (0, pad), (0, 0), (0, 0))
    kb = jnp.pad(k, padw).reshape(B, nb, MOBA_BLOCK, H, D).transpose(0, 3, 1, 2, 4)
    vb = jnp.pad(v, padw).reshape(B, nb, MOBA_BLOCK, H, D).transpose(0, 3, 1, 2, 4)
    kmean = jnp.mean(kb.astype(jnp.float32), axis=3)
    gate = jnp.einsum('bshd,bhnd->bhsn', q.astype(jnp.float32), kmean)
    past = jnp.arange(nb)[None, :] < (jnp.arange(S) // MOBA_BLOCK)[:, None]
    gate = jnp.where(past, gate, -jnp.inf)
    topk = min(MOBA_TOPK, nb)
    sel_score, sel_idx = lax.top_k(gate, topk)
    sel_valid = jnp.isfinite(sel_score)

    nc = S // MOBA_Q_CHUNK
    qc = q.reshape(B, nc, MOBA_Q_CHUNK, H, D).transpose(1, 0, 3, 2, 4)
    idx_c = sel_idx.reshape(B, H, nc, MOBA_Q_CHUNK, topk).transpose(2, 0, 1, 3, 4)
    val_c = sel_valid.reshape(B, H, nc, MOBA_Q_CHUNK, topk).transpose(2, 0, 1, 3, 4)
    bi = jnp.arange(B)[:, None, None, None]
    hi = jnp.arange(H)[None, :, None, None]
    hi5 = jnp.arange(H)[None, :, None, None, None]
    tab_h = bias_tab.T
    j = jnp.arange(MOBA_BLOCK)
    scale = D ** -0.5
    n_sel = topk * MOBA_BLOCK

    def chunk(args):
        qch, idx, valid, c = args
        qpos = c * MOBA_Q_CHUNK + jnp.arange(MOBA_Q_CHUNK)
        gk = kb[bi, hi, idx]
        gv = vb[bi, hi, idx]
        dist_p = qpos[None, None, :, None, None] - (idx[..., None] * MOBA_BLOCK + j)
        bias_p = tab_h[hi5, rel_bucket(dist_p)]
        lp = jnp.einsum('bhqd,bhqnjd->bhqnj', qch, gk).astype(jnp.float32) * scale + bias_p
        lp = jnp.where(valid[..., None], lp, -jnp.inf).reshape(B, H, MOBA_Q_CHUNK, n_sel)
        ob = (c * MOBA_Q_CHUNK) // MOBA_BLOCK
        ko = lax.dynamic_index_in_dim(kb, ob, axis=2, keepdims=False)
        vo = lax.dynamic_index_in_dim(vb, ob, axis=2, keepdims=False)
        dist_o = qpos[:, None] - (ob * MOBA_BLOCK + j)[None, :]
        bias_o = tab_h[:, rel_bucket(dist_o)]
        lo = jnp.einsum('bhqd,bhjd->bhqj', qch, ko).astype(jnp.float32) * scale + bias_o
        lo = jnp.where(dist_o >= 0, lo, -jnp.inf)
        p = jax.nn.softmax(jnp.concatenate([lp, lo], axis=-1), axis=-1).astype(v.dtype)
        pp = p[..., :n_sel].reshape(B, H, MOBA_Q_CHUNK, topk, MOBA_BLOCK)
        po = p[..., n_sel:]
        return (jnp.einsum('bhqnj,bhqnje->bhqe', pp, gv)
                + jnp.einsum('bhqj,bhje->bhqe', po, vo))

    out = lax.map(chunk, (qc, idx_c, val_c, jnp.arange(nc)))
    return out.transpose(1, 0, 3, 2, 4).reshape(B, S, H * D)

def causal_dwconv(u, w, b):
    C = u.shape[-1]
    y = lax.conv_general_dilated(u, w[:, None, :], window_strides=(1,),
                                 padding=[(CONV_WIDTH - 1, 0)],
                                 dimension_numbers=('NWC', 'WIO', 'NWC'),
                                 feature_group_count=C)
    return y + b

def conv_ffn(h, w_up, conv_w, conv_b, w_down):
    u = causal_dwconv(h @ w_up, conv_w, conv_b)
    g, up = jnp.split(u, 2, axis=-1)
    return (jax.nn.silu(g) * up) @ w_down

def first_inputs(seed: int = 0) -> dict:
    key = jax.random.key(seed)
    ks = jax.random.split(key, 14)
    f32 = jnp.float32
    nrm = lambda k, s: jax.random.normal(k, s, f32)
    resid = (2 * DEPTH) ** -0.5
    return {
        'x': nrm(ks[0], (BATCH, SEQ, D_MODEL)),
        'ln_attn_g': 1.0 + 0.02 * nrm(ks[1], (DEPTH, D_MODEL)),
        'w_in': nrm(ks[2], (DEPTH, D_MODEL, PROJ_WIDTH)) * D_MODEL ** -0.5,
        'qk_norm_g': 1.0 + 0.02 * nrm(ks[3], (DEPTH, 4, HEAD_DIM)),
        'diff_lambda': 0.1 * nrm(ks[4], (DEPTH, 4, HEAD_DIM)),
        'diff_subln_g': 1.0 + 0.02 * nrm(ks[5], (DEPTH, DIFF_V_DIM)),
        'w_out': nrm(ks[6], (DEPTH, MIX_WIDTH, D_MODEL)) * MIX_WIDTH ** -0.5 * resid,
        'ln_ffn_g': 1.0 + 0.02 * nrm(ks[7], (DEPTH, D_MODEL)),
        'w_up': nrm(ks[8], (DEPTH, D_MODEL, 2 * D_FF)) * D_MODEL ** -0.5,
        'conv_w': nrm(ks[9], (DEPTH, CONV_WIDTH, 2 * D_FF)) * CONV_WIDTH ** -0.5,
        'conv_b': 0.02 * nrm(ks[10], (DEPTH, 2 * D_FF)),
        'w_down': nrm(ks[11], (DEPTH, D_FF, D_MODEL)) * D_FF ** -0.5 * resid,
        'rel_bias': 0.5 * nrm(ks[12], (REL_BUCKETS, N_BIAS_HEADS)),
    }

def first_block(x, ln_attn_g, w_in, qk_norm_g, diff_lambda, diff_subln_g, w_out,
              ln_ffn_g, w_up, conv_w, conv_b, w_down, rel_bias):
    B, S = x.shape[:2]
    cuts = [DIFF_WIDTH, 2 * DIFF_WIDTH, 3 * DIFF_WIDTH,
            3 * DIFF_WIDTH + MOBA_WIDTH, 3 * DIFF_WIDTH + 2 * MOBA_WIDTH]
    bias_diff = rel_bias[:, :DIFF_HEADS]
    bias_moba = rel_bias[:, DIFF_HEADS:]
    for i in range(DEPTH):
        lam_init = 0.8 - 0.6 * math.exp(-0.3 * i)
        h = rms_norm(x, ln_attn_g[i])
        dq, dk, dv, mq, mk, mv = jnp.split(h @ w_in[i], cuts, axis=-1)
        dq = rms_norm(dq.reshape(B, S, DIFF_HEADS, 2, HEAD_DIM), qk_norm_g[i, 0])
        dk = rms_norm(dk.reshape(B, S, DIFF_HEADS, 2, HEAD_DIM), qk_norm_g[i, 1])
        dv = dv.reshape(B, S, DIFF_HEADS, DIFF_V_DIM)
        lf = diff_lambda[i].astype(jnp.float32)
        lam = jnp.exp(jnp.sum(lf[0] * lf[1])) - jnp.exp(jnp.sum(lf[2] * lf[3])) + lam_init
        y_diff = diff_attention(dq, dk, dv, lam, lam_init, diff_subln_g[i], bias_diff)
        mq = rms_norm(mq.reshape(B, S, MOBA_HEADS, HEAD_DIM), qk_norm_g[i, 2])
        mk = rms_norm(mk.reshape(B, S, MOBA_HEADS, HEAD_DIM), qk_norm_g[i, 3])
        mv = mv.reshape(B, S, MOBA_HEADS, HEAD_DIM)
        y_moba = moba_attention(mq, mk, mv, bias_moba)
        x = x + jnp.concatenate([y_diff, y_moba], axis=-1) @ w_out[i]
        x = x + conv_ffn(rms_norm(x, ln_ffn_g[i]), w_up[i], conv_w[i], conv_b[i], w_down[i])
    return x


GRID_W = 64
CTX_LEN = 256
CONV_W = 1024
CONV_K = 3
N_HEADS = 8
N_KV_HEADS = 2
HEAD_DIM_2 = 128
GROUP = N_HEADS // N_KV_HEADS
Q_BLOCK = 128
ROPE_THETA = 10000.0
ROPE_AXIS_DIM = HEAD_DIM_2 // 2
ROPE_PAIRS = ROPE_AXIS_DIM // 2
ATTN_SCALE = HEAD_DIM_2 ** -0.5
GLA_HEADS = 4
GLA_DK = D_MODEL // 2
GLA_DV = D_MODEL
GLA_DKH = GLA_DK // GLA_HEADS
GLA_DVH = GLA_DV // GLA_HEADS
GLA_RANK = 16
GLA_TAU = 16.0
GLA_CHUNK = 64
N_BRANCH = 3
EPS = 1e-6

IN_SPLITS = (CONV_W, CONV_W, CONV_W, CONV_W,
             N_HEADS * HEAD_DIM_2, N_KV_HEADS * HEAD_DIM_2, N_KV_HEADS * HEAD_DIM_2,
             N_HEADS * HEAD_DIM_2,
             GLA_DK, GLA_DK, GLA_DV, GLA_RANK, GLA_RANK, GLA_DV,
             N_BRANCH * D_MODEL)
IN_WIDTH = sum(IN_SPLITS)


def _rmsnorm(x, g):
    xf = x.astype(jnp.float32)
    y = xf * lax.rsqrt(jnp.mean(xf * xf, axis=-1, keepdims=True) + EPS)
    return (y * g.astype(jnp.float32)).astype(x.dtype)

def _split_proj(p):
    offsets = np.cumsum(IN_SPLITS)[:-1].tolist()
    return jnp.split(p, offsets, axis=-1)

def _short_conv(u, w):
    up = jnp.pad(u, ((0, 0), (1, 1), (0, 0)))
    return w[0] * up[:, :-2] + w[1] * up[:, 1:-1] + w[2] * up[:, 2:]

def _axial_rope_tables(n_tokens):
    n_rows = n_tokens // GRID_W
    row = jnp.repeat(jnp.arange(n_rows, dtype=jnp.float32), GRID_W)
    col = jnp.tile(jnp.arange(GRID_W, dtype=jnp.float32), n_rows)
    freqs = ROPE_THETA ** (-jnp.arange(ROPE_PAIRS, dtype=jnp.float32) * 2.0 / ROPE_AXIS_DIM)
    ang = jnp.stack([row[:, None] * freqs, col[:, None] * freqs], axis=1)
    return jnp.cos(ang), jnp.sin(ang)

def _apply_rope(x, cos, sin):
    b_, t_, h_, _ = x.shape
    xr = x.reshape(b_, t_, h_, 2, 2, ROPE_PAIRS)
    x1, x2 = xr[..., 0, :], xr[..., 1, :]
    c_, s_ = cos[None, :, None], sin[None, :, None]
    out = jnp.stack([x1 * c_ - x2 * s_, x2 * c_ + x1 * s_], axis=-2)
    return out.reshape(b_, t_, h_, HEAD_DIM_2).astype(x.dtype)

def _attn_heads(q, k, v, q_g, k_g, rope):
    b_, t_ = q.shape[:2]
    q = _rmsnorm(q.reshape(b_, t_, N_HEADS, HEAD_DIM_2), q_g)
    k = _rmsnorm(k.reshape(b_, t_, N_KV_HEADS, HEAD_DIM_2), k_g)
    v = v.reshape(b_, t_, N_KV_HEADS, HEAD_DIM_2)
    if rope is not None:
        q = _apply_rope(q, *rope)
        k = _apply_rope(k, *rope)
    return q, k, v

def _sdpa_blocks(q, keys, vals):
    b_, t_ = q.shape[:2]
    nb = t_ // Q_BLOCK
    qb = q.reshape(b_, nb, Q_BLOCK, N_KV_HEADS, GROUP, HEAD_DIM_2).transpose(1, 0, 2, 3, 4, 5)

    def one_block(qblk):
        s = jnp.einsum('bqkgd,bskd->bkgqs', qblk, keys).astype(jnp.float32) * ATTN_SCALE
        p = jax.nn.softmax(s, axis=-1).astype(vals.dtype)
        return jnp.einsum('bkgqs,bskd->bqkgd', p, vals)

    o = lax.map(one_block, qb)
    return o.transpose(1, 0, 2, 3, 4, 5).reshape(b_, t_, N_HEADS * HEAD_DIM_2)

def _gla_inputs(q, k, v, r_f, r_b, w_df, b_df, w_db, b_db):
    b_, t_ = q.shape[:2]
    q = q.reshape(b_, t_, GLA_HEADS, GLA_DKH) * (GLA_DKH ** -0.5)
    k = k.reshape(b_, t_, GLA_HEADS, GLA_DKH)
    v = v.reshape(b_, t_, GLA_HEADS, GLA_DVH)
    la_f = (jax.nn.log_sigmoid((r_f @ w_df + b_df).astype(jnp.float32)) / GLA_TAU).reshape(b_, t_, GLA_HEADS, GLA_DKH)
    la_b = (jax.nn.log_sigmoid((r_b @ w_db + b_db).astype(jnp.float32)) / GLA_TAU).reshape(b_, t_, GLA_HEADS, GLA_DKH)
    return q, k, v, la_f, la_b

def _gla_scan(q, k, v, log_a, s0):
    b_, t_, h_, _ = q.shape
    dv = v.shape[-1]
    nc = t_ // GLA_CHUNK

    def chunks(a):
        return a.astype(jnp.float32).reshape(b_, nc, GLA_CHUNK, h_, a.shape[-1]).transpose(1, 0, 3, 2, 4)

    mask = jnp.tril(jnp.ones((GLA_CHUNK, GLA_CHUNK), dtype=bool))

    def step(s, inp):
        qc, kc, vc, ac = inp
        bcum = jnp.cumsum(ac, axis=2)
        o_inter = jnp.einsum('bhtd,bhde->bhte', qc * jnp.exp(bcum), s)
        diff = bcum[:, :, :, None, :] - bcum[:, :, None, :, :]
        decay = jnp.exp(jnp.where(mask[:, :, None], diff, -jnp.inf))
        att = jnp.einsum('bhtd,bhsd,bhtsd->bhts', qc, kc, decay)
        o_intra = jnp.einsum('bhts,bhse->bhte', att, vc)
        b_last = bcum[:, :, -1:, :]
        s_new = jnp.exp(b_last[:, :, 0, :])[..., None] * s + jnp.einsum('bhsd,bhse->bhde', kc * jnp.exp(b_last - bcum), vc)
        return s_new, o_inter + o_intra

    s_f, o = lax.scan(step, s0, (chunks(q), chunks(k), chunks(v), chunks(log_a)))
    o = o.transpose(1, 0, 3, 2, 4).reshape(b_, t_, h_, dv)
    return o.astype(v.dtype), s_f

def _flip(a):
    return jnp.flip(a, axis=1)

def _gla_bidirectional(ctx_in, lat_in):
    qc, kc, vc, lfc, lbc = ctx_in
    ql, kl, vl, lfl, lbl = lat_in
    s0 = jnp.zeros((qc.shape[0], GLA_HEADS, GLA_DKH, GLA_DVH), jnp.float32)
    o_cf, s_f = _gla_scan(qc, kc, vc, lfc, s0)
    o_cb, s_b = _gla_scan(_flip(qc), _flip(kc), _flip(vc), _flip(lbc), s0)
    o_lf, _ = _gla_scan(ql, kl, vl, lfl, s_f)
    o_lb, _ = _gla_scan(_flip(ql), _flip(kl), _flip(vl), _flip(lbl), s_b)
    return o_lf + _flip(o_lb), o_cf + _flip(o_cb)

def _mixer_output(parts, att_o, gla_o, conv_w_l, gla_g_l, w_br_conv_l, w_br_attn_l, w_br_gla_l, b_gate_l, w_out_l):
    a_b, a_c, a_x, a_z = parts[0], parts[1], parts[2], parts[3]
    z_attn, z_gla, mg = parts[7], parts[13], parts[14]
    b_, t_ = a_b.shape[:2]
    br_a = ((a_b * _short_conv(a_c * a_x, conv_w_l)) * jax.nn.silu(a_z)) @ w_br_conv_l
    br_b = (att_o * jax.nn.silu(z_attn)) @ w_br_attn_l
    br_c = (_rmsnorm(gla_o, gla_g_l).reshape(b_, t_, GLA_DV) * jax.nn.silu(z_gla)) @ w_br_gla_l
    g_a, g_b, g_c = jnp.split(jax.nn.sigmoid(mg + b_gate_l), N_BRANCH, axis=-1)
    return (g_a * br_a + g_b * br_b + g_c * br_c) @ w_out_l

def second_inputs(seed: int = 0) -> dict:
    key = jax.random.key(seed)
    ks = jax.random.split(key, 24)
    n = jax.random.normal
    f32 = jnp.float32
    return {
        "x": n(ks[0], (BATCH, SEQ, D_MODEL), f32),
        "c": n(ks[1], (BATCH, D_MODEL), f32),
        "ctx": n(ks[2], (BATCH, CTX_LEN, D_MODEL), f32),
        "c_ctx": n(ks[3], (D_MODEL,), f32),
        "w_ada": n(ks[4], (DEPTH, D_MODEL, 3 * D_MODEL), f32) * D_MODEL ** -0.5,
        "b_ada": 0.02 * n(ks[5], (DEPTH, 3 * D_MODEL), f32),
        "g_pre": 1.0 + 0.02 * n(ks[6], (DEPTH, D_MODEL), f32),
        "g_post": 1.0 + 0.02 * n(ks[7], (DEPTH, D_MODEL), f32),
        "w_in": n(ks[8], (DEPTH, D_MODEL, IN_WIDTH), f32) * D_MODEL ** -0.5,
        "conv_w": n(ks[9], (DEPTH, CONV_K, CONV_W), f32) * CONV_K ** -0.5,
        "q_norm_g": 1.0 + 0.02 * n(ks[10], (DEPTH, HEAD_DIM_2), f32),
        "k_norm_g": 1.0 + 0.02 * n(ks[11], (DEPTH, HEAD_DIM_2), f32),
        "w_decay_fwd": n(ks[12], (DEPTH, GLA_RANK, GLA_DK), f32) * GLA_RANK ** -0.5,
        "b_decay_fwd": 0.01 * n(ks[13], (DEPTH, GLA_DK), f32),
        "w_decay_bwd": n(ks[14], (DEPTH, GLA_RANK, GLA_DK), f32) * GLA_RANK ** -0.5,
        "b_decay_bwd": 0.01 * n(ks[15], (DEPTH, GLA_DK), f32),
        "gla_norm_g": 1.0 + 0.02 * n(ks[16], (DEPTH, GLA_DVH), f32),
        "w_br_conv": n(ks[17], (DEPTH, CONV_W, D_MODEL), f32) * CONV_W ** -0.5,
        "w_br_attn": n(ks[18], (DEPTH, N_HEADS * HEAD_DIM_2, D_MODEL), f32) * (N_HEADS * HEAD_DIM_2) ** -0.5,
        "w_br_gla": n(ks[19], (DEPTH, GLA_DV, D_MODEL), f32) * GLA_DV ** -0.5,
        "b_gate": 0.02 * n(ks[20], (DEPTH, N_BRANCH * D_MODEL), f32),
        "w_out": n(ks[21], (DEPTH, D_MODEL, D_MODEL), f32) * D_MODEL ** -0.5,
    }

def second_block(x, c, ctx, c_ctx, w_ada, b_ada, g_pre, g_post, w_in, conv_w, q_norm_g, k_norm_g,
              w_decay_fwd, b_decay_fwd, w_decay_bwd, b_decay_bwd, gla_norm_g,
              w_br_conv, w_br_attn, w_br_gla, b_gate, w_out):
    n_tok = x.shape[1]
    rope = _axial_rope_tables(n_tok)
    xc = ctx
    for l in range(DEPTH):
        last = l == DEPTH - 1
        mod_l = jax.nn.silu(c) @ w_ada[l] + b_ada[l]
        sh_l, sc_l, gt_l = jnp.split(mod_l[:, None, :], 3, axis=-1)
        mod_c = jax.nn.silu(c_ctx) @ w_ada[l] + b_ada[l]
        sh_c, sc_c, gt_c = jnp.split(mod_c, 3, axis=-1)
        h_l = _rmsnorm(x, g_pre[l]) * (1.0 + sc_l) + sh_l
        h_c = _rmsnorm(xc, g_pre[l]) * (1.0 + sc_c) + sh_c
        pl = _split_proj(h_l @ w_in[l])
        pc = _split_proj(h_c @ w_in[l])
        q_l, k_l, v_l = _attn_heads(pl[4], pl[5], pl[6], q_norm_g[l], k_norm_g[l], rope)
        q_c, k_c, v_c = _attn_heads(pc[4], pc[5], pc[6], q_norm_g[l], k_norm_g[l], None)
        keys = jnp.concatenate([k_l, k_c], axis=1)
        vals = jnp.concatenate([v_l, v_c], axis=1)
        att_l = _sdpa_blocks(q_l, keys, vals)
        dec = (w_decay_fwd[l], b_decay_fwd[l], w_decay_bwd[l], b_decay_bwd[l])
        gla_c_in = _gla_inputs(pc[8], pc[9], pc[10], pc[11], pc[12], *dec)
        gla_l_in = _gla_inputs(pl[8], pl[9], pl[10], pl[11], pl[12], *dec)
        gla_l, gla_c = _gla_bidirectional(gla_c_in, gla_l_in)
        shared = (conv_w[l], gla_norm_g[l], w_br_conv[l], w_br_attn[l], w_br_gla[l], b_gate[l], w_out[l])
        out_l = _mixer_output(pl, att_l, gla_l, *shared)
        if not last:
            att_c = _sdpa_blocks(q_c, k_c, v_c)
            out_c = _mixer_output(pc, att_c, gla_c, *shared)
            xc = xc + gt_c * _rmsnorm(out_c, g_post[l])
        x = x + gt_l * _rmsnorm(out_l, g_post[l])
    return x


def setup_inputs(seed=0):
    out = dict(first_inputs(seed))
    for name, value in second_inputs(seed + 1).items():
        if name != "x":
            out[name + "_2"] = value
    return out


def reference(
    x, ln_attn_g, w_in, qk_norm_g, diff_lambda, diff_subln_g, w_out, ln_ffn_g, w_up, conv_w,
    conv_b, w_down, rel_bias, c_2, ctx_2, c_ctx_2, w_ada_2, b_ada_2, g_pre_2, g_post_2, w_in_2,
    conv_w_2, q_norm_g_2, k_norm_g_2, w_decay_fwd_2, b_decay_fwd_2, w_decay_bwd_2,
    b_decay_bwd_2, gla_norm_g_2, w_br_conv_2, w_br_attn_2, w_br_gla_2, b_gate_2, w_out_2,
):
    x = first_block(
        x, ln_attn_g, w_in, qk_norm_g, diff_lambda, diff_subln_g, w_out, ln_ffn_g, w_up, conv_w,
        conv_b, w_down, rel_bias,
    )
    return second_block(
        x, c_2, ctx_2, c_ctx_2, w_ada_2, b_ada_2, g_pre_2, g_post_2, w_in_2, conv_w_2,
        q_norm_g_2, k_norm_g_2, w_decay_fwd_2, b_decay_fwd_2, w_decay_bwd_2, b_decay_bwd_2,
        gla_norm_g_2, w_br_conv_2, w_br_attn_2, w_br_gla_2, b_gate_2, w_out_2,
    )


_drawn_inputs = setup_inputs


def setup_inputs(seed=0):
    import zlib

    import numpy as np

    out = dict(_drawn_inputs(seed))
    spreads = {}
    factors = {'qk_norm_g': 3.873,
     'diff_subln_g': 4.694,
     'ln_ffn_g': 3.244,
     'conv_b': 3.219,
     'g_post_2': 16.659,
     'q_norm_g_2': 33.803,
     'k_norm_g_2': 30.843,
     'b_decay_fwd_2': 21.482,
     'b_decay_bwd_2': 8.0,
     'gla_norm_g_2': 32.101,
     'b_gate_2': 8.0}
    for name, (base, spread) in spreads.items():
        noise = np.random.default_rng([zlib.crc32(name.encode()), seed]).standard_normal(out[name].shape)
        drawn = base * np.exp(spread * noise) if base else spread * noise
        out[name] = __import__('jax').numpy.asarray(drawn.astype(out[name].dtype))
    for name, factor in factors.items():
        out[name] = (out[name] * factor).astype(out[name].dtype)
    return out
```

```python
import concourse.bass as bass
from concourse import mybir
import math
import numpy as np

F32 = mybir.dt.float32
F32R = mybir.dt.float32r
U8 = mybir.dt.uint8
I32 = mybir.dt.int32
ALU = mybir.AluOpType
ACT = mybir.ActivationFunctionType
AX = mybir.AxisListType
ADD, SUB, MUL, MAX, MIN = ALU.add, ALU.subtract, ALU.mult, ALU.max, ALU.min

EPS = 1e-6
BUCKET_STARTS = list(range(17)) + [21, 27, 35, 46, 59, 77, 99, 128, 166, 216]
FF_TILES = 22
PCOLS = {}
_at = 0
for _name, _n in (("ln_attn", 16), ("ln_ffn", 16), ("qkg", 8), ("subg", 2), ("cw", 2 * 3 * 44), ("cb", 88),
                  ("c", 16), ("b_ada", 48), ("g_pre", 16), ("g_post", 16), ("cw2", 48), ("glag", 4),
                  ("b_gate", 48)):
    PCOLS[_name] = _at
    _at += _n
NPAR = _at
LEVELS = (64, 32, 16, 8, 4, 2, 1)


class Engine:

    def __init__(self, name, sem):
        self.name, self.sem, self.count, self.todo, self.seen = name, sem, 0, [], {}

    def wait(self, *tokens):
        for t in tokens:
            if t is None:
                continue
            sem, value = t
            key = id(sem)
            if self.seen.get(key, 0) < value:
                self.seen[key] = value
                self.todo.append(lambda e, s=sem, v=value: e.wait_ge(s, v))

    def run(self, fn, after=(), inc=True):
        self.wait(*after)
        if inc:
            self.count += 1
            self.todo.append(lambda e, f=fn, s=self.sem: f(e).then_inc(s, 1))
            return (self.sem, self.count)
        self.todo.append(fn)
        return None

    def last(self):
        return (self.sem, self.count) if self.count else None


class Dma:

    def __init__(self, sem):
        self.sem, self.count = sem, 0

    def start(self, eng, out, in_, after=()):
        eng.wait(*after)
        self.count += 16
        eng.todo.append(lambda e, o=out, i=in_, s=self.sem: e.dma_start(o, i).then_inc(s, 16))
        return (self.sem, self.count)


def V(ap, *dims, off=0):
    return bass.AP(ap.tensor, ap.offset + off, [list(ap.ap[0])] + [list(d) for d in dims])


def program(nc, order, A, sems, sb, banks, out):
    PE, AC, DV, PO, SP = (Engine(n, sems[n]) for n in ("pe", "act", "dve", "pool", "sp"))
    used = []

    def act(o, i, func, after=(), scale=1.0, bias=None, accum=None):
        kw = {}
        if bias is not None:
            kw["bias"] = bias
        if accum is not None:
            kw["accum_out"] = accum
        return AC.run(lambda e: e.activation(o, i, func, scale=scale, **kw), after)

    def tt(E, o, a, b, op, after=()):
        return E.run(lambda e: e.tensor_tensor(o, a, b, op), after)

    def ts(E, o, a, s1, s2, op0, op1, after=()):
        if op1 is None:
            return E.run(lambda e: e.tensor_scalar(o, a, s1, None, op0), after)
        return E.run(lambda e: e.tensor_scalar(o, a, s1, s2, op0, op1), after)

    def stt(o, a, s, b, op0, op1, after=()):
        return DV.run(lambda e: e.scalar_tensor_tensor(out=o, in0=a, scalar=s, in1=b, op0=op0, op1=op1), after)

    def copy(E, o, i, after=()):
        return E.run(lambda e: e.tensor_copy(o, i), after)

    def red(o, i, op, after=(), negate=None):
        return DV.run(lambda e: e.tensor_reduce(out=o, in_=i, axis=AX.X, op=op, negate=negate), after)

    def mm(o, l, r, start, stop, after=(), inc=False):
        return PE.run(lambda e: e.matmul(o, l, r, start=start, stop=stop), after, inc)

    def tp(o, i, ident, after=(), inc=False):
        return PE.run(lambda e: e.transpose(o, i, ident), after, inc)

    def fence():
        return [e.last() for e in (PE, AC, DV, PO)]

    free = [[] for _ in range(8)]

    class Ring:
        def __init__(self, ids):
            self.ids, self.at = ids, 0

        def get(self):
            b = self.ids[self.at % len(self.ids)]
            self.at += 1
            assert free[b] is not None, "bank still held"
            toks, free[b] = free[b], None
            return b, banks[b], toks

    def let(b, *toks):
        free[b] = list(toks)

    NR, NS = 5, 4
    raw_free = [[] for _ in range(NR)]
    spl_free = [[] for _ in range(NS)]
    raw_dma = [Dma(sems[f"raw{i}"]) for i in range(NR)]
    st = {"load": 0, "split": 0, "get": 0, "nsplit": 0}
    loaded, ready, done_raw = {}, {}, set()

    def load_upto(n):
        while order is not None and st["load"] <= n and st["load"] < len(order):
            u = st["load"]
            if u >= NR and u - NR not in done_raw:
                return
            name, idx, cols, kind = order[u]
            s = u % NR
            loaded[u] = raw_dma[s].start(SP, sb["RAW"][:, s, 0:cols], A[name][idx, :, 0:cols], raw_free[s])
            st["load"] += 1

    def split_upto(n):
        while order is not None and st["split"] <= n and st["split"] < len(order):
            u = st["split"]
            load_upto(u + NR - 1)
            if u not in loaded:
                return
            name, idx, cols, kind = order[u]
            s = u % NR
            raw = sb["RAW"][:, s, 0:cols]
            if kind == "raw":
                ready[u] = (raw, None, s, None, [loaded[u]])
            else:
                k = st["nsplit"]
                st["nsplit"] += 1
                q = k % NS
                hi, lo = sb["SPH"][:, q, 0:cols], sb["SPL"][:, q, 0:cols]
                t1 = act(hi, raw, ACT.Copy, [loaded[u]] + spl_free[q])
                eng = PO if k % 4 == 3 else DV
                t2 = tt(eng, lo, raw, hi.bitcast(F32), SUB, [loaded[u], t1] + spl_free[q])
                raw_free[s] = [t1, t2]
                done_raw.add(u)
                ready[u] = (hi, lo, None, q, [t1, t2])
            st["split"] += 1

    def get_w(name, idx, cols=1024, kind="split"):
        used.append((name, idx, cols, kind))
        u = st["get"]
        st["get"] += 1
        if order is None:
            if kind == "raw":
                return sb["RAW"][:, 0, 0:cols], None, []
            return sb["SPH"][:, 0, 0:cols], sb["SPL"][:, 0, 0:cols], []
        assert order[u] == (name, idx, cols, kind)
        split_upto(u + NS - 1)
        hi, lo, s, q, toks = ready[u]
        return hi, lo, toks

    def put_w(tok):
        if order is None:
            return
        u = st["get"] - 1
        _, _, s, q, _ = ready.pop(u)
        if s is not None:
            raw_free[s] = [tok]
            done_raw.add(u)
        else:
            spl_free[q] = [tok]

    cdma = Dma(sems["cst"])

    def cload(o, i, after=()):
        return cdma.start(AC, o, i, after)
    cload(sb["IDENT"][:, :], A["ident"])
    cload(sb["PAR"][:, :], A["par"])
    cload(sb["TRI"][:, :], A["tri"])
    cload(sb["MASKF"][:, :], A["mask"])
    cload(sb["OH"][0:32, 0:384], A["onehot"])
    cload(sb["RB"][0:32, 0:12], A["rel_bias"])
    cload(sb["MROW"][0:12, 0:384], A["maskrow"])
    cload(sb["LAMR"][:, :], A["lamr"])
    for t in range(2):
        T_const = cload(sb["XS"][:, t, :], A["x"][0, t * 128:(t + 1) * 128, :])
    IDENT = sb["IDENT"][:, :]
    t_mask = copy(DV, sb["MASK"][:, :], sb["MASKF"][:, :], [T_const])
    t_one = DV.run(lambda e: e.memset(sb["ONE"][:, :], 1.0))

    def par(name, i=0, n=1):
        c = PCOLS[name] + i
        return sb["PAR"][:, c:c + n]

    def rsqrt(dst, ss, inv, n, after=()):
        w = sb["RS"]
        xh, y, t = w[:, 0, 0:n], w[:, 1, 0:n], w[:, 2, 0:n]
        k = ts(DV, xh, ss, inv, EPS, MUL, ADD, after)
        k = ts(DV, t.bitcast(I32), xh.bitcast(I32), 1, None, ALU.logical_shift_right, None, [k])
        k = ts(DV, y.bitcast(I32), t.bitcast(I32), -1.0, float(0x5f3759df), MUL, ADD, [k])
        for i in range(3):
            k = tt(DV, t, y, y, MUL, [k])
            k = stt(t, t, -0.5, xh, MUL, MUL, [k])
            k = stt(dst if i == 2 else y, t, 1.5, y, ADD, MUL, [k])
        return k

    def norm_T(tiles, XN, ring, gain, after):
        nt = len(tiles)
        ss, rs = sb["SS"][:, 0:nt], sb["SS"][:, 4:4 + nt]
        k = None
        for i, t in enumerate(tiles):
            k = act(XN[:, i, :], sb["XS"][:, t, :], ACT.Square, after, accum=sb["SS"][:, i:i + 1])
        k = rsqrt(rs, ss, 1.0 / 1024, nt, [k])
        xt = []
        for i, t in enumerate(tiles):
            E = DV if i % 2 == 0 else PO
            xt.append(ts(E, XN[:, i, :], sb["XS"][:, t, :], sb["SS"][:, 4 + i:5 + i], None, MUL, None, [k]))
        done = []
        for kt in range(8):
            b, P, fr = ring.get()
            for i in range(nt):
                tk = tp(P[:, i * 128:(i + 1) * 128], XN[:, i, kt * 128:(kt + 1) * 128], IDENT,
                        fr + [xt[i], T_const], inc=i == nt - 1)
            done += gain(kt, b, P, tk)
        return done

    HH, HL = sb["HTH"], sb["HTL"]

    def group_T(P, col, hi, lo, n0, n1, after, xh=None, xl=None):
        xh, xl = xh or HH, xl or HL
        wh, wl = (a.rearrange("p (k c) -> p k c", k=8) for a in (hi, lo))
        o = P[:, col:col + n1 - n0]
        PE.wait(*after)
        for kt in range(8):
            mm(o, wh[:, kt, :], xh[:, kt, n0:n1], kt == 0, False)
            mm(o, wh[:, kt, :], xl[:, kt, n0:n1], False, False)
            tk = mm(o, wl[:, kt, :], xh[:, kt, n0:n1], False, kt == 7, inc=kt == 7)
        return tk

    def group_N(name, g, tiles, ring, hdone, units=4, xh=None, xl=None):
        xh, xl = xh or HH, xl or HL
        got = [ring.get() for _ in tiles]
        for u in range(units):
            hi, lo, wt = get_w(name, g * units + u)
            wh, wl = (a.rearrange("p (k c) -> p k c", k=2) for a in (hi, lo))
            PE.wait(*wt, *hdone)
            for i, t in enumerate(tiles):
                b, P, fr = got[i]
                PE.wait(*fr)
                for j in range(2):
                    kt = 2 * u + j
                    s = slice(t * 128, (t + 1) * 128)
                    mm(P[:, :], xh[:, kt, s], wh[:, j, :], kt == 0, False)
                    mm(P[:, :], xl[:, kt, s], wh[:, j, :], False, False)
                    tk = mm(P[:, :], xh[:, kt, s], wl[:, j, :], False, kt == 2 * units - 1, inc=j == 1)
            put_w(tk)
        n = len(tiles)
        return [(got[i][0], got[i][1], (tk[0], tk[1] - (n - 1 - i))) for i in range(n)]

    def drain(g):
        for _ in g:
            pass

    def weave(main, side, ratio=1):
        live = True
        acc = 0.0
        for _ in main:
            acc += ratio
            while live and acc >= 1:
                acc -= 1
                try:
                    next(side)
                except StopIteration:
                    live = False
        if live:
            drain(side)

    lo4, hi4 = Ring([0, 1, 2, 3]), Ring([4, 5, 6, 7])
    all8 = Ring(list(range(8)))

    b, P, fr = hi4.get()
    tk = mm(P[0:12, 0:384], sb["RB"][0:32, 0:12], sb["OH"][0:32, 0:384], True, True, [T_const], inc=True)
    t1 = tt(DV, sb["RROW"][0:12, :], P[0:12, 0:384], sb["MROW"][0:12, 0:384], ADD, [tk, T_const])
    let(b, t1)
    rd = Dma(sems["bias"])
    tr = rd.start(AC, A["rscr"], V(sb["RROW"][0:12, :], [0, 128], [1, 384]), [t1])
    src = A["rscr"]
    BIAS = sb["BIAS"]
    for part in range(3):
        o = 128 if part == 0 else (part - 1) * 128
        t_bias = rd.start(AC, BIAS[:, :, part * 128:(part + 1) * 128],
                          bass.AP(src.tensor, src.offset + 127 + o, [[383, 128], [128 * 384, 12], [1, 128]]), [tr])

    def ada_gen(ring, t0):
        c, cs = par("c", 0, 16), sb["CS"]
        k = act(cs[:, 0, :], c, ACT.Tanh, [t0], scale=0.5)
        k = stt(cs[:, 1, :], cs[:, 0, :], 1.0, c, ADD, MUL, [k])
        k = ts(DV, cs[:, 1, :], cs[:, 1, :], 0.5, None, MUL, None, [k])
        rhs = cs[:, 1, :].rearrange("p (k s) -> p k s", s=2)
        for l in range(2):
            b, P, fr = ring.get()
            for ft in range(24):
                w, _, wt = get_w("w_ada", l * 24 + ft, kind="raw")
                wv = w.rearrange("p (k c) -> p k c", k=8)
                PE.wait(k, *wt, *fr)
                for kt in range(8):
                    tk = mm(P[:, 2 * ft:2 * ft + 2], wv[:, kt, :], rhs[:, kt, :], kt == 0, kt == 7, inc=kt == 7)
                put_w(tk)
                yield
            MT = sb["MODT"]
            ba = par("b_ada", l * 24, 24)
            t = tt(DV, MT[:, l, :, :], P[:, 0:48].rearrange("p (f s) -> p f s", s=2),
                   V(ba, [1, 24], [0, 2]), ADD, [tk])
            let(b, t)
            mod_done.append(t)
            gp = par("g_pre", l * 8, 8)
            mod_done.append(stt(sb["GP"][:, l, :, :], MT[:, l, 8:16, :], 1.0, V(gp, [1, 8], [0, 2]), ADD, MUL, [t]))
    mod_done = []

    QKT, VN, YN, QKN = sb["QKT"], sb["VN"], sb["YN"], sb["QKN"]
    x_done = [T_const]
    for l in range(2):
        lam_init = 0.8 - 0.6 * math.exp(-0.3 * l)
        sm = sb["SM"]
        lr = sb["LAMR"]
        k = []
        for j in range(2):
            a0 = (l * 4 + 2 * j) * 64
            k1 = tt(DV, sb["LT"][:, 0:64], lr[:, a0:a0 + 64], lr[:, a0 + 64:a0 + 128], MUL, [T_const, DV.last()])
            k2 = red(sm[:, j:j + 1], sb["LT"][:, 0:64], ADD, [k1])
            k.append(act(sm[:, 2 + j:3 + j], sm[:, j:j + 1], ACT.Exp, [k2]))
        k1 = tt(DV, sm[:, 4:5], sm[:, 3:4], sm[:, 2:3], SUB, k)
        t_lam = ts(DV, sm[:, 5:6], sm[:, 4:5], -lam_init, None, ADD, None, [k1])
        ts(DV, sm[:, 6:7], par("qkg", l * 4), 0.125, None, MUL, None, [T_const])
        ts(DV, sm[:, 7:8], par("qkg", l * 4 + 2), 0.125, None, MUL, None)
        t_cols = ts(DV, sm[:, 8:9], par("subg", l), 1.0 - lam_init, None, MUL, None)

        def gain1(name):
            def f(kt, b, P, tk):
                g = par(name, l * 8 + kt)
                a = act(HH[:, kt, 0:256], P[:, 0:256], ACT.Copy, [tk], scale=g)
                d = stt(HL[:, kt, 0:256], P[:, 0:256], g, HH[:, kt, 0:256].bitcast(F32), MUL, SUB, [a])
                let(b, d)
                return [a, d]
            return f
        hd = norm_T((0, 1), sb["XN1"], all8, gain1("ln_attn"), x_done + fence())

        qk_done, v_done = {}, {}
        pend = None

        def qk_finish(sec, kn):
            for half in range(2):
                b, P, fr = all8.get()
                PE.wait(*fr)
                for f in range(2):
                    for t in range(2):
                        ft = half * 2 + f
                        tk = tp(P[:, (f * 2 + t) * 128:(f * 2 + t + 1) * 128],
                                QKN[:, sec % 2, t, ft * 128:(ft + 1) * 128], IDENT, [kn[t]], inc=f == 1 and t == 1)
                base = {0: 0, 1: 4, 3: 8, 4: 12}[sec] + half * 2
                g = {0: sm[:, 6:7], 1: par("qkg", l * 4 + 1), 3: sm[:, 7:8], 4: par("qkg", l * 4 + 3)}[sec]
                o = QKT[:, base:base + 2, :].rearrange("p a b -> p (a b)")
                t = act(o, P[:, :], ACT.Copy, [tk, t_cols], scale=g)
                let(b, t)
                qk_done[(sec, half)] = t
        for sec in range(6):
            got = group_N(f"w_in{l}", sec, (0, 1), all8, hd)
            if pend is not None:
                qk_finish(*pend)
                pend = None
            if sec in (2, 5):
                for t, (b, P, tk) in enumerate(got):
                    k = act(VN[:, t, (sec == 5) * 512:(sec == 5) * 512 + 512], P[:, :], ACT.Copy, [tk])
                    let(b, k)
                    v_done[(sec, t)] = k
                continue
            ks = []
            for t, (b, P, tk) in enumerate(got):
                k = act(sb["SQ"][:, t, :], P[:, :], ACT.Square, [tk, DV.last()])
                ks.append(red(sb["QS"][:, 0, t * 8:t * 8 + 8], sb["SQ"][:, t, :].rearrange("p (h d) -> p h d", d=64),
                              ADD, [k]))
            k = rsqrt(sb["QS"][:, 1, 0:16], sb["QS"][:, 0, 0:16], 1.0 / 64, 16, ks)
            kn = []
            for t, (b, P, tk) in enumerate(got):
                k2 = tt(DV, QKN[:, sec % 2, t, :].rearrange("p (h d) -> p h d", d=64),
                        P[:, :].rearrange("p (h d) -> p h d", d=64),
                        V(sb["QS"][:, 1, t * 8:t * 8 + 1], [1, 8], [0, 64]), MUL, [k, PE.last()])
                let(b, k2)
                kn.append(k2)
            pend = (sec, kn)

        R = sb["RR"]
        E3, PT = sb["E3"], sb["PT3"]
        e_done, e_free, pt_free = {}, [[] for _ in range(4)], [[], []]
        y_done = []
        sc_ring, tp_ring, pv_ring = Ring([0, 1]), Ring([2, 3]), Ring([4, 5, 6, 7])
        pv = {}

        def scores(u):
            s, fam = u % 8, u // 8
            half, ft = s % 2, s // 2
            hb = s // 2 if fam == 0 else 4 + s
            b, P, fr = sc_ring.get()
            p0 = half * 64
            q = QKT[p0:p0 + 64, fam * 8 + ft, :]
            kk = QKT[p0:p0 + 64, fam * 8 + 4 + ft, :]
            PE.wait(*fr, qk_done[(fam * 3, ft // 2)], qk_done[(fam * 3 + 1, ft // 2)])
            mm(P[:, 0:128], q[:, 0:128], kk[:, 0:128], True, True)
            tk = mm(P[:, 128:384], q[:, 128:256], kk[:, 0:256], True, True, inc=True)
            e = u % 4
            LG = E3[:, e, :]
            k = tt(DV, LG, P[:, 0:384], BIAS[:, hb, :], ADD, [tk, t_bias] + e_free[e])
            let(b, k)
            ka = red(R[:, 0, 2 * u:2 * u + 1], LG[:, 0:128], MAX, [k], negate=True)
            kb = red(R[:, 0, 2 * u + 1:2 * u + 2], LG[:, 128:384], MAX, [k], negate=True)
            act(LG[:, 0:128], LG[:, 0:128], ACT.Exp, [ka], bias=R[:, 0, 2 * u:2 * u + 1],
                accum=R[:, 1, 2 * u:2 * u + 1])
            ke = act(LG[:, 128:384], LG[:, 128:384], ACT.Exp, [kb], bias=R[:, 0, 2 * u + 1:2 * u + 2],
                     accum=R[:, 1, 2 * u + 1:2 * u + 2])
            kr = DV.run(lambda e_: e_.reciprocal(R[:, 2, 2 * u:2 * u + 2], R[:, 1, 2 * u:2 * u + 2]), [ke])
            if fam == 0:
                if half == 0:
                    k = ts(DV, LG[:, 0:128], LG[:, 0:128], R[:, 2, 2 * u:2 * u + 1], None, MUL, None, [kr])
                    k = ts(DV, LG[:, 128:384], LG[:, 128:384], R[:, 2, 2 * u + 1:2 * u + 2], None, MUL, None, [k])
                    e_done[u] = k
                else:
                    kl = tt(DV, R[:, 3, 2 * u:2 * u + 2], R[:, 2, 2 * u:2 * u + 2],
                            V(sm[:, 5:6], [0, 2]), MUL, [kr, t_lam])
                    prev = E3[:, (u - 1) % 4, :]
                    k = stt(LG[:, 0:128], LG[:, 0:128], R[:, 3, 2 * u:2 * u + 1], prev[:, 0:128], MUL, ADD,
                            [kl, e_done[u - 1]])
                    k = stt(LG[:, 128:384], LG[:, 128:384], R[:, 3, 2 * u + 1:2 * u + 2], prev[:, 128:384], MUL, ADD,
                            [k])
                    e_free[(u - 1) % 4] = [k]
                    e_done[u] = k
            else:
                e_done[u] = kr

        def trans(u):
            e = u % 4
            b, P, fr = tp_ring.get()
            PE.wait(*fr, e_done[u])
            for j in range(3):
                tk = tp(P[:, j * 128:(j + 1) * 128], E3[:, e, j * 128:(j + 1) * 128], IDENT, inc=j == 2)
            e_free[e] = [tk]
            w = u % 2
            k = act(PT[:, w, :], P[:, 0:384], ACT.Copy, [tk] + pt_free[w])
            let(b, k)
            pt_done[u] = k
        pt_done = {}

        def values(u):
            w = u % 2
            fam = u // 8
            s = u % 8
            if fam == 0:
                h, dv, per = s // 2, 128, 2
                c0 = h * 128
            else:
                h, dv, per = s, 64, 4
                c0 = 512 + h * 64
            i = h % per
            if i == 0:
                pv[fam] = pv_ring.get()
            b, P, fr = pv[fam]
            PE.wait(*fr, pt_done[u], *v_done.values())
            o = P[:, :].rearrange("p (i t d) -> p i t d", i=per, t=2)
            mm(o[:, i, 0, :], PT[:, w, 0:128], VN[:, 0, c0:c0 + dv], True, True)
            mm(o[:, i, 1, :], PT[:, w, 128:256], VN[:, 0, c0:c0 + dv], True, False)
            tk = mm(o[:, i, 1, :], PT[:, w, 256:384], VN[:, 1, c0:c0 + dv], False, True, inc=True)
            pt_free[w] = [tk]
            if i < per - 1:
                return
            cb = c0 - i * dv
            yo = V(YN[:, 0, cb:cb + 1], [dv, per], [1024, 2], [1, dv])
            if fam == 1:
                r0 = 2 * (u - per + 1)
                k = tt(DV, yo, o, V(R[:, 2, r0:r0 + 1], [2, per], [1, 2], [0, dv]), MUL, [tk])
                let(b, k)
                y_done.append(k)
            else:
                k = act(sb["SQ"][:, 0, :], P[:, :], ACT.Square, [tk, DV.last()])
                k = red(sb["QS"][:, 0, 0:4], sb["SQ"][:, 0, :].rearrange("p (g d) -> p g d", d=128), ADD, [k])
                k = rsqrt(sb["QS"][:, 1, 0:4], sb["QS"][:, 0, 0:4], 1.0 / 128, 4, [k])
                k = tt(DV, yo, o, V(sb["QS"][:, 1, 0:1], [2, per], [1, 2], [0, dv]), MUL, [k])
                let(b, k)
                y_done.append(k)

        def attn1():
            us = [u for u in range(16)]
            tr_ = [u for u in us if u >= 8 or u % 2 == 1]
            ev = []
            for u in us:
                scores(u)
                yield
                if u >= 2 and (u - 2) in tr_:
                    trans(u - 2)
                    yield
                if u >= 3 and (u - 3) in tr_:
                    values(u - 3)
                    yield
            for u in (16, 17, 18):
                if (u - 2) in tr_ and u - 2 < 16:
                    trans(u - 2)
                if (u - 3) in tr_:
                    values(u - 3)
                yield
        if l == 0:
            weave(attn1(), ada_gen(Ring([3]), T_const), 1.5) if False else drain(attn1())
        else:
            drain(attn1())
        yd = []
        for kt2 in range(4):
            b, P, fr = all8.get()
            PE.wait(*fr, *y_done)
            for f in range(2):
                for t in range(2):
                    kt = kt2 * 2 + f
                    tk = tp(P[:, (f * 2 + t) * 128:(f * 2 + t + 1) * 128], YN[:, t, kt * 128:(kt + 1) * 128], IDENT,
                            inc=f == 1 and t == 1)
            oh = HH[:, kt2 * 2:kt2 * 2 + 2, 0:256]
            ol = HL[:, kt2 * 2:kt2 * 2 + 2, 0:256]
            Pv = P[:, :].rearrange("p (f n) -> p f n", f=2)
            g = sm[:, 8:9] if kt2 < 2 else 1.0
            a = act(oh, Pv, ACT.Copy, [tk, t_cols], scale=g)
            d = stt(ol, Pv, g, oh.bitcast(F32), MUL, SUB, [a])
            let(b, d)
            yd += [a, d]
        xd = []
        for g in range(2):
            for t, (b, P, tk) in enumerate(group_N(f"w_out{l}", g, (0, 1), all8, yd)):
                xs = sb["XS"][:, t, g * 512:(g + 1) * 512]
                k = tt(DV, xs, P[:, :], xs, ADD, [tk])
                let(b, k)
                xd.append(k)

        hd = norm_T((0, 1), sb["XN1"], all8, gain1("ln_ffn"), xd)
        up_ring = Ring([0, 1, 2, 3])
        accs = [(i, banks[i], free[i]) for i in (4, 5, 6, 7)]
        for i in (4, 5, 6, 7):
            free[i] = None
        f_free = [[], [], [], []]
        a_free = [[], [], []]
        a_done = {}

        def ff_up(j):
            b, P, fr = up_ring.get()
            for side in range(2):
                hi, lo, wt = get_w(f"w_up{l}", side * FF_TILES + j)
                tk = group_T(P, side * 256, hi, lo, 0, 256, fr + wt + hd)
                put_w(tk)
            i = j % 2
            C = sb["FC"]
            outs = []
            for side in range(2):
                ft = side * FF_TILES + j
                w = [par("cw", (l * 3 + q) * 44 + ft) for q in range(3)]
                c = C[:, i, side, :]
                u = P[:, side * 256:(side + 1) * 256]
                outs.append(act(c, u, ACT.Identity, [tk] + f_free[i], scale=w[2], bias=par("cb", l * 44 + ft)))
            for side in range(2):
                ft = side * FF_TILES + j
                w = [par("cw", (l * 3 + q) * 44 + ft) for q in range(3)]
                c = C[:, i, side, :]
                u = P[:, side * 256:(side + 1) * 256]
                k = stt(c[:, 1:256], u[:, 0:255], w[1], c[:, 1:256], MUL, ADD, [outs[1]])
                k = stt(c[:, 2:256], u[:, 0:254], w[0], c[:, 2:256], MUL, ADD, [k])
                outs[side] = k
            let(b, k)
            th = sb["FT"][:, i, :]
            kt_ = act(th, C[:, i, 0, :], ACT.Tanh, [outs[0]], scale=0.5)
            k = stt(th, th, 1.0, C[:, i, 0, :], ADD, MUL, [kt_])
            k = stt(th, th, 0.5, C[:, i, 1, :], MUL, MUL, [k, outs[1]])
            s = j % 3
            kh = act(sb["AH"][:, s, :], th, ACT.Copy, [k] + a_free[s])
            kl = tt(PO, sb["AL"][:, s, :], th, sb["AH"][:, s, :].bitcast(F32), SUB, [kh] + a_free[s])
            f_free[i] = [k, kh, kl]
            a_done[j] = [kh, kl]

        def ff_down(j):
            hi, lo, wt = get_w(f"w_down{l}", j)
            s = j % 3
            PE.wait(*wt, *a_done[j])
            for t in range(2):
                for g in range(2):
                    b, P, fr = accs[t * 2 + g]
                    PE.wait(*fr)
                    xh, xl = sb["AH"][:, s, t * 128:(t + 1) * 128], sb["AL"][:, s, t * 128:(t + 1) * 128]
                    wh, wl = hi[:, g * 512:(g + 1) * 512], lo[:, g * 512:(g + 1) * 512]
                    mm(P[:, :], xh, wh, j == 0, False)
                    mm(P[:, :], xl, wh, False, False)
                    tk = mm(P[:, :], xh, wl, False, j == FF_TILES - 1, inc=True)
            put_w(tk)
            a_free[s] = [tk]
            return tk
        for j in range(FF_TILES + 2):
            if j < FF_TILES:
                ff_up(j)
            if j >= 2:
                tk = ff_down(j - 2)
        x_done = []
        for t in range(2):
            for g in range(2):
                b, P, _ = accs[t * 2 + g]
                xs = sb["XS"][:, t, g * 512:(g + 1) * 512]
                k = tt(DV, xs, P[:, :], xs, ADD, [tk])
                let(b, k)
                x_done.append(k)

    drain(ada_gen(Ring([3]), T_const))

    F0 = fence()
    xdma = Dma(sems["xs"])
    for t in range(2):
        k = xdma.start(PO, sb["XS"][:, 2 + t, :], A["ctx"][0, t * 128:(t + 1) * 128, :], F0)
    x_done = x_done + [k]
    spill = [Dma(sems["sp0"]), Dma(sems["sp1"])]
    sp_done = [spill[0].start(PO, A["xscr"][0, 0:256, :].rearrange("(t p) d -> p t d", p=128),
                              sb["XS"][:, 0:2, :], x_done)]
    sp_done.append(spill[1].start(PO, A["xscr"][0, 256:512, :].rearrange("(t p) d -> p t d", p=128),
                                  sb["XS"][:, 2:4, :], x_done))
    gdma, tdma, wdma, rdma = Dma(sems["gd"]), Dma(sems["td"]), Dma(sems["wd"]), Dma(sems["rdl"])
    odma = Dma(sems["out"])
    MT, GP = sb["MODT"], sb["GP"]
    ASC = 128 ** -0.5
    for l in range(2):
        last = l == 1
        NT = 256 if last else 512
        streams = (0,) if last else (1, 0)
        F0 = fence()
        tabs = []
        for i, nm in enumerate(("q", "k")):
            tabs.append(tdma.start(PO, sb["GN"][:, i, :], V(A["qkn"][l * 2 + i:l * 2 + i + 1, :], [1, 128])
                                   if False else bass.AP(A["qkn"].tensor, A["qkn"].offset + (l * 2 + i) * 128,
                                                         [[0, 128], [1, 128]]), F0))
            tabs.append(tdma.start(PO, sb["ROPE"][:, i, :, :, :], A["rope"], F0))
        tt_ = tabs[-1]
        k = ts(DV, sb["GN"][:, 0, :], sb["GN"][:, 0, :], ASC, None, MUL, None, [tt_])
        t_rope = []
        for i in range(2):
            g = sb["GN"][:, i, :]
            t_rope.append(tt(DV, sb["ROPE"][:, i, 0, :, :], sb["ROPE"][:, i, 0, :, :],
                             V(g, [0, 2], [1, 128]), MUL, [tt_, k]))
            for t in range(2):
                for hf in range(2):
                    o = V(sb["ROPE"][:, i, 1, t, hf * 32:hf * 32 + 1], [64, 2], [1, 32])
                    t_rope.append(tt(DV, o, o, V(sb["GN"][:, i, (1 - hf) * 32:(1 - hf) * 32 + 1], [64, 2], [1, 32]),
                                     MUL, [tt_, k]))
        t_wd = wdma.start(PO, sb["WDEC"][:, :], A["wdec"][l, :, :], F0)

        def gain2(kt, b, P, tk):
            w = sb["HV"][:, kt % 2, :]
            ds = []
            for s in range(2):
                ds.append(ts(DV, w[:, s * 256:(s + 1) * 256], P[:, s * 256:(s + 1) * 256], GP[:, l, kt, s:s + 1],
                             MT[:, l, kt, s:s + 1], MUL, ADD, [tk] + hv_free[kt % 2] + mod_done))
            let(b, ds[1])
            a = act(HH[:, kt, :], w, ACT.Copy, ds)
            d = tt(PO, HL[:, kt, :], w, HH[:, kt, :].bitcast(F32), SUB, [a])
            hv_free[kt % 2] = [a, d]
            return [a, d]
        hv_free = [[], []]
        hd = norm_T((0, 1, 2, 3), sb["XN2"], all8, gain2, x_done + F0)
        F1 = fence()

        GQ, GK, GV = sb["GQ"], sb["GK"], sb["GV"]
        tiles4 = (0, 1, 2, 3)
        hi, lo, wt = get_w(f"wr{l}", 0, cols=256)
        b, P, fr = all8.get()
        wh, wl = (a.rearrange("p (k c) -> p k c", k=8) for a in (hi, lo))
        PE.wait(*wt, *hd, *fr)
        for t in range(4):
            s = slice(t * 128, (t + 1) * 128)
            for kt in range(8):
                o = P[:, t * 32:(t + 1) * 32]
                mm(o, HH[:, kt, s], wh[:, kt, :], kt == 0, False)
                mm(o, HL[:, kt, s], wh[:, kt, :], False, False)
                tk = mm(o, HH[:, kt, s], wl[:, kt, :], False, kt == 7, inc=kt == 7)
        put_w(tk)
        kr = act(sb["RN"][:, :], P[:, 0:128], ACT.Copy, [tk] + F1)
        let(b, kr)
        k1s = DV.run(lambda e: e.memset(sb["RT"][32:33, :], 1.0), F1)
        for ft in range(4):
            hi, lo, wt = get_w(f"wgk{l}", ft)
            b, P, fr = all8.get()
            tk = group_T(P, 0, hi, lo, 0, 512, fr + wt + hd)
            put_w(tk)
            k = act(GK[:, ft, :], P[:, :], ACT.Copy, [tk] + F1)
            let(b, k)
            gk_done = k
        for ft in range(4):
            hi, lo, wt = get_w(f"wgq{l}", ft)
            b, P, fr = all8.get()
            tk = group_T(P, 0, hi, lo, 0, NT, fr + wt + hd)
            put_w(tk)
            k = act(GQ[:, ft, 0:NT], P[:, 0:NT], ACT.Copy, [tk] + F1, scale=ASC)
            let(b, k)
            gq_done = k
        b, P, fr = all8.get()
        PE.wait(*fr, kr)
        for t in range(4):
            tk = tp(P[0:32, t * 128:(t + 1) * 128], sb["RN"][:, t * 32:(t + 1) * 32], IDENT, inc=t == 3)
        k_rt = act(sb["RT"][0:32, :], P[0:32, :], ACT.Copy, [tk, k1s] + F1)
        let(b, k_rt)
        for g in range(2):
            for t, (b, P, tk) in enumerate(group_N(f"wgv{l}", g, tiles4, all8, hd)):
                k = act(GV[:, t, g * 512:(g + 1) * 512], P[:, :], ACT.Copy, [tk] + F1)
                let(b, k)
                gv_done = k

        def gla(ring):
            LA, E4, B = sb["LA"], sb["E4"], sb["BC"]
            for s in (1, 0):
                full = s in streams
                F = fence() + sp_done
                ks = []
                for t in range(2):
                    for d in range(2):
                        i = t * 2 + d
                        b, P, fr = ring.get()
                        c = s * 256 + t * 128
                        tk = mm(P[:, :], sb["RT"][0:33, c:c + 128], sb["WDEC"][:, d * 512:(d + 1) * 512], True, True,
                                fr + [k_rt, t_wd, k1s], inc=True)
                        ka = act(E4[:, i, :], P[:, :], ACT.Abs, [tk] + F)
                        kb = ts(DV, LA[:, i, :], P[:, :], 0.0, None, MIN, None, [ka] + F)
                        let(b, kb)
                        ks.append((act(E4[:, i, :], E4[:, i, :], ACT.Exp, [ka], scale=-1.0), kb))
                        yield
                la = []
                for i in range(4):
                    k = act(E4[:, i, :], E4[:, i, :], ACT.Ln, [ks[i][0], t_one], bias=sb["ONE"][:, 0:1])
                    la.append(tt(DV, LA[:, i, :], LA[:, i, :], E4[:, i, :], SUB, [k, ks[i][1]]))
                yield
                TRI = sb["TRI"]
                bd = []
                for d in range(2):
                    for hp in range(2):
                        b, P, fr = ring.get()
                        PE.wait(*fr, *la)
                        for hh in range(2):
                            h = hp * 2 + hh
                            o = hh * 256
                            sl = slice(h * 128, (h + 1) * 128)
                            if d == 0:
                                mm(P[:, o:o + 256], LA[:, 0, sl], TRI[:, 0:256], True, False)
                                tk = mm(P[:, o + 128:o + 256], LA[:, 2, sl], TRI[:, 0:128], False, True, inc=True)
                            else:
                                mm(P[:, o:o + 256], LA[:, 3, sl], TRI[:, 128:384], True, False)
                                tk = mm(P[:, o:o + 128], LA[:, 1, sl], TRI[:, 256:384], False, True, inc=True)
                        k = act(B[:, d, hp * 2:hp * 2 + 2, :].rearrange("p h n -> p (h n)"), P[:, :], ACT.Copy, [tk] + F)
                        let(b, k)
                        bd.append(k)
                        yield
                q = GQ[:, :, s * 256:(s + 1) * 256]
                kk = GK[:, :, s * 256:(s + 1) * 256]
                sdone = bd + [gk_done, gq_done, gv_done, la[-1]]
                mi = [0]
                m_free = [F, F]

                def level(d, h):
                    i = mi[0] % 2
                    mi[0] += 1
                    E, M = sb["EB"][:, i, :, :], sb["MB"][:, i, :, :]
                    bv = B[:, d, :, :]
                    nb = 1024 // (2 * h)
                    up = lambda a: V(a, [2 * h, nb], [1, h], off=h)
                    dn = lambda a: V(a, [2 * h, nb], [1, h])
                    upq = lambda a: V(a, [512, 4], [2 * h, 128 // h], [1, h], off=h)
                    dnq = lambda a: V(a, [512, 4], [2 * h, 128 // h], [1, h])
                    up4 = lambda a: V(a, [256, 4], [2 * h, 128 // h], [1, h], off=h)
                    dn4 = lambda a: V(a, [256, 4], [2 * h, 128 // h], [1, h])
                    if d == 0:
                        ref = V(bv, [2 * h, nb], [0, h], off=h - 1)
                        k1 = tt(DV, up(E), up(bv), ref, SUB, m_free[i] + sdone)
                        k2 = tt(DV, dn(E), ref, dn(bv), SUB)
                    else:
                        ref = V(bv, [2 * h, nb], [0, h], off=h)
                        k1 = tt(DV, up(E), ref, up(bv), SUB, m_free[i] + sdone)
                        k2 = tt(DV, dn(E), dn(bv), ref, SUB)
                    ke = act(E, E, ACT.Exp, [k2] + sdone)
                    qs, ks_ = (upq, dnq) if d == 0 else (dnq, upq)
                    qd, kd = (up4, dn4) if d == 0 else (dn4, up4)
                    EQ = PO if h >= 8 else DV
                    k1 = tt(EQ, qd(M), qs(q), qd(E), MUL, [ke] + m_free[i] + sdone)
                    k2 = tt(DV, kd(M), ks_(kk), kd(E), MUL, [ke])
                    return i, M, [k1, k2]
                attT, attX = sb["ATT"], sb["ATX"]
                if full:
                    ad = []
                    for hp in range(2):
                        b, P, fr = ring.get()
                        PE.wait(*fr, *sdone)
                        for hh in range(2):
                            for t in range(2):
                                h = hp * 2 + hh
                                sl = slice(t * 128, (t + 1) * 128)
                                tk = mm(P[:, (hh * 2 + t) * 128:(hh * 2 + t + 1) * 128], kk[:, h, sl], q[:, h, sl],
                                        True, True, inc=hh == 1 and t == 1)
                        o = attT[:, hp * 4:hp * 4 + 4, :]
                        k = stt(o, P[:, :].rearrange("p (a n) -> p a n", a=4), 2.0,
                                V(sb["IDENT"][:, 0:1], [0, 4], [1, 128]), MUL, MUL, [tk] + F)
                        let(b, k)
                        ad.append(k)
                        yield
                    for d in range(2):
                        for li, h in enumerate(LEVELS):
                            i, M, kms = level(d, h)
                            yield
                            for hp in range(2):
                                b, P, fr = ring.get()
                                PE.wait(*fr, *kms)
                                for hh in range(2):
                                    for t in range(2):
                                        hd_ = hp * 2 + hh
                                        v = M[:, hd_, t * 128:(t + 1) * 128]
                                        tk = mm(P[:, (hh * 2 + t) * 128:(hh * 2 + t + 1) * 128], v, v,
                                                True, True, inc=hh == 1 and t == 1)
                                mk = V(sb["MASK"][:, (d * 7 + li) * 128:(d * 7 + li) * 128 + 1], [0, 4], [1, 128])
                                o = attT[:, hp * 4:hp * 4 + 4, :]
                                k = DV.run(lambda e, o=o, mk=mk, P=P: e.copy_predicated(
                                    o, mk, P[:, :].rearrange("p (a n) -> p a n", a=4)), [tk, ad[hp], t_mask])
                                let(b, k)
                                ad[hp] = k
                                yield
                            m_free[i] = [tk]
                    xd_ = []
                    for d in range(2):
                        i, M, kms = level(d, 128)
                        b, P, fr = ring.get()
                        PE.wait(*fr, *kms)
                        for h in range(4):
                            kp = M[:, h, 0:128] if d == 0 else M[:, h, 128:256]
                            qp = M[:, h, 128:256] if d == 0 else M[:, h, 0:128]
                            tk = mm(P[:, h * 128:(h + 1) * 128], kp, qp, True, True, inc=h == 3)
                        k = act(attX[:, d * 4:d * 4 + 4, :].rearrange("p a n -> p (a n)"), P[:, :], ACT.Copy, [tk] + F)
                        let(b, k)
                        xd_.append(k)
                        m_free[i] = [tk]
                        yield
                dm = []
                for d in range(2):
                    i = mi[0] % 2
                    mi[0] += 1
                    E, M = sb["EB"][:, i, :, :], sb["MB"][:, i, :, :]
                    if s == 0:
                        ke = act(E, B[:, d, :, :], ACT.Exp, m_free[i] + sdone + [DV.last()])
                        k = tt(DV, M, q, E, MUL, [ke] + sdone)
                    else:
                        end = V(B[:, d, :, :], [256, 4], [0, 256], off=255 if d == 0 else 0)
                        k1 = tt(DV, E, end, B[:, d, :, :], SUB, m_free[i] + sdone)
                        ke = act(E, E, ACT.Exp, [k1])
                        k = tt(DV, M, kk, E, MUL, [ke] + sdone)
                    dm.append((M, k))
                yield
                if s == 1:
                    state_done = []
                    for d in range(2):
                        M, km = dm[d]
                        for hp in range(2):
                            b, P, fr = ring.get()
                            PE.wait(*fr, km)
                            for hh in range(2):
                                for t in range(2):
                                    tk = tp(P[:, (hh * 2 + t) * 128:(hh * 2 + t + 1) * 128],
                                            M[:, hp * 2 + hh, t * 128:(t + 1) * 128], IDENT, inc=hh == 1 and t == 1)
                            k = act(sb["KE"][:, :, :].rearrange("p a n -> p (a n)"), P[:, :], ACT.Copy,
                                    [tk, PE.last()] + F)
                            let(b, k)
                            b, P, fr = ring.get()
                            PE.wait(*fr, k)
                            for hh in range(2):
                                h = hp * 2 + hh
                                for t in range(2):
                                    tk = mm(P[:, hh * 256:(hh + 1) * 256], sb["KE"][:, hh * 2 + t, :],
                                            (sb["GV"][:, 2 + t, h * 256:(h + 1) * 256]), t == 0, t == 1, inc=t == 1)
                            k = act(sb["ST"][:, d, hp * 2:hp * 2 + 2, :].rearrange("p a n -> p (a n)"), P[:, :],
                                    ACT.Copy, [tk] + F)
                            let(b, k)
                            state_done.append(k)
                            yield
                if full:
                    od = []
                    for h in range(4):
                        b, P, fr = ring.get()
                        PE.wait(*fr, *ad, *xd_)
                        if s == 0:
                            PE.wait(*state_done, dm[0][1], dm[1][1])
                        vh = [GV[:, s * 2 + t, h * 256:(h + 1) * 256] for t in range(2)]
                        for t in range(2):
                            o = P[:, t * 256:(t + 1) * 256]
                            mm(o, attT[:, h * 2 + t, :], vh[t], True, False)
                            if s == 0:
                                for d in range(2):
                                    mm(o, dm[d][0][:, h, t * 128:(t + 1) * 128], sb["ST"][:, d, h, :], False, False)
                            tk = mm(o, attX[:, (1 - t) * 4 + h, :], vh[1 - t], False, True, inc=True)
                        od.append((b, P, tk, h))
                        yield
                        if len(od) > 1:
                            fin_o(*od.pop(0), s)
                    pend_o = od
                if full:
                    for o_ in pend_o:
                        fin_o(*o_, s)
                    F3 = [DV.last(), AC.last()]
                    gs = sb["GSS"]
                    for t in range(2):
                        for h in range(4):
                            k = act(sb["SQ2"][:, :], GV[:, s * 2 + t, h * 256:(h + 1) * 256], ACT.Square,
                                    F3 + [AC.last()],
                                    accum=gs[:, 0, t * 4 + h:t * 4 + h + 1])
                    k = rsqrt(gs[:, 1, 0:8], gs[:, 0, 0:8], 1.0 / 256, 8, [k])
                    for t in range(2):
                        v = V(GV[:, s * 2 + t, 0:1], [256, 4], [1, 256])
                        og_done.append(tt(PO, v, v, V(gs[:, 1, t * 4:t * 4 + 1], [1, 4], [0, 256]), MUL, [k]))
                    yield

        def fin_o(b, P, tk, h, s):
            v = V(GV[:, s * 2, h * 256:h * 256 + 1], [1024, 2], [1, 256])
            k = act(v, P[:, :].rearrange("p (t n) -> p t n", t=2), ACT.Copy, [tk, PE.last()])
            let(b, k)
        og_done = []

        AF = sb["AF"]
        fA = fence()
        wk = {"af": [fA, fA]}
        af_done = []
        ns = 1 if last else 2

        def branch_a(ring):
            for ft in range(8):
                i = ft % 2
                c_sb, u_sb, cv = sb["WA"][:, i, 0, 0:NT], sb["WA"][:, i, 1, 0:NT], sb["WA"][:, i, 2, 0:NT]
                pb = {}
                for nm in ("c", "x", "b", "z"):
                    hi, lo, wt = get_w(f"wa{l}", {"b": 0, "c": 8, "x": 16, "z": 24}[nm] + ft)
                    b, P, fr = ring.get()
                    tk = group_T(P, 0, hi, lo, 0, NT, fr + wt + hd)
                    put_w(tk)
                    pb[nm] = (b, P[:, 0:NT], tk)
                    if nm == "c":
                        kc = act(c_sb, pb[nm][1], ACT.Copy, [tk] + wk["af"][i])
                        let(b, kc)
                    elif nm == "x":
                        ku = tt(DV, u_sb, P[:, 0:NT], c_sb, MUL, [tk, kc] + wk["af"][i])
                        let(b, ku)
                        w = [par("cw2", (l * 3 + q) * 8 + ft) for q in range(3)]
                        k = act(cv, u_sb, ACT.Copy, [ku] + wk["af"][i], scale=w[1])
                        for s in range(ns):
                            o = s * 256
                            k = stt(cv[:, o + 1:o + 256], u_sb[:, o:o + 255], w[0], cv[:, o + 1:o + 256], MUL, ADD, [k])
                            k = stt(cv[:, o:o + 255], u_sb[:, o + 1:o + 256], w[2], cv[:, o:o + 255], MUL, ADD, [k])
                        kcv = k
                    elif nm == "b":
                        kb = stt(cv, P[:, 0:NT], 0.5, cv, MUL, MUL, [tk, kcv])
                        let(b, kb)
                    else:
                        kt_ = act(c_sb, P[:, 0:NT], ACT.Tanh, [tk, ku], scale=0.5)
                        kz = stt(c_sb, c_sb, 1.0, P[:, 0:NT], ADD, MUL, [kt_])
                        let(b, kz)
                        k = tt(DV, AF[:, ft, 0:NT], c_sb, cv, MUL, [kz, kb] + fA)
                        wk["af"][i] = [k]
                        af_done.append(k)
                    yield
        weave(branch_a(lo4), gla(hi4), 4.0)

        F2 = fence()
        ABH, ABL = sb["ABH"], sb["ABL"]

        def split_ab(kt, v, after, n=NT):
            a = act(ABH[:, kt, 0:n], v, ACT.Copy, after)
            d = tt(PO if kt % 2 else DV, ABL[:, kt, 0:n], v, ABH[:, kt, 0:n].bitcast(F32), SUB, [a] + list(after))
            return [a, d]
        ab = []
        for kt in range(8):
            ab += split_ab(kt, AF[:, kt, 0:NT], F2)
        F3 = fence()
        QT, KT, VV = sb["QT"], sb["KT"], sb["VV"]
        ro = sb["ROPE"]

        def norm_heads(P, tk, n, i, t, slot, w0):
            sq, qn, t2 = sb["SQ3"], sb["QNB"][:, slot, w0:w0 + n * 128], sb["QT2"]
            k = act(sq[:, 0:n * 128], P, ACT.Square, [tk, DV.last()] + F3)
            k = red(sb["GSS"][:, 0, 0:n], sq[:, 0:n * 128].rearrange("p (h d) -> p h d", d=128), ADD, [k])
            k = rsqrt(sb["GSS"][:, 1, 0:n], sb["GSS"][:, 0, 0:n], 1.0 / 128, n, [k])
            k0 = tt(DV, qn.rearrange("p (h d) -> p h d", d=128), P.rearrange("p (h d) -> p h d", d=128),
                    V(sb["GSS"][:, 1, 0:1], [1, n], [0, 128]), MUL, [k] + qn_free[slot] + F3)
            if t >= 2:
                g = sb["GN"][:, i, :]
                k1 = tt(DV, qn.rearrange("p (h d) -> p h d", d=128), qn.rearrange("p (h d) -> p h d", d=128),
                        V(g, [0, n], [1, 128]), MUL, [k0] + t_rope)
                return k0, k1
            ks = []
            for hf in range(2):
                ks.append(tt(DV, V(t2[:, hf * 32:hf * 32 + 1], [128, n], [64, 2], [1, 32]),
                             V(qn, [128, n], [64, 2], [1, 32], off=(1 - hf) * 32),
                             V(ro[:, i, 1, t, hf * 32:hf * 32 + 1], [0, n], [64, 2], [1, 32]), MUL,
                             [k0, PO.last()] + t_rope + F3))
            k1 = tt(DV, qn.rearrange("p (h d) -> p h d", d=128), qn.rearrange("p (h d) -> p h d", d=128),
                    V(ro[:, i, 0, t, 0:1], [0, n], [1, 128]), MUL, ks)
            k1 = tt(DV, qn, qn, t2[:, 0:n * 128], ADD, [k1])
            return k0, k1
        qn_free = [[], [], [], []]
        q_done = {}
        got = group_N(f"wkv{l}", 0, tiles4, all8, hd)
        kn = []
        for t, (b, P, tk) in enumerate(got):
            kv = act(VV[:, t, :], P[:, 256:512], ACT.Copy, [tk] + F2)
            k0, k1 = norm_heads(P[:, 0:256], kv, 2, 1, t, t, 0)
            let(b, k0)
            kn.append(k1)
        v2_done = kv
        tlist = (0, 1) if last else (0, 1, 2, 3)

        def heads_T(nh, kn, tl, dst, base):
            r = []
            for h in range(nh):
                b, P, fr = all8.get()
                PE.wait(*fr, *kn)
                for i, t in enumerate(tl):
                    tk = tp(P[:, i * 128:(i + 1) * 128], sb["QNB"][:, t, h * 128:(h + 1) * 128], IDENT,
                            inc=i == len(tl) - 1)
                k = act(dst[:, base + h, 0:len(tl) * 128], P[:, 0:len(tl) * 128], ACT.Copy, [tk] + F2)
                let(b, k)
                r.append(k)
            for t in tl:
                qn_free[t] = [tk]
            return r
        pend = (2, kn, tiles4, KT, 0)
        for g in range(2):
            got = group_N(f"wq{l}", g, tlist, all8, hd)
            r = heads_T(*pend)
            if g == 0:
                k2_done = r
            else:
                for h in range(4):
                    q_done[h] = r[h]
            kn = []
            for t, (b, P, tk) in enumerate(got):
                k0, k1 = norm_heads(P[:, :], tk, 4, 0, t, t, 0)
                let(b, k0)
                kn.append(k1)
            pend = (4, kn, tlist, QT, g * 4)
        r = heads_T(*pend)
        for h in range(4):
            q_done[4 + h] = r[h]
        F4 = fence()

        jobs = [(0, h, t) for h in range(8) for t in range(2)]
        if not last:
            jobs += [(1, h, t) for h in range(8) for t in range(2)]

        def attn2(ring):
            AE, AP2, AR = sb["AE"], sb["APT"], sb["AR"]
            e_free, p_free = [F4, F4, F4], [F4, F4]
            ed, pd, ob = {}, {}, {}
            n = len(jobs)

            def sc(j):
                s, h, t = jobs[j]
                nk = 512 if s == 0 else 256
                k0 = 0 if s == 0 else 256
                b, P, fr = ring.get()
                c = s * 256 + t * 128
                tk = mm(P[:, 0:nk], QT[:, h, c:c + 128], KT[:, h // 4, k0:k0 + nk], True, True,
                        fr + [q_done[h]] + k2_done, inc=True)
                e, a = j % 3, j % 4
                k = red(AR[:, 0, a:a + 1], P[:, 0:nk], MAX, [tk] + F4, negate=True)
                k = act(AE[:, e, 0:nk], P[:, 0:nk], ACT.Exp, [k] + e_free[e], bias=AR[:, 0, a:a + 1],
                        accum=AR[:, 1, a:a + 1])
                let(b, k)
                k = DV.run(lambda en: en.reciprocal(AR[:, 2, a:a + 1], AR[:, 1, a:a + 1]), [k])
                ed[j] = ts(DV, AE[:, e, 0:nk], AE[:, e, 0:nk], AR[:, 2, a:a + 1], None, MUL, None, [k])

            def tr_(j):
                s, h, t = jobs[j]
                nk = 4 if s == 0 else 2
                b, P, fr = ring.get()
                e, w = j % 3, j % 2
                PE.wait(*fr, ed[j])
                for i in range(nk):
                    tk = tp(P[:, i * 128:(i + 1) * 128], AE[:, e, i * 128:(i + 1) * 128], IDENT, inc=i == nk - 1)
                e_free[e] = [tk]
                k = act(AP2[:, w, 0:nk * 128], P[:, 0:nk * 128], ACT.Copy, [tk] + p_free[w])
                let(b, k)
                pd[j] = k

            def pv_(j):
                s, h, t = jobs[j]
                nk = 4 if s == 0 else 2
                if t == 0:
                    ob[0] = ring.get()
                b, P, fr = ob[0]
                w = j % 2
                PE.wait(*fr, pd[j], v2_done)
                for i in range(nk):
                    kt = i if s == 0 else 2 + i
                    tk = mm(P[:, t * 128:(t + 1) * 128], VV[:, kt, (h // 4) * 128:(h // 4 + 1) * 128],
                            AP2[:, w, i * 128:(i + 1) * 128], i == 0, i == nk - 1, inc=i == nk - 1)
                p_free[w] = [tk]
                if t == 1:
                    k = act(QT[:, h, s * 256:(s + 1) * 256], P[:, 0:256], ACT.Copy, [tk])
                    let(b, k)
                    o_done.append(k)
            for j in range(n + 3):
                if j < n:
                    sc(j)
                    yield
                if 0 <= j - 1 < n:
                    tr_(j - 1)
                    yield
                if 0 <= j - 2 < n:
                    pv_(j - 2)
                    yield
        o_done = []

        S = sb["S"]
        bgh = sb["BG"]
        t_bg = ts(DV, bgh[:, 0:24], par("b_gate", l * 24, 24), 0.5, None, MUL, None)
        s_done = {}

        def branch_out(bi, ring, ab):
            for ft in range(8):
                hi, lo, wt = get_w(f"wmg{l}", bi * 8 + ft)
                b, P, fr = ring.get()
                tk = group_T(P, 0, hi, lo, 0, NT, fr + wt + hd)
                put_w(tk)
                g = sb["GT"][:, ft % 2, 0:NT]
                kg = act(g, P[:, 0:NT], ACT.Tanh, [tk, t_bg, DV.last(), PO.last()] + F4, scale=0.5, bias=bgh[:, bi * 8 + ft:bi * 8 + ft + 1])
                let(b, kg)
                yield
                hi, lo, wt = get_w(f"wbr{l}", bi * 8 + ft)
                b, P, fr = ring.get()
                tk = group_T(P, 0, hi, lo, 0, NT, fr + wt + ab, ABH, ABL)
                put_w(tk)
                if bi == 0:
                    k = stt(S[:, ft, 0:NT], g, 1.0, P[:, 0:NT], ADD, MUL, [tk, kg] + F4)
                else:
                    k = stt(g, g, 1.0, P[:, 0:NT], ADD, MUL, [tk, kg])
                let(b, k)
                if bi:
                    k = tt(PO, S[:, ft, 0:NT], S[:, ft, 0:NT], g, ADD, [k, s_done[ft]])
                s_done[ft] = k
                yield
        weave(branch_out(0, lo4, ab), attn2(hi4), 6.0)

        def z_stage(name, value, ring):
            r = []
            for ft in range(8):
                hi, lo, wt = get_w(name, ft)
                b, P, fr = ring.get()
                tk = group_T(P, 0, hi, lo, 0, NT, fr + wt + hd)
                put_w(tk)
                i = ft % 2
                z = sb["ZB"][:, i, 0:NT]
                kt_ = act(z, P[:, 0:NT], ACT.Tanh, [tk, DV.last(), PO.last()], scale=0.5)
                kz = stt(z, z, 1.0, P[:, 0:NT], ADD, MUL, [kt_])
                let(b, kz)
                kv = value(ft, z, kz)
                r += split_ab(ft, z, [kv])
                yield r
        ab = []

        def val_b(ft, z, kz):
            return stt(z, z, 0.5, QT[:, ft, 0:NT], MUL, MUL, [kz] + o_done)

        for ab in z_stage(f"wzb{l}", val_b, lo4):
            pass
        drain(branch_out(1, all8, ab))

        def val_c(ft, z, kz):
            b, P, fr = hi4.get()
            PE.wait(*fr, *og_done)
            nt = NT // 128
            for t in range(nt):
                tk = tp(P[:, t * 128:(t + 1) * 128], GV[:, t, ft * 128:(ft + 1) * 128], IDENT, inc=t == nt - 1)
            k = ts(DV, z, z, 0.5, None, MUL, None, [kz])
            k = stt(z, P[:, 0:NT], par("glag", l * 2 + ft % 2), z, MUL, MUL, [tk, k])
            let(b, k)
            return k
        for ab in z_stage(f"wzc{l}", val_c, lo4):
            pass
        F5 = fence()
        gb = []
        for s in range(ns):
            k = tt(DV, sb["GC"][:, s, :], MT[:, l, 16:24, s], par("g_post", l * 8, 8), MUL, F5 + mod_done)
            for hf in range(2):
                b, P, fr = all8.get()
                for j in range(4):
                    dg = sb["DG"][:, j % 2, :]
                    kd = ts(DV, dg, IDENT, sb["GC"][:, s, hf * 4 + j:hf * 4 + j + 1], 16.0, MUL, MUL,
                            [k, PE.last()])
                    tk = mm(P[:, j * 128:(j + 1) * 128], sb["TRI"][:, 128:256], dg, True, True, fr + [kd], inc=True)
                kk_ = act(sb["GB"][:, s, hf * 512:(hf + 1) * 512], P[:, :], ACT.Copy, [tk] + F5)
                let(b, kk_)
                gb.append(kk_)
        drain(branch_out(2, all8, ab))
        F6 = fence()
        xr = rdma.start(PO, sb["AFX"][:, 0:NT // 128, :],
                        A["xscr"][0, 0:NT, :].rearrange("(t p) d -> p t d", p=128), F6 + sp_done)
        sd = []
        tpe = PE.last()
        for kt in range(8):
            a = act(ABH[:, kt, 0:NT], S[:, kt, 0:NT], ACT.Copy, [s_done[kt], tpe], scale=0.5)
            d = stt(ABL[:, kt, 0:NT], S[:, kt, 0:NT], 0.5, ABH[:, kt, 0:NT].bitcast(F32), MUL, SUB, [a])
            sd += [a, d]
        gs = sb["GSS"]
        kk2 = {}
        for g in range(2):
            for i, (b, P, tk) in enumerate(group_N(f"wo2{l}", g, tlist, all8, sd, xh=ABH, xl=ABL)):
                k = act(sb["ZB"][:, 0, :], P[:, :], ACT.Square, [tk, AC.last()] + F6, accum=gs[:, 0, g * 4 + i:g * 4 + i + 1])
                k2 = copy(DV, sb["XS"][:, i, g * 512:(g + 1) * 512], P[:, :], [k] + F6)
                let(b, k2)
                kk2[(g, i)] = [k, k2]
        nt = len(tlist)
        al = [x for v in kk2.values() for x in v]
        k = tt(DV, gs[:, 0, 0:nt], gs[:, 0, 0:nt], gs[:, 0, 4:4 + nt], ADD, al)
        k = rsqrt(gs[:, 1, 0:nt], gs[:, 0, 0:nt], 1.0 / 1024, nt, [k])
        x_done = []
        for i in range(nt):
            xs = sb["XS"][:, i, :]
            k1 = stt(xs, xs, gs[:, 1, i:i + 1], sb["GB"][:, i // 2, :], MUL, MUL, [k] + gb)
            k1 = tt(PO if i % 2 else DV, xs, xs, sb["AFX"][:, i, :], ADD, [k1, xr])
            x_done.append(k1)
        if not last:
            sp_done = []
            for s in range(2):
                sp_done.append(spill[s].start(PO, A["xscr"][0, s * 256:(s + 1) * 256, :].rearrange("(t p) d -> p t d", p=128),
                                              sb["XS"][:, 2 * s:2 * s + 2, :], x_done + [xr]))
        else:
            t_out = odma.start(SP, out[0, :, :].rearrange("(t p) d -> p t d", p=128), sb["XS"][:, 0:2, :], x_done)
            SP.wait(t_out)
    SP.wait(*sp_done)
    return used, {"pe": PE, "act": AC, "dve": DV, "pool": PO, "sp": SP}


def build(nc, args, out):
    base = 16512

    class Map:

        def __init__(self):
            self.t = {}

        def put(self, name, off, shape, dt=F32):
            n = int(np.prod(shape[1:])) * (1 if dt == U8 else 4)
            h = nc.alloc_sbuf_tensor_at(name, shape, dt, offset=base + off)
            self.t[name] = h
            return -(-(off + n) // 32) * 32
    m = Map()
    o = m.put("RAW", 0, [128, 5, 1024])
    o = m.put("SPH", o, [128, 4, 1024], F32R)
    o = m.put("SPL", o, [128, 4, 1024], F32R)
    o = m.put("HTH", o, [128, 8, 512], F32R)
    o = m.put("HTL", o, [128, 8, 512], F32R)
    D = o
    o = m.put("IDENT", D, [128, 128])
    o = m.put("PAR", o, [128, NPAR])
    o = m.put("TRI", o, [128, 384])
    o = m.put("MASK", o, [128, 14 * 128], U8)
    o = m.put("MODT", o, [128, 2, 24, 2])
    o = m.put("GP", o, [128, 2, 8, 2])
    o = m.put("CS", o, [128, 2, 16])
    o = m.put("RS", o, [128, 3, 32])
    o = m.put("SS", o, [128, 8])
    o = m.put("GSS", o, [128, 2, 8])
    o = m.put("ONE", o, [128, 1])
    o = m.put("BG", o, [128, 24])
    o = m.put("GC", o, [128, 2, 8])
    o = m.put("ROPE", o, [128, 2, 2, 2, 128])
    o = m.put("GN", o, [128, 2, 128])
    C = o
    q = m.put("XS", C, [128, 4, 1024])
    m.put("QT", C, [128, 8, 512])
    m.put("LA", C, [128, 4, 512])
    m.put("E4", C + 8192, [128, 4, 512])
    m.put("EB", C + 8192, [128, 2, 4, 256])
    m.put("MB", C, [128, 2, 4, 256])
    m.put("KT", q, [128, 2, 512])
    m.put("VV", q + 4096, [128, 4, 256])
    m.put("BC", q, [128, 2, 4, 256])
    g = q + 8192
    m.put("GQ", g, [128, 4, 512])
    m.put("GK", g + 8192, [128, 4, 512])
    m.put("S", g, [128, 8, 512])
    v = m.put("GV", g + 16384, [128, 4, 1024])
    m.put("GB", g + 16384, [128, 2, 1024])
    m.put("DG", g + 16384 + 8192, [128, 2, 128])
    a = m.put("AF", v, [128, 8, 512])
    m.put("AFX", v, [128, 4, 1024])
    w = m.put("AE", v, [128, 3, 512])
    w = m.put("APT", w, [128, 2, 512])
    w = m.put("AR", w, [128, 3, 4])
    m.put("GT", v + 12288, [128, 2, 512])
    Z = a
    m.put("XN2", Z, [128, 4, 1024])
    m.put("HV", Z + 16384, [128, 2, 512])
    z = m.put("ATT", Z, [128, 8, 128])
    z = m.put("ATX", z, [128, 8, 128])
    z = m.put("ST", z, [128, 2, 4, 256])
    z = m.put("KE", z, [128, 4, 128])
    z = m.put("RT", z, [33, 512])
    z = m.put("RN", z, [128, 128])
    z = m.put("SQ2", z, [128, 256])
    z = m.put("WA", z, [128, 2, 3, 512])
    zmax = z
    zw = m.put("WDEC", z, [33, 1024])
    m.put("ABH", Z, [128, 8, 512], F32R)
    e = m.put("ABL", Z + 16384, [128, 8, 512], F32R)
    e = m.put("ZB", e, [128, 2, 512])
    m.t["end2"] = max(e, zw)
    qq = m.put("QNB", v, [128, 4, 512])
    m.put("QT2", v + 8192, [128, 512])
    m.put("SQ3", v + 10240, [128, 512])
    p = m.put("YN", C + 8192, [128, 2, 1024])
    p = m.put("QKN", p, [128, 2, 2, 512])
    p = m.put("VN", p, [128, 2, 1024])
    p = m.put("QKT", p, [128, 16, 256])
    p = m.put("BIAS", p, [128, 12, 384])
    p = m.put("E3", p, [128, 4, 384])
    p = m.put("PT3", p, [128, 2, 384])
    m.put("MASKF", p, [128, 14 * 128])
    p = m.put("XN1", p, [128, 2, 1024])
    p = m.put("SQ", p, [128, 2, 512])
    p = m.put("QS", p, [128, 2, 16])
    p = m.put("RR", p, [128, 4, 32])
    p = m.put("SM", p, [128, 16])
    p = m.put("LT", p, [128, 64])
    p = m.put("LAMR", p, [128, 512])
    p = m.put("FC", p, [128, 2, 2, 256])
    p = m.put("FT", p, [128, 2, 256])
    p = m.put("AH", p, [128, 3, 256], F32R)
    p = m.put("AL", p, [128, 3, 256], F32R)
    e3 = m.t["E3"]
    x1 = m.put("OH", C + 8192, [32, 384])
    x1 = m.put("RB", x1, [32, 12])
    x1 = m.put("MROW", x1, [12, 384])
    x1 = m.put("RROW", x1, [12, 384])
    top = max(p, m.t.pop("end2"))
    print("SBUF top", base + top, "of", nc.sbuf_usable_end)
    assert base + top <= nc.sbuf_usable_end
    sb = m.t

    names = ["pe", "act", "dve", "pool", "sp"] + [f"raw{i}" for i in range(5)] + \
        ["cst", "bias", "xs", "sp0", "sp1", "gd", "td", "wd", "rdl", "out"]
    sems = {n: nc.alloc_semaphore("s_" + n) for n in names}
    banks = [nc.alloc_psum_tensor(f"pb{i}", [128, 512], F32) for i in range(8)]
    order, _ = program(nc, None, args, sems, sb, banks, out)
    _, E = program(nc, order, args, sems, sb, banks, out)
    print({k: len(e.todo) for k, e in E.items()})

    with nc.Block() as block:
        @block.sync
        def _(eng):
            for f in E["sp"].todo:
                f(eng)

        @block.scalar
        def _(eng):
            for f in E["act"].todo:
                f(eng)

        @block.vector
        def _(eng):
            for f in E["dve"].todo:
                f(eng)

        @block.gpsimd
        def _(eng):
            for f in E["pool"].todo:
                f(eng)

        @block.tensor
        def _(eng):
            for f in E["pe"].todo:
                f(eng)


def shape_constants():
    ident = np.eye(128, dtype=np.float32)
    s, t = np.arange(128)[:, None], np.arange(128)[None, :]
    tri = np.concatenate([(s <= t), np.ones((128, 128)), (s >= t)], axis=1).astype(np.float32) / np.float32(16)
    masks = []
    for d in range(2):
        for h in LEVELS:
            a, b = (s, t) if d == 0 else (t, s)
            masks.append((a // (2 * h) == b // (2 * h)) & (a % (2 * h) < h) & (b % (2 * h) >= h))
    mask = np.concatenate(masks, axis=1).astype(np.float32)
    bucket = np.searchsorted(np.array(BUCKET_STARTS), np.arange(256), side="right") - 1
    onehot = np.zeros((32, 384), np.float32)
    for i in range(256):
        onehot[bucket[255 - i], i] = 1.0
    maskrow = np.zeros((12, 384), np.float32)
    maskrow[:, 256:] = -1e30
    pos = np.arange(256)
    fr = (10000.0 ** (-np.arange(32, dtype=np.float32) * 2.0 / 64)).astype(np.float32)
    ang = np.stack([(pos // 64).astype(np.float32)[:, None] * fr, (pos % 64).astype(np.float32)[:, None] * fr], 1)
    c, sn = np.cos(ang), np.sin(ang)
    Ct = np.stack([c, c], axis=2).reshape(256, 128)
    St = np.stack([-sn, sn], axis=2).reshape(256, 128)
    rope = np.stack([Ct, St]).reshape(2, 2, 128, 128).transpose(2, 0, 1, 3).astype(np.float32)
    return dict(ident=ident, tri=tri, mask=mask, onehot=onehot, maskrow=maskrow, rope=np.ascontiguousarray(rope))


def lay_out(inp):
    i = {k: np.asarray(v) for k, v in inp.items()}
    d = shape_constants()

    def T(w):
        return np.ascontiguousarray(w.reshape(8, 128, -1, 128).transpose(2, 1, 0, 3)).reshape(-1, 128, 1024)

    def N(w):
        k, c = w.shape
        return np.ascontiguousarray(w.reshape(k // 256, 2, 128, c // 512, 512).transpose(3, 0, 2, 1, 4)).reshape(-1, 128, 1024)

    def cols(a):
        return a.reshape(-1, 128).T
    for l in range(2):
        d[f"w_in{l}"] = N(i["w_in"][l])
        d[f"w_out{l}"] = N(i["w_out"][l])
        d[f"w_up{l}"] = T(i["w_up"][l])
        d[f"w_down{l}"] = i["w_down"][l].reshape(FF_TILES, 128, 1024)
        w = i["w_in_2"][l]
        d[f"wa{l}"] = T(w[:, 0:4096])
        d[f"wq{l}"] = N(w[:, 4096:5120])
        d[f"wkv{l}"] = N(w[:, 5120:5632])
        d[f"wzb{l}"] = T(w[:, 5632:6656])
        d[f"wgq{l}"] = T(w[:, 6656:7168])
        d[f"wgk{l}"] = T(w[:, 7168:7680])
        d[f"wgv{l}"] = N(w[:, 7680:8704])
        d[f"wr{l}"] = np.ascontiguousarray(w[:, 8704:8736].reshape(8, 128, 32).transpose(1, 0, 2)).reshape(1, 128, 256)
        d[f"wzc{l}"] = T(w[:, 8736:9760])
        d[f"wmg{l}"] = T(w[:, 9760:12832])
        d[f"wbr{l}"] = np.concatenate([T(i[n][l]) for n in ("w_br_conv_2", "w_br_attn_2", "w_br_gla_2")])
        d[f"wo2{l}"] = N(i["w_out_2"][l])
    d["w_ada"] = np.concatenate([T(i["w_ada_2"][l]) for l in range(2)])
    wdec = np.zeros((2, 33, 1024), np.float32)
    wdec[:, 0:16, 0:512] = i["w_decay_fwd_2"]
    wdec[:, 16:32, 512:1024] = i["w_decay_bwd_2"]
    wdec[:, 32, 0:512] = i["b_decay_fwd_2"]
    wdec[:, 32, 512:1024] = i["b_decay_bwd_2"]
    d["wdec"] = wdec
    qk = i["qk_norm_g"]
    d["par"] = np.ascontiguousarray(np.concatenate([
        cols(i["ln_attn_g"]), cols(i["ln_ffn_g"]), cols(np.concatenate([qk, qk], axis=-1)), cols(i["diff_subln_g"]),
        cols(i["conv_w"]), cols(i["conv_b"]),
        np.stack([i["c_2"][0].reshape(8, 128), i["c_ctx_2"].reshape(8, 128)], axis=1).reshape(16, 128).T,
        cols(i["b_ada_2"]), cols(i["g_pre_2"]), cols(i["g_post_2"]), cols(i["conv_w_2"]), cols(i["gla_norm_g_2"]),
        cols(i["b_gate_2"])], axis=1))
    d["lamr"] = np.ascontiguousarray(np.broadcast_to(i["diff_lambda"].reshape(1, 512), (128, 512)))
    d["qkn"] = np.ascontiguousarray(np.stack([i["q_norm_g_2"], i["k_norm_g_2"]], axis=1).reshape(4, 128))
    d["rel_bias"] = i["rel_bias"]
    d["x"] = i["x"]
    d["ctx"] = i["ctx_2"]
    return d


def kernel(**inputs):
    import concourse.bacc as bacc
    from concourse.bass_utils import run_bass_kernel_spmd

    nc = bacc.Bacc("TRN2", target_bir_lowering=False, num_devices=1)
    arrays, args = {}, {}
    for name, a in lay_out(inputs).items():
        a = np.ascontiguousarray(a)
        arrays["in_" + name] = a
        args[name] = nc.dram_tensor("in_" + name, a.shape, mybir.dt.from_np(a.dtype), kind="ExternalInput").ap()
    args["rscr"] = nc.dram_tensor("rscr", (12, 128, 384), F32, kind="Internal").ap()
    args["xscr"] = nc.dram_tensor("xscr", (1, 512, 1024), F32, kind="Internal").ap()
    out = nc.dram_tensor("out0", (1, 256, 1024), F32, kind="ExternalOutput").ap()
    build(nc, args, out)
    r = run_bass_kernel_spmd(nc, [arrays], core_ids=[0])
    return r.results[0]["out0"]
```

```python
import concourse.bass as bass
from concourse import mybir
import math
import numpy as np

F32 = mybir.dt.float32
F32R = mybir.dt.float32r
U8 = mybir.dt.uint8
I32 = mybir.dt.int32
ALU = mybir.AluOpType
ACT = mybir.ActivationFunctionType
AX = mybir.AxisListType
ADD, SUB, MUL, MAX, MIN = ALU.add, ALU.subtract, ALU.mult, ALU.max, ALU.min

EPS = 1e-6
BUCKET_STARTS = list(range(17)) + [21, 27, 35, 46, 59, 77, 99, 128, 166, 216]
FF_TILES = 22
PCOLS = {}
_at = 0
for _name, _n in (("ln_attn", 16), ("ln_ffn", 16), ("qkg", 8), ("subg", 2), ("cw", 2 * 3 * 44), ("cb", 88),
                  ("c", 16), ("b_ada", 48), ("g_pre", 16), ("g_post", 16), ("cw2", 48), ("glag", 4),
                  ("b_gate", 48)):
    PCOLS[_name] = _at
    _at += _n
NPAR = _at
MARKS = []
RA = [2.0, 2.0]
LEVELS = (64, 32, 16, 8, 4, 2, 1)


class Engine:

    def __init__(self, name, sem):
        self.name, self.sem, self.count, self.todo, self.seen, self.n = name, sem, 0, [], {}, 0

    def wait(self, *tokens):
        for t in tokens:
            if t is None:
                continue
            sem, value = t
            key = id(sem)
            if self.seen.get(key, 0) < value:
                self.seen[key] = value
                self.todo.append(lambda e, s=sem, v=value: e.wait_ge(s, v))

    def run(self, fn, after=(), inc=True):
        self.wait(*after)
        self.n += 1
        if inc:
            self.count += 1
            self.todo.append(lambda e, f=fn, s=self.sem: f(e).then_inc(s, 1))
            return (self.sem, self.count)
        self.todo.append(fn)
        return None

    def last(self):
        return (self.sem, self.count) if self.count else None


class Dma:

    def __init__(self, sem):
        self.sem, self.count = sem, 0

    def start(self, eng, out, in_, after=()):
        eng.wait(*after)
        self.count += 16
        eng.todo.append(lambda e, o=out, i=in_, s=self.sem: e.dma_start(o, i).then_inc(s, 16))
        return (self.sem, self.count)


def V(ap, *dims, off=0):
    return bass.AP(ap.tensor, ap.offset + off, [list(ap.ap[0])] + [list(d) for d in dims])


def program(nc, order, A, sems, sb, banks, out):
    PE, AC, DV, PO, SP = (Engine(n, sems[n]) for n in ("pe", "act", "dve", "pool", "sp"))
    used = []
    MARKS.clear()

    def act(o, i, func, after=(), scale=1.0, bias=None, accum=None):
        kw = {}
        if bias is not None:
            kw["bias"] = bias
        if accum is not None:
            kw["accum_out"] = accum
        return AC.run(lambda e: e.activation(o, i, func, scale=scale, **kw), after)

    def tt(E, o, a, b, op, after=()):
        return E.run(lambda e: e.tensor_tensor(o, a, b, op), after)

    def ts(E, o, a, s1, s2, op0, op1, after=()):
        if op1 is None:
            return E.run(lambda e: e.tensor_scalar(o, a, s1, None, op0), after)
        return E.run(lambda e: e.tensor_scalar(o, a, s1, s2, op0, op1), after)

    def stt(o, a, s, b, op0, op1, after=()):
        return DV.run(lambda e: e.scalar_tensor_tensor(out=o, in0=a, scalar=s, in1=b, op0=op0, op1=op1), after)

    def copy(E, o, i, after=()):
        return E.run(lambda e: e.tensor_copy(o, i), after)

    def red(o, i, op, after=(), negate=None):
        return DV.run(lambda e: e.tensor_reduce(out=o, in_=i, axis=AX.X, op=op, negate=negate), after)

    def mm(o, l, r, start, stop, after=(), inc=False):
        PE.n += l.dtype == F32
        return PE.run(lambda e: e.matmul(o, l, r, start=start, stop=stop), after, inc)

    def tp(o, i, ident, after=(), inc=False):
        return PE.run(lambda e: e.transpose(o, i, ident), after, inc)

    def mark(label):
        MARKS.append((label, PE.n))

    def fence():
        return [e.last() for e in (PE, AC, DV, PO)]

    free = [[] for _ in range(8)]

    class Ring:
        def __init__(self, ids):
            self.ids, self.at = ids, 0

        def get(self):
            for _ in self.ids:
                b = self.ids[self.at % len(self.ids)]
                self.at += 1
                if free[b] is not None:
                    toks, free[b] = free[b], None
                    return b, banks[b], toks
            raise AssertionError("every bank of the ring is held")

    def let(b, *toks):
        free[b] = list(toks)

    NR, NS = 5, 4
    raw_free = [[] for _ in range(NR)]
    spl_free = [[] for _ in range(NS)]
    raw_dma = [Dma(sems[f"raw{i}"]) for i in range(NR)]
    st = {"load": 0, "split": 0, "get": 0, "nsplit": 0}
    held = set()
    loaded, ready, done_raw = {}, {}, set()

    def load_upto(n):
        while order is not None and st["load"] <= n and st["load"] < len(order):
            u = st["load"]
            if u >= NR and u - NR not in done_raw:
                return
            name, idx, cols, kind = order[u]
            s = u % NR
            loaded[u] = raw_dma[s].start(SP, sb["RAW"][:, s, 0:cols], A[name][idx, :, 0:cols], raw_free[s])
            st["load"] += 1

    def split_upto(n):
        while order is not None and st["split"] <= n and st["split"] < len(order):
            u = st["split"]
            load_upto(u + NR - 1)
            if u not in loaded:
                return
            name, idx, cols, kind = order[u]
            s = u % NR
            raw = sb["RAW"][:, s, 0:cols]
            if kind == "raw":
                ready[u] = (raw, None, s, None, [loaded[u]])
            else:
                k = st["nsplit"]
                q = k % NS
                if q in held:
                    return
                held.add(q)
                st["nsplit"] += 1
                hi, lo = sb["SPH"][:, q, 0:cols], sb["SPL"][:, q, 0:cols]
                t1 = act(hi, raw, ACT.Copy, [loaded[u]] + spl_free[q])
                eng = PO if k % 3 == 2 else DV
                t2 = tt(eng, lo, raw, hi.bitcast(F32), SUB, [loaded[u], t1] + spl_free[q])
                raw_free[s] = [t1, t2]
                done_raw.add(u)
                ready[u] = (hi, lo, None, q, [t1, t2])
            st["split"] += 1

    def get_w(name, idx, cols=1024, kind="split"):
        used.append((name, idx, cols, kind))
        u = st["get"]
        st["get"] += 1
        if order is None:
            if kind == "raw":
                return sb["RAW"][:, 0, 0:cols], None, []
            return sb["SPH"][:, 0, 0:cols], sb["SPL"][:, 0, 0:cols], []
        assert order[u] == (name, idx, cols, kind)
        split_upto(u + NS + 1)
        hi, lo, s, q, toks = ready[u]
        return hi, lo, toks

    def put_w(tok, back=0):
        if order is None:
            return
        u = st["get"] - 1 - back
        _, _, s, q, _ = ready.pop(u)
        if s is not None:
            raw_free[s] = [tok]
            done_raw.add(u)
        else:
            spl_free[q] = [tok]
            held.discard(q)

    xdma, cdma = Dma(sems["xs"]), Dma(sems["cst"])
    xdma.start(AC, sb["XS"][:, 0, :], A["x"][0, 0:128, :])
    xdma.start(AC, sb["XS"][:, 1, :], A["x"][0, 128:256, :])
    xdma.start(AC, sb["IDENT"][:, :], A["ident"])
    T_x = xdma.start(AC, sb["PAR"][:, :], A["par"])
    for o, i in ((sb["OH"][0:32, 0:384], "onehot"), (sb["RB"][0:32, 0:12], "rel_bias"),
                 (sb["MROW"][0:12, 0:384], "maskrow"), (sb["LAMR"][:, :], "lamr")):
        T_bias_in = cdma.start(PO, o, A[i])
    kdma = Dma(sems["cst2"])
    kdma.start(PO, sb["TRI"][:, :], A["tri"])
    kdma.start(PO, sb["MASKF"][:, :], A["mask"])
    T_const = kdma.start(PO, sb["XS"][:, 2:4, :], A["ctx"][0, :, :].rearrange("(t p) d -> p t d", p=128))
    IDENT = sb["IDENT"][:, :]
    t_one = DV.run(lambda e: e.memset(sb["ONE"][:, :], 1.0))

    def par(name, i=0, n=1):
        c = PCOLS[name] + i
        return sb["PAR"][:, c:c + n]

    def rsqrt(dst, ss, inv, n, after=()):
        w = sb["RS"]
        xh, y, t = w[:, 0, 0:n], w[:, 1, 0:n], w[:, 2, 0:n]
        k = ts(DV, xh, ss, inv, EPS, MUL, ADD, after)
        k = ts(DV, t.bitcast(I32), xh.bitcast(I32), 1, None, ALU.logical_shift_right, None, [k])
        k = ts(DV, y.bitcast(I32), t.bitcast(I32), -1.0, float(0x5f3759df), MUL, ADD, [k])
        for i in range(3):
            k = tt(DV, t, y, y, MUL, [k])
            k = stt(t, t, -0.5, xh, MUL, MUL, [k])
            k = stt(dst if i == 2 else y, t, 1.5, y, ADD, MUL, [k])
        return k

    norm_prev = []

    def norm_T(tiles, XN, DG, ring, gain, after, done, side=(), ahead=0):
        side = iter(side)
        nt = len(tiles)
        prev = list(norm_prev)
        ks = []
        for i, t in enumerate(tiles):
            x, acc = sb["XS"][:, t, :], sb["SS"][:, i:i + 1]
            if i % 2 == 0:
                ks.append(act(XN[:, i, :], x, ACT.Square, list(after[i]) + prev, accum=acc))
            else:
                DV.wait(*after[i], *prev)
                ks.append(DV.run(lambda e, o=XN[:, i, :], x=x, acc=acc: e.scalar_tensor_tensor(
                    out=o, in0=x, scalar=1.0, in1=x, op0=MUL, op1=MUL, accum_out=acc)))
        dg = []
        k = rsqrt(sb["SS"][:, 4:4 + nt], sb["SS"][:, 0:nt], 1.0 / 1024, nt, ks + prev)
        for i in range(nt):
            dg.append(ts(DV, DG[:, i, :], IDENT, sb["SS"][:, 4 + i:5 + i], None, MUL, None, [k, T_x]))
        for _ in range(ahead):
            next(side, None)
        for kt in range(8):
            next(side, None)
            b, P, fr = ring.get()
            for i, t in enumerate(tiles):
                tk = mm(P[:, i * 128:(i + 1) * 128], sb["XS"][:, t, kt * 128:(kt + 1) * 128], DG[:, i, :],
                        True, True, fr + [dg[i]] + list(after[i]), inc=i == nt - 1)
            done.setdefault(kt, [])
            done[kt] += gain(kt, b, P, tk)
        norm_prev[:] = [tk, DV.last()]
        drain(side)

    HH, HL = sb["HTH"], sb["HTL"]

    def group_T(P, col, hi, lo, n0, n1, after, xh=None, xl=None, hdone=None):
        xh, xl = xh or HH, xl or HL
        wh, wl = (a.rearrange("p (k c) -> p k c", k=8) for a in (hi, lo))
        o = P[:, col:col + n1 - n0]
        PE.wait(*after)
        hdone = hdone or {}
        for kt in range(8):
            PE.wait(*hdone.get(kt, ()))
            mm(o, wh[:, kt, :], xh[:, kt, n0:n1], kt == 0, False)
            mm(o, wh[:, kt, :], xl[:, kt, n0:n1], False, False)
            tk = mm(o, wl[:, kt, :], xh[:, kt, n0:n1], False, kt == 7, inc=kt == 7)
        return tk

    def group_T_half(P, n, hi, lo, after, part, hdone):
        wh, wl = (a.rearrange("p (k c) -> p k c", k=8) for a in (hi, lo))
        PE.wait(*after)
        for kt in range(4 * part, 4 * part + 4):
            PE.wait(*hdone[kt])
            mm(P[:, 0:n], wh[:, kt, :], HH[:, kt, 0:n], kt == 0, False)
            mm(P[:, 0:n], wh[:, kt, :], HL[:, kt, 0:n], False, False)
            tk = mm(P[:, 0:n], wl[:, kt, :], HH[:, kt, 0:n], False, kt == 7, inc=kt == 7)
        return tk

    def group_N_gen(name, g, tiles, ring, hdone, res, xh=None, xl=None, by_tile=False):
        xh, xl = xh or HH, xl or HL
        n = len(tiles)
        got = [ring.get() for _ in tiles]

        def part(i, t, u, hi, lo):
            wh, wl = (a.rearrange("p (k c) -> p k c", k=2) for a in (hi, lo))
            P = got[i][1]
            PE.wait(*got[i][2])
            s = slice(t * 128, (t + 1) * 128)
            for j in range(2):
                kt = 2 * u + j
                PE.wait(*hdone.get(kt, ()))
                mm(P[:, :], xh[:, kt, s], wh[:, j, :], kt == 0, False)
                mm(P[:, :], xl[:, kt, s], wh[:, j, :], False, False)
                tk = mm(P[:, :], xh[:, kt, s], wl[:, j, :], False, kt == 7, inc=j == 1)
            return tk
        if by_tile:
            us = []
            for u in range(4):
                us.append(get_w(name, g * 4 + u))
            for i, t in enumerate(tiles):
                for u, (hi, lo, wt) in enumerate(us):
                    PE.wait(*wt)
                    tk = part(i, t, u, hi, lo)
                    if i == n - 1:
                        put_w(tk, 3 - u)
                res.append((got[i][0], got[i][1], tk))
                yield
            return
        for u in range(4):
            hi, lo, wt = get_w(name, g * 4 + u)
            PE.wait(*wt)
            toks = [part(i, t, u, hi, lo) for i, t in enumerate(tiles)]
            put_w(toks[-1])
            if u == 3:
                res += [(got[i][0], got[i][1], toks[i]) for i in range(n)]
            yield

    def group_N(*a, **k):
        res = []
        drain(group_N_gen(*a, res, **k))
        return res

    def drain(g):
        for _ in g:
            pass

    def weave(main, side, ratio=1):
        live = True
        acc = 0.0
        for _ in main:
            acc += ratio
            while live and acc >= 1:
                try:
                    acc -= next(side) or 1
                except StopIteration:
                    live = False
        if live:
            drain(side)

    lo4, hi4 = Ring([0, 1, 2, 3]), Ring([4, 5, 6, 7])
    ada_ring = Ring([7])
    low7 = Ring([0, 1, 2, 3, 4, 5, 6])
    all8 = Ring(list(range(8)))

    c, cs = par("c", 0, 16), sb["CS"]
    k = act(cs[:, 0, :], c, ACT.Tanh, [T_x], scale=0.5)
    k = stt(cs[:, 1, :], cs[:, 0, :], 1.0, c, ADD, MUL, [k])
    t_cs = ts(DV, cs[:, 1, :], cs[:, 1, :], 0.5, None, MUL, None, [k])
    mod_done = {0: [], 1: []}

    def ada_steps():
        MT = sb["MODT"]
        for l in range(2):
            for g in range(6):
                b, P, fr = ada_ring.get()
                for u in range(4):
                    w, _, wt = get_w("w_ada", l * 24 + g * 4 + u, kind="raw")
                    PE.wait(t_cs, *fr, *wt)
                    for j in range(2):
                        kt = 2 * u + j
                        tk = mm(P[0:2, :], cs[:, 1, kt * 2:kt * 2 + 2], w[:, j * 512:(j + 1) * 512], kt == 0, kt == 7,
                                inc=j == 1)
                    put_w(tk)
                    if u < 3:
                        yield
                k = act(sb["AROW"][0:2, :], P[0:2, :], ACT.Copy, [tk, PE.last()])
                yield
                for j in range(4):
                    tk = tp(P[:, 2 * j:2 * j + 2], sb["AROW"][0:2, j * 128:(j + 1) * 128], IDENT[0:2, 0:2], [k],
                            inc=j == 3)
                k = tt(DV, MT[:, l, 4 * g:4 * g + 4, :], P[:, 0:8].rearrange("p (j s) -> p j s", j=4),
                       V(par("b_ada", l * 24 + 4 * g, 4), [1, 4], [0, 2]), ADD, [tk])
                let(b, k)
                if g == 5:
                    k2 = stt(sb["GP"][:, l, :, :], MT[:, l, 8:16, :], 1.0, V(par("g_pre", l * 8, 8), [1, 8], [0, 2]),
                             ADD, MUL, [k])
                    mod_done[l] = [k, k2]
                yield "group"
    ada = ada_steps()

    def fill_ada(groups):
        for _ in range(groups):
            for end in ada:
                yield
                if end:
                    break

    BIAS = sb["BIAS"]

    def bias_strips():
        b, P, fr = hi4.get()
        tk = mm(P[0:12, 0:384], sb["RB"][0:32, 0:12], sb["OH"][0:32, 0:384], True, True, fr + [T_bias_in], inc=True)
        t1 = tt(DV, sb["RROW"][0:12, :], P[0:12, 0:384], sb["MROW"][0:12, 0:384], ADD, [tk, T_bias_in])
        let(b, t1)
        rd = Dma(sems["bias"])
        tr = rd.start(PO, A["rscr"], V(sb["RROW"][0:12, :], [0, 128], [1, 384]), [t1])
        src = A["rscr"]
        for part in range(3):
            o = 128 if part == 0 else (part - 1) * 128
            t_bias = rd.start(PO, BIAS[:, :, part * 128:(part + 1) * 128],
                              bass.AP(src.tensor, src.offset + 127 + o, [[383, 128], [128 * 384, 12], [1, 128]]), [tr])
        return t_bias

    QKT, VN, YN, QKN = sb["QKT"], sb["VN"], sb["YN"], sb["QKN"]
    x_done = [[T_x], [T_x]]
    for l in range(2):
        lam_init = 0.8 - 0.6 * math.exp(-0.3 * l)
        sm = sb["SM"]
        lr = sb["LAMR"]
        k = []
        for j in range(2):
            a0 = (l * 4 + 2 * j) * 64
            k1 = tt(DV, sb["LT"][:, 0:64], lr[:, a0:a0 + 64], lr[:, a0 + 64:a0 + 128], MUL, [T_bias_in, T_x, DV.last()])
            k2 = red(sm[:, j:j + 1], sb["LT"][:, 0:64], ADD, [k1])
            k.append(act(sm[:, 2 + j:3 + j], sm[:, j:j + 1], ACT.Exp, [k2]))
        k1 = tt(DV, sm[:, 4:5], sm[:, 3:4], sm[:, 2:3], SUB, k)
        t_lam = ts(DV, sm[:, 5:6], sm[:, 4:5], -lam_init, None, ADD, None, [k1])
        ts(DV, sm[:, 6:7], par("qkg", l * 4), 0.125, None, MUL, None, [T_x])
        ts(DV, sm[:, 7:8], par("qkg", l * 4 + 2), 0.125, None, MUL, None)
        t_cols = ts(DV, sm[:, 8:9], par("subg", l), 1.0 - lam_init, None, MUL, None)

        def gain1(name):
            def f(kt, b, P, tk):
                g = par(name, l * 8 + kt)
                a = act(HH[:, kt, 0:256], P[:, 0:256], ACT.Copy, [tk], scale=g)
                d = stt(HL[:, kt, 0:256], P[:, 0:256], g, HH[:, kt, 0:256].bitcast(F32), MUL, SUB, [a])
                let(b, d)
                return [a, d]
            return f
        mark(f"b1.{l} norm")
        hd = {}
        norm_T((0, 1), sb["XN1"], sb["DG1"], low7, gain1("ln_attn"), x_done, hd,
               fill_ada(2), 5)
        if l == 0:
            t_bias = bias_strips()
            t_mask = copy(DV, sb["MASK"][:, :], sb["MASKF"][:, :], [T_const])

        mark(f"b1.{l} qkv")
        qk_done, v_done = {}, {}
        pend = None
        FQ = fence()

        def qk_finish(sec, kn):
            for half in range(2):
                b, P, fr = all8.get()
                PE.wait(*fr)
                for f in range(2):
                    for t in range(2):
                        ft = half * 2 + f
                        tk = tp(P[:, (f * 2 + t) * 128:(f * 2 + t + 1) * 128],
                                QKN[:, sec % 2, t, ft * 128:(ft + 1) * 128], IDENT, [kn[t]], inc=f == 1 and t == 1)
                base = {0: 0, 1: 4, 3: 8, 4: 12}[sec] + half * 2
                g = {0: sm[:, 6:7], 1: par("qkg", l * 4 + 1), 3: sm[:, 7:8], 4: par("qkg", l * 4 + 3)}[sec]
                o = QKT[:, base:base + 2, :].rearrange("p a b -> p (a b)")
                t = act(o, P[:, :], ACT.Copy, [tk, t_cols] + FQ, scale=g)
                let(b, t)
                qk_done[(sec, half)] = t
        for sec in range(6):
            got = group_N(f"w_in{l}", sec, (0, 1), all8, hd)
            if pend is not None:
                qk_finish(*pend)
                pend = None
            if sec in (2, 5):
                for t, (b, P, tk) in enumerate(got):
                    k = act(VN[:, t, (sec == 5) * 512:(sec == 5) * 512 + 512], P[:, :], ACT.Copy, [tk])
                    let(b, k)
                    v_done[(sec, t)] = k
                continue
            ks = []
            for t, (b, P, tk) in enumerate(got):
                k = act(sb["SQ"][:, t, :], P[:, :], ACT.Square, [tk, DV.last()])
                ks.append(red(sb["QS"][:, 0, t * 8:t * 8 + 8], sb["SQ"][:, t, :].rearrange("p (h d) -> p h d", d=64),
                              ADD, [k]))
            k = rsqrt(sb["QS"][:, 1, 0:16], sb["QS"][:, 0, 0:16], 1.0 / 64, 16, ks)
            kn = []
            for t, (b, P, tk) in enumerate(got):
                k2 = tt(DV, QKN[:, sec % 2, t, :].rearrange("p (h d) -> p h d", d=64),
                        P[:, :].rearrange("p (h d) -> p h d", d=64),
                        V(sb["QS"][:, 1, t * 8:t * 8 + 1], [1, 8], [0, 64]), MUL, [k, PE.last()])
                let(b, k2)
                kn.append(k2)
            pend = (sec, kn)

        mark(f"b1.{l} attn")
        R = sb["RR"]
        E3, PT = sb["E3"], sb["PT3"]
        FA = fence()
        e_done, e_free, pt_free = {}, [FA] * 4, [FA] * 2
        y_done = []
        sc_ring, tp_ring, pv_ring = Ring([0, 1, 2]), Ring([3, 4]), Ring([5, 6])
        pv = {}

        def scores(u):
            s, fam = u % 8, u // 8
            half, ft = s % 2, s // 2
            hb = s // 2 if fam == 0 else 4 + s
            b, P, fr = sc_ring.get()
            p0 = half * 64
            q = QKT[p0:p0 + 64, fam * 8 + ft, :]
            kk = QKT[p0:p0 + 64, fam * 8 + 4 + ft, :]
            PE.wait(*fr, qk_done[(fam * 3, ft // 2)], qk_done[(fam * 3 + 1, ft // 2)])
            mm(P[:, 0:128], q[:, 0:128], kk[:, 0:128], True, True)
            tk = mm(P[:, 128:384], q[:, 128:256], kk[:, 0:256], True, True, inc=True)
            e = u % 4
            LG = E3[:, e, :]
            k = tt(DV, LG, P[:, 0:384], BIAS[:, hb, :], ADD, [tk, t_bias] + e_free[e])
            let(b, k)
            ka = red(R[:, 0, 2 * u:2 * u + 1], LG[:, 0:128], MAX, [k], negate=True)
            kb = red(R[:, 0, 2 * u + 1:2 * u + 2], LG[:, 128:384], MAX, [k], negate=True)
            act(LG[:, 0:128], LG[:, 0:128], ACT.Exp, [ka], bias=R[:, 0, 2 * u:2 * u + 1],
                accum=R[:, 1, 2 * u:2 * u + 1])
            ke = act(LG[:, 128:384], LG[:, 128:384], ACT.Exp, [kb], bias=R[:, 0, 2 * u + 1:2 * u + 2],
                     accum=R[:, 1, 2 * u + 1:2 * u + 2])
            ex_done[u] = ke

        def probs(u):
            s, fam = u % 8, u // 8
            half, ft = s % 2, s // 2
            LG = E3[:, u % 4, :]
            ke = ex_done[u]
            kr = DV.run(lambda e_: e_.reciprocal(R[:, 2, 2 * u:2 * u + 2], R[:, 1, 2 * u:2 * u + 2]), [ke])
            if fam == 0:
                if half == 0:
                    k = ts(DV, LG[:, 0:128], LG[:, 0:128], R[:, 2, 2 * u:2 * u + 1], None, MUL, None, [kr])
                    k = ts(DV, LG[:, 128:384], LG[:, 128:384], R[:, 2, 2 * u + 1:2 * u + 2], None, MUL, None, [k])
                    e_done[u] = k
                else:
                    kl = tt(DV, R[:, 3, 2 * u:2 * u + 2], R[:, 2, 2 * u:2 * u + 2],
                            V(sm[:, 5:6], [0, 2]), MUL, [kr, t_lam])
                    prev = E3[:, (u - 1) % 4, :]
                    k = stt(LG[:, 0:128], LG[:, 0:128], R[:, 3, 2 * u:2 * u + 1], prev[:, 0:128], MUL, ADD,
                            [kl, e_done[u - 1]])
                    k = stt(LG[:, 128:384], LG[:, 128:384], R[:, 3, 2 * u + 1:2 * u + 2], prev[:, 128:384], MUL, ADD,
                            [k])
                    e_free[(u - 1) % 4] = [k]
                    e_done[u] = k
            else:
                e_done[u] = kr

        def trans(u):
            e = u % 4
            b, P, fr = tp_ring.get()
            PE.wait(*fr, e_done[u])
            for j in range(3):
                tk = tp(P[:, j * 128:(j + 1) * 128], E3[:, e, j * 128:(j + 1) * 128], IDENT, inc=j == 2)
            e_free[e] = [tk]
            w = u % 2
            k = act(PT[:, w, :], P[:, 0:384], ACT.Copy, [tk] + pt_free[w])
            let(b, k)
            pt_done[u] = k
        pt_done, ex_done = {}, {}

        def values(u):
            w = u % 2
            fam = u // 8
            s = u % 8
            if fam == 0:
                h, dv, per = s // 2, 128, 2
                c0 = h * 128
            else:
                h, dv, per = s, 64, 4
                c0 = 512 + h * 64
            i = h % per
            if i == 0:
                pv[fam] = pv_ring.get()
            b, P, fr = pv[fam]
            PE.wait(*fr, pt_done[u], *v_done.values())
            o = P[:, :].rearrange("p (i t d) -> p i t d", i=per, t=2)
            mm(o[:, i, 0, :], PT[:, w, 0:128], VN[:, 0, c0:c0 + dv], True, True)
            mm(o[:, i, 1, :], PT[:, w, 128:256], VN[:, 0, c0:c0 + dv], True, False)
            tk = mm(o[:, i, 1, :], PT[:, w, 256:384], VN[:, 1, c0:c0 + dv], False, True, inc=True)
            pt_free[w] = [tk]
            if i < per - 1:
                return
            cb = c0 - i * dv
            yo = V(YN[:, 0, cb:cb + 1], [dv, per], [1024, 2], [1, dv])
            if fam == 1:
                r0 = 2 * (u - per + 1)
                k = tt(DV, yo, o, V(R[:, 2, r0:r0 + 1], [2, per], [1, 2], [0, dv]), MUL, [tk])
                let(b, k)
                y_done.append(k)
            else:
                k = act(sb["SQ"][:, 0, :], P[:, :], ACT.Square, [tk, DV.last()])
                k = red(sb["QS"][:, 0, 0:4], sb["SQ"][:, 0, :].rearrange("p (g d) -> p g d", d=128), ADD, [k])
                k = rsqrt(sb["QS"][:, 1, 0:4], sb["QS"][:, 0, 0:4], 1.0 / 128, 4, [k])
                k = tt(DV, yo, o, V(sb["QS"][:, 1, 0:1], [2, per], [1, 2], [0, dv]), MUL, [k])
                let(b, k)
                y_done.append(k)

        def attn1():
            us = [u for u in range(16)]
            tr_ = [u for u in us if u >= 8 or u % 2 == 1]
            ev = []
            for u in range(20):
                if u < 16:
                    scores(u)
                if 0 <= u - 1 < 16:
                    probs(u - 1)
                if u - 2 in tr_:
                    trans(u - 2)
                if u - 3 in tr_:
                    values(u - 3)
                yield
        weave(attn1(), fill_ada(3), 0.8)
        mark(f"b1.{l} wout")
        yd = {}
        for kt2 in range(4):
            b, P, fr = all8.get()
            PE.wait(*fr, *y_done)
            for f in range(2):
                for t in range(2):
                    kt = kt2 * 2 + f
                    tk = tp(P[:, (f * 2 + t) * 128:(f * 2 + t + 1) * 128], YN[:, t, kt * 128:(kt + 1) * 128], IDENT,
                            inc=f == 1 and t == 1)
            oh = HH[:, kt2 * 2:kt2 * 2 + 2, 0:256]
            ol = HL[:, kt2 * 2:kt2 * 2 + 2, 0:256]
            Pv = P[:, :].rearrange("p (f n) -> p f n", f=2)
            g = sm[:, 8:9] if kt2 < 2 else 1.0
            a = act(oh, Pv, ACT.Copy, [tk, t_cols], scale=g)
            d = stt(ol, Pv, g, oh.bitcast(F32), MUL, SUB, [a])
            let(b, d)
            yd[2 * kt2] = yd[2 * kt2 + 1] = [a, d]
        xd = [[], []]
        for g in range(2):
            for t, (b, P, tk) in enumerate(group_N(f"w_out{l}", g, (0, 1), all8, yd, by_tile=g == 1)):
                xs = sb["XS"][:, t, g * 512:(g + 1) * 512]
                k = tt(DV, xs, P[:, :], xs, ADD, [tk])
                let(b, k)
                xd[t].append(k)

        mark(f"b1.{l} norm2")
        hd = {}
        norm_T((0, 1), sb["XN1"], sb["DG1"], low7, gain1("ln_ffn"), xd, hd, fill_ada(1), 2)
        mark(f"b1.{l} ffn")
        up_ring = Ring([0, 1, 2, 3])
        accs = [(i, banks[i], free[i]) for i in (4, 5, 6, 7)]
        for i in (4, 5, 6, 7):
            free[i] = None
        FF = fence()
        f_free = [FF, FF]
        a_free = [[], [], []]
        a_done = {}

        def ff_up(j):
            b, P, fr = up_ring.get()
            for side in range(2):
                hi, lo, wt = get_w(f"w_up{l}", side * FF_TILES + j)
                tk = group_T(P, side * 256, hi, lo, 0, 256, fr + wt, hdone=hd)
                put_w(tk)
            i = j % 2
            C = sb["FC"]
            outs = []
            for side in range(2):
                ft = side * FF_TILES + j
                w = [par("cw", (l * 3 + q) * 44 + ft) for q in range(3)]
                c = C[:, i, side, :]
                u = P[:, side * 256:(side + 1) * 256]
                outs.append(act(c, u, ACT.Identity, [tk] + f_free[i], scale=w[2], bias=par("cb", l * 44 + ft)))
            for side in range(2):
                ft = side * FF_TILES + j
                w = [par("cw", (l * 3 + q) * 44 + ft) for q in range(3)]
                c = C[:, i, side, :]
                u = P[:, side * 256:(side + 1) * 256]
                k = stt(c[:, 1:256], u[:, 0:255], w[1], c[:, 1:256], MUL, ADD, [outs[1]])
                k = stt(c[:, 2:256], u[:, 0:254], w[0], c[:, 2:256], MUL, ADD, [k])
                outs[side] = k
            let(b, k)
            th = sb["FT"][:, i, :]
            kt_ = act(th, C[:, i, 0, :], ACT.Tanh, [outs[0]], scale=0.5)
            k = stt(th, th, 1.0, C[:, i, 0, :], ADD, MUL, [kt_])
            k = stt(th, th, 0.5, C[:, i, 1, :], MUL, MUL, [k, outs[1]])
            s = j % 3
            kh = act(sb["AH"][:, s, :], th, ACT.Copy, [k] + a_free[s])
            kl = tt(PO, sb["AL"][:, s, :], th, sb["AH"][:, s, :].bitcast(F32), SUB, [kh] + a_free[s])
            f_free[i] = [k, kh, kl]
            a_done[j] = [kh, kl]

        def ff_down(j):
            hi, lo, wt = get_w(f"w_down{l}", j)
            s = j % 3
            PE.wait(*wt, *a_done[j])
            for t in range(2):
                for g in range(2):
                    b, P, fr = accs[t * 2 + g]
                    PE.wait(*fr)
                    xh, xl = sb["AH"][:, s, t * 128:(t + 1) * 128], sb["AL"][:, s, t * 128:(t + 1) * 128]
                    wh, wl = hi[:, g * 512:(g + 1) * 512], lo[:, g * 512:(g + 1) * 512]
                    mm(P[:, :], xh, wh, j == 0, False)
                    mm(P[:, :], xl, wh, False, False)
                    tk = mm(P[:, :], xh, wl, False, j == FF_TILES - 1, inc=True)
            put_w(tk)
            a_free[s] = [tk]
            return tk
        for j in range(FF_TILES + 2):
            if j < FF_TILES:
                ff_up(j)
            if j >= 2:
                tk = ff_down(j - 2)
        x_done = [[], []]
        for t in range(2):
            for g in range(2):
                b, P, _ = accs[t * 2 + g]
                xs = sb["XS"][:, t, g * 512:(g + 1) * 512]
                k = tt(DV, xs, P[:, :], xs, ADD, [tk])
                let(b, k)
                x_done[t].append(k)

    mark("ada")
    mark("ada")
    drain(ada)

    mark("b2")
    spill = [Dma(sems["sp0"]), Dma(sems["sp1"])]
    sp_done = [spill[0].start(PO, A["xscr"][0, 0:256, :].rearrange("(t p) d -> p t d", p=128),
                              sb["XS"][:, 0:2, :], x_done[0] + x_done[1])]
    sp_done.append(spill[1].start(PO, A["xscr"][0, 256:512, :].rearrange("(t p) d -> p t d", p=128),
                                  sb["XS"][:, 2:4, :], [T_const]))
    x_done += [[T_const], [T_const]]
    gdma, tdma, wdma, rdma = Dma(sems["gd"]), Dma(sems["td"]), Dma(sems["wd"]), Dma(sems["rdl"])
    odma = Dma(sems["out"])
    MT, GP = sb["MODT"], sb["GP"]
    ASC = 128 ** -0.5
    for l in range(2):
        last = l == 1
        NT = 256 if last else 512
        streams = (0,) if last else (1, 0)
        mark(f"b2.{l} norm")
        F0 = [x for v in x_done for x in v] if l else fence()
        tabs = []
        for i, nm in enumerate(("q", "k")):
            tabs.append(tdma.start(PO, sb["GN"][:, i, :], V(A["qkn"][l * 2 + i:l * 2 + i + 1, :], [1, 128])
                                   if False else bass.AP(A["qkn"].tensor, A["qkn"].offset + (l * 2 + i) * 128,
                                                         [[0, 128], [1, 128]]), F0))
            tabs.append(tdma.start(PO, sb["ROPE"][:, i, :, :, :], A["rope"], F0))
        tt_ = tabs[-1]
        k = ts(DV, sb["GN"][:, 0, :], sb["GN"][:, 0, :], ASC, None, MUL, None, [tt_])
        t_rope = []
        for i in range(2):
            g = sb["GN"][:, i, :]
            t_rope.append(tt(DV, sb["ROPE"][:, i, 0, :, :], sb["ROPE"][:, i, 0, :, :],
                             V(g, [0, 2], [1, 128]), MUL, [tt_, k]))
            for t in range(2):
                for hf in range(2):
                    o = V(sb["ROPE"][:, i, 1, t, hf * 32:hf * 32 + 1], [64, 2], [1, 32])
                    t_rope.append(tt(DV, o, o, V(sb["GN"][:, i, (1 - hf) * 32:(1 - hf) * 32 + 1], [64, 2], [1, 32]),
                                     MUL, [tt_, k]))
        t_wd = wdma.start(PO, sb["WDEC"][:, :], A["wdec"][l, :, :], F0)

        def gain2(kt, b, P, tk):
            w = sb["HV"][:, kt % 2, :]
            ds = []
            for s in range(2):
                ds.append(ts(DV, w[:, s * 256:(s + 1) * 256], P[:, s * 256:(s + 1) * 256], GP[:, l, kt, s:s + 1],
                             MT[:, l, kt, s:s + 1], MUL, ADD, [tk] + hv_free[kt % 2] + mod_done[l]))
            let(b, ds[1])
            a = act(HH[:, kt, :], w, ACT.Copy, ds)
            d = tt(PO if kt % 2 else DV, HL[:, kt, :], w, HH[:, kt, :].bitcast(F32), SUB, [a])
            hv_free[kt % 2] = [a, d]
            return [a, d]
        hv_free = [[], []]
        hd = {}
        norm_T((0, 1, 2, 3), sb["XN2"], sb["DG2"], all8, gain2, [F0] * 4, hd)
        mark(f"b2.{l} gla in")
        F1 = fence()

        GQ, GK, GV = sb["GQ"], sb["GK"], sb["GV"]
        tiles4 = (0, 1, 2, 3)
        hi, lo, wt = get_w(f"wr{l}", 0, cols=256)
        b, P, fr = all8.get()
        wh, wl = (a.rearrange("p (k c) -> p k c", k=8) for a in (hi, lo))
        PE.wait(*wt, *fr)
        for kt in range(8):
            PE.wait(*hd[kt])
            mm(P[0:32, :], wh[:, kt, :], HH[:, kt, :], kt == 0, False)
            mm(P[0:32, :], wh[:, kt, :], HL[:, kt, :], False, False)
            tk = mm(P[0:32, :], wl[:, kt, :], HH[:, kt, :], False, kt == 7, inc=kt == 7)
        put_w(tk)
        k_rt = act(sb["RT"][0:32, :], P[0:32, :], ACT.Copy, [tk] + F1)
        let(b, k_rt)
        k1s = DV.run(lambda e: e.memset(sb["RT"][32:33, :], 1.0), F1)
        for ft in range(4):
            hi, lo, wt = get_w(f"wgk{l}", ft)
            b, P, fr = all8.get()
            tk = group_T(P, 0, hi, lo, 0, 512, fr + wt, hdone=hd)
            put_w(tk)
            k = act(GK[:, ft, :], P[:, :], ACT.Copy, [tk] + F1)
            let(b, k)
            gk_done = k
        for ft in range(4):
            hi, lo, wt = get_w(f"wgq{l}", ft)
            b, P, fr = all8.get()
            tk = group_T(P, 0, hi, lo, 0, NT, fr + wt, hdone=hd)
            put_w(tk)
            k = act(GQ[:, ft, 0:NT], P[:, 0:NT], ACT.Copy, [tk] + F1, scale=ASC)
            let(b, k)
            gq_done = k
        for g in range(2):
            for t, (b, P, tk) in enumerate(group_N(f"wgv{l}", g, tiles4, all8, hd)):
                k = act(GV[:, t, g * 512:(g + 1) * 512], P[:, :], ACT.Copy, [tk] + F1)
                let(b, k)
                gv_done = k

        def gla(ring):
            LA, E4, B, TRI = sb["LA"], sb["E4"], sb["BC"], sb["TRI"]
            attT, attX, ST, KE = sb["ATT"], sb["ATX"], sb["ST"], sb["KE"]
            state_done = []
            for s in (1, 0):
                full = s in streams
                F = fence() + sp_done
                got, ks, la = {}, {}, []
                for i in range(5):
                    if i < 4:
                        b, P, fr = ring.get()
                        c = s * 256 + (i // 2) * 128
                        tk = mm(P[:, :], sb["RT"][0:33, c:c + 128], sb["WDEC"][:, (i % 2) * 512:(i % 2 + 1) * 512],
                                True, True, fr + [k_rt, t_wd, k1s], inc=True)
                        got[i] = (b, P, tk)
                    if i >= 1:
                        b, P, tk = got[i - 1]
                        ka = act(E4[:, i - 1, :], P[:, :], ACT.Abs, [tk] + F)
                        kb = ts(DV, LA[:, i - 1, :], P[:, :], 0.0, None, MIN, None, [ka] + F)
                        let(b, kb)
                        ks[i - 1] = (act(E4[:, i - 1, :], E4[:, i - 1, :], ACT.Exp, [ka], scale=-1.0), kb)
                    yield
                for i in range(4):
                    k = act(E4[:, i, :], E4[:, i, :], ACT.Ln, [ks[i][0], t_one], bias=sb["ONE"][:, 0:1])
                    la.append(tt(DV, LA[:, i, :], LA[:, i, :], E4[:, i, :], SUB, [k, ks[i][1]]))
                yield
                bd = []
                for i in range(5):
                    if i < 4:
                        d, hp = i // 2, i % 2
                        b, P, fr = ring.get()
                        PE.wait(*fr, *la)
                        for hh in range(2):
                            h = hp * 2 + hh
                            o = hh * 256
                            sl = slice(h * 128, (h + 1) * 128)
                            if d == 0:
                                mm(P[:, o:o + 256], LA[:, 0, sl], TRI[:, 0:256], True, False)
                                tk = mm(P[:, o + 128:o + 256], LA[:, 2, sl], TRI[:, 0:128], False, True, inc=True)
                            else:
                                mm(P[:, o:o + 256], LA[:, 3, sl], TRI[:, 128:384], True, False)
                                tk = mm(P[:, o:o + 128], LA[:, 1, sl], TRI[:, 256:384], False, True, inc=True)
                        got[i] = (b, P, tk)
                    if i >= 1:
                        d, hp = (i - 1) // 2, (i - 1) % 2
                        b, P, tk = got[i - 1]
                        k = act(B[:, d, hp * 2:hp * 2 + 2, :].rearrange("p h n -> p (h n)"), P[:, :], ACT.Copy, [tk] + F)
                        let(b, k)
                        bd.append(k)
                    yield
                q = GQ[:, :, s * 256:(s + 1) * 256]
                kk = GK[:, :, s * 256:(s + 1) * 256]
                sdone = bd + [gk_done, gq_done, gv_done, la[-1]]
                ad = [None, None]
                xd_ = []
                items = []
                if full:
                    items = [("diag", hp, 0) for hp in range(2)]
                    items += [("level", d, h) for d in range(2) for h in LEVELS]
                    items += [("cross", d, 128) for d in range(2)]
                items += [("edge", d, 0) for d in range(2)]
                n = len(items)
                slot, mslot, c = {}, {}, 0
                MBS = [sb[f"MB{i}"][:, :, :] for i in range(3)]
                for j, it in enumerate(items):
                    if it[0] != "diag":
                        slot[j], mslot[j] = c % 2, c % 3
                        c += 1
                e_done, m_done, c_done = {}, {}, {}
                m_free = [list(F), list(F), list(F)]
                e_free = [list(F), list(F)]

                def views(h):
                    nb = 1024 // (2 * h)
                    up = lambda a: V(a, [2 * h, nb], [1, h], off=h)
                    dn = lambda a: V(a, [2 * h, nb], [1, h])
                    per = lambda a, st_, off: V(a, [st_, 4], [2 * h, 128 // h], [1, h], off=off)
                    return nb, up, dn, per

                def decay(j):
                    kind, d, h = items[j]
                    if kind == "diag":
                        return
                    i = slot[j]
                    E, bv = sb["EB"][:, i, :, :], B[:, d, :, :]
                    if kind == "edge":
                        if s == 0:
                            e_done[j] = act(E, bv, ACT.Exp, e_free[i] + sdone)
                        else:
                            end = V(bv, [256, 4], [0, 256], off=255 if d == 0 else 0)
                            k1 = tt(DV, E, end, bv, SUB, e_free[i] + sdone)
                            e_done[j] = act(E, E, ACT.Exp, [k1])
                        return
                    nb, up, dn, per = views(h)
                    ref = V(bv, [2 * h, nb], [0, h], off=h - 1 if d == 0 else h)
                    hi_, lo_ = (up, dn) if d == 0 else (dn, up)
                    k1 = tt(DV, hi_(E), hi_(bv), ref, SUB, e_free[i] + sdone)
                    k2 = tt(DV, lo_(E), ref, lo_(bv), SUB)
                    e_done[j] = act(E, E, ACT.Exp, [k2] + sdone)

                def scale(j):
                    kind, d, h = items[j]
                    if kind == "diag":
                        return
                    i = slot[j]
                    E, M = sb["EB"][:, i, :, :], MBS[mslot[j]]
                    if kind == "edge":
                        k = tt(DV, M, q if s == 0 else kk, E, MUL, [e_done[j]] + m_free[mslot[j]] + sdone)
                        m_done[j] = e_free[i] = [k]
                        return
                    nb, up, dn, per = views(h)
                    qo, ko = (h, 0) if d == 0 else (0, h)
                    k1 = tt(PO if h >= 4 else DV, per(M, 256, qo), per(q, 512, qo), per(E, 256, qo), MUL,
                            [e_done[j]] + m_free[mslot[j]] + sdone)
                    k2 = tt(DV, per(M, 256, ko), per(kk, 512, ko), per(E, 256, ko), MUL,
                            [e_done[j]] + m_free[mslot[j]] + sdone)
                    m_done[j] = e_free[i] = [k1, k2]

                def product(j):
                    kind, d, h = items[j]
                    if kind == "edge":
                        return
                    r = []
                    if kind == "cross":
                        b, P, fr = ring.get()
                        PE.wait(*fr, *m_done[j])
                        M = MBS[mslot[j]]
                        for x in range(4):
                            kp = M[:, x, 0:128] if d == 0 else M[:, x, 128:256]
                            qp = M[:, x, 128:256] if d == 0 else M[:, x, 0:128]
                            tk = mm(P[:, x * 128:(x + 1) * 128], kp, qp, True, True, inc=x == 3)
                        r.append((b, P, tk, 0))
                    else:
                        for hp in ((d,) if kind == "diag" else range(2)):
                            b, P, fr = ring.get()
                            PE.wait(*fr, *(sdone if kind == "diag" else m_done[j]))
                            for x in range(4):
                                hd_, sl = hp * 2 + x // 2, slice((x % 2) * 128, (x % 2 + 1) * 128)
                                if kind == "diag":
                                    l_, r_ = kk[:, hd_, sl], q[:, hd_, sl]
                                else:
                                    l_ = r_ = MBS[mslot[j]][:, hd_, sl]
                                tk = mm(P[:, x * 128:(x + 1) * 128], l_, r_, True, True, inc=x == 3)
                            r.append((b, P, tk, hp))
                    if kind != "diag":
                        m_free[mslot[j]] = [tk]
                    c_done[j] = r

                def keep(j):
                    kind, d, h = items[j]
                    for b, P, tk, hp in c_done.get(j, ()):
                        P4 = P[:, :].rearrange("p (a n) -> p a n", a=4)
                        o = attT[:, hp * 4:hp * 4 + 4, :]
                        if kind == "diag":
                            k = ad[hp] = stt(o, P4, 2.0, V(sb["IDENT"][:, 0:1], [0, 4], [1, 128]), MUL, MUL, [tk] + F)
                        elif kind == "level":
                            m0 = (d * 7 + LEVELS.index(h)) * 128
                            mk = V(sb["MASK"][:, m0:m0 + 1], [0, 4], [1, 128])
                            k = ad[hp] = DV.run(lambda e, o=o, mk=mk, P4=P4: e.copy_predicated(o, mk, P4),
                                                [tk, ad[hp], t_mask])
                        else:
                            k = act(attX[:, d * 4:d * 4 + 4, :], P4, ACT.Copy, [tk] + F)
                            xd_.append(k)
                        let(b, k)

                for j in range(n + 4):
                    if j < n:
                        decay(j)
                    if 0 <= j - 4 < n:
                        keep(j - 4)
                    if 0 <= j - 3 < n:
                        product(j - 3)
                    if 0 <= j - 1 < n:
                        scale(j - 1)
                    yield 2
                dm = [(MBS[mslot[n - 2 + d]], m_done[n - 2 + d]) for d in range(2)]
                if s == 1:
                    got = {}
                    for i in range(7):
                        if i < 4:
                            d, hp = i // 2, i % 2
                            M, km = dm[d]
                            b, P, fr = ring.get()
                            PE.wait(*fr, *km)
                            for hh in range(2):
                                for t in range(2):
                                    tk = tp(P[:, (hh * 2 + t) * 128:(hh * 2 + t + 1) * 128],
                                            M[:, hp * 2 + hh, t * 128:(t + 1) * 128], IDENT, inc=hh == 1 and t == 1)
                            k = act(KE[:, i, :, :].rearrange("p a n -> p (a n)"), P[:, :], ACT.Copy,
                                    [tk] + dm[0][1] + dm[1][1])
                            let(b, k)
                            got[i] = k
                        if 1 <= i < 5:
                            d, hp = (i - 1) // 2, (i - 1) % 2
                            b, P, fr = ring.get()
                            PE.wait(*fr, got[i - 1])
                            for hh in range(2):
                                h = hp * 2 + hh
                                for t in range(2):
                                    tk = mm(P[:, hh * 256:(hh + 1) * 256], KE[:, i - 1, hh * 2 + t, :],
                                            GV[:, 2 + t, h * 256:(h + 1) * 256], t == 0, t == 1, inc=t == 1)
                            got[10 + i] = (b, P, tk)
                        if 2 <= i < 6:
                            d, hp = (i - 2) // 2, (i - 2) % 2
                            b, P, tk = got[10 + i - 1]
                            k = act(ST[:, d, hp * 2:hp * 2 + 2, :].rearrange("p a n -> p (a n)"), P[:, :],
                                    ACT.Copy, [tk] + F)
                            let(b, k)
                            state_done.append(k)
                        yield
                if not full:
                    continue
                for h in range(5):
                    if h < 4:
                        b, P, fr = ring.get()
                        PE.wait(*fr, *ad, *xd_)
                        if s == 0:
                            PE.wait(*state_done, *dm[0][1], *dm[1][1])
                        vh = [GV[:, s * 2 + t, h * 256:(h + 1) * 256] for t in range(2)]
                        for t in range(2):
                            o = P[:, t * 256:(t + 1) * 256]
                            mm(o, attT[:, h * 2 + t, :], vh[t], True, False)
                            if s == 0:
                                for d in range(2):
                                    mm(o, dm[d][0][:, h, t * 128:(t + 1) * 128], ST[:, d, h, :], False, False)
                            tk = mm(o, attX[:, (1 - t) * 4 + h, :], vh[1 - t], False, True, inc=True)
                        got[h] = (b, P, tk)
                    if h >= 1:
                        b, P, tk = got[h - 1]
                        k = act(V(GV[:, s * 2, (h - 1) * 256:(h - 1) * 256 + 1], [1024, 2], [1, 256]),
                                P[:, :].rearrange("p (t n) -> p t n", t=2), ACT.Copy, [tk])
                        let(b, k)
                    yield
                gs = sb["GSS"]
                F3 = [DV.last(), k]
                for t in range(2):
                    for h in range(4):
                        k = act(sb["SQ2"][:, :], GV[:, s * 2 + t, h * 256:(h + 1) * 256], ACT.Square,
                                F3 + [AC.last()], accum=gs[:, 0, t * 4 + h:t * 4 + h + 1])
                yield
                k = rsqrt(gs[:, 1, 0:8], gs[:, 0, 0:8], 1.0 / 256, 8, [k])
                for t in range(2):
                    v = V(GV[:, s * 2 + t, 0:1], [256, 4], [1, 256])
                    og_done.append(tt(PO, v, v, V(gs[:, 1, t * 4:t * 4 + 1], [1, 4], [0, 256]), MUL, [k]))
                yield
        og_done = []

        AF = sb["AF"]
        fA = fence()
        wk = {"af": [fA, fA]}
        af_done = []
        ns = 1 if last else 2

        def branch_a(ring):
            for ft in range(8):
                i = ft % 2
                c_sb, u_sb, cv = sb["WA"][:, i, 0, 0:NT], sb["WA"][:, i, 1, 0:NT], sb["WA"][:, i, 2, 0:NT]
                pb = {}
                for nm in ("c", "x", "b", "z"):
                    hi, lo, wt = get_w(f"wa{l}", {"b": 0, "c": 8, "x": 16, "z": 24}[nm] + ft)
                    b, P, fr = ring.get()
                    group_T_half(P, NT, hi, lo, fr + wt, 0, hd)
                    yield
                    tk = group_T_half(P, NT, hi, lo, (), 1, hd)
                    put_w(tk)
                    pb[nm] = (b, P[:, 0:NT], tk)
                    if nm == "c":
                        kc = act(c_sb, pb[nm][1], ACT.Copy, [tk] + wk["af"][i])
                        let(b, kc)
                    elif nm == "x":
                        ku = tt(DV, u_sb, P[:, 0:NT], c_sb, MUL, [tk, kc] + wk["af"][i])
                        let(b, ku)
                        w = [par("cw2", (l * 3 + q) * 8 + ft) for q in range(3)]
                        k = act(cv, u_sb, ACT.Copy, [ku] + wk["af"][i], scale=w[1])
                        for s in range(ns):
                            o = s * 256
                            k = stt(cv[:, o + 1:o + 256], u_sb[:, o:o + 255], w[0], cv[:, o + 1:o + 256], MUL, ADD, [k])
                            k = stt(cv[:, o:o + 255], u_sb[:, o + 1:o + 256], w[2], cv[:, o:o + 255], MUL, ADD, [k])
                        kcv = k
                    elif nm == "b":
                        kb = stt(cv, P[:, 0:NT], 0.5, cv, MUL, MUL, [tk, kcv])
                        let(b, kb)
                    else:
                        kt_ = act(c_sb, P[:, 0:NT], ACT.Tanh, [tk, ku], scale=0.5)
                        kz = stt(c_sb, c_sb, 1.0, P[:, 0:NT], ADD, MUL, [kt_])
                        let(b, kz)
                        k = tt(DV, AF[:, ft, 0:NT], c_sb, cv, MUL, [kz, kb] + fA)
                        wk["af"][i] = [k]
                        af_done.append(k)
                    yield
        mark(f"b2.{l} A|gla")
        weave(branch_a(lo4), gla(hi4), RA[l])

        mark(f"b2.{l} kv q")
        F2 = fence()
        ABH, ABL = sb["ABH"], sb["ABL"]

        def split_ab(kt, v, after, n=NT):
            a = act(ABH[:, kt, 0:n], v, ACT.Copy, after)
            d = tt(PO if kt % 2 else DV, ABL[:, kt, 0:n], v, ABH[:, kt, 0:n].bitcast(F32), SUB, [a] + list(after))
            return [a, d]
        ab = {}

        def conv_split():
            for kt in range(8):
                ab[kt] = split_ab(kt, AF[:, kt, 0:NT], F2)
                yield
        QT, KT, VV = sb["QT"], sb["KT"], sb["VV"]
        ro = sb["ROPE"]

        def norm_heads(P, tk, n, i, t, slot, w0):
            sq, qn, t2 = sb["SQ3"], sb["QNB"][:, slot, w0:w0 + n * 128], sb["QT2"]
            k = act(sq[:, 0:n * 128], P, ACT.Square, [tk, DV.last()] + F3)
            k = red(sb["GSS"][:, 0, 0:n], sq[:, 0:n * 128].rearrange("p (h d) -> p h d", d=128), ADD, [k])
            k = rsqrt(sb["GSS"][:, 1, 0:n], sb["GSS"][:, 0, 0:n], 1.0 / 128, n, [k])
            k0 = tt(DV, qn.rearrange("p (h d) -> p h d", d=128), P.rearrange("p (h d) -> p h d", d=128),
                    V(sb["GSS"][:, 1, 0:1], [1, n], [0, 128]), MUL, [k] + qn_free[slot] + F3)
            if t >= 2:
                g = sb["GN"][:, i, :]
                k1 = tt(DV, qn.rearrange("p (h d) -> p h d", d=128), qn.rearrange("p (h d) -> p h d", d=128),
                        V(g, [0, n], [1, 128]), MUL, [k0] + t_rope)
                return k0, k1
            ks = []
            for hf in range(2):
                ks.append(tt(DV, V(t2[:, hf * 32:hf * 32 + 1], [128, n], [64, 2], [1, 32]),
                             V(qn, [128, n], [64, 2], [1, 32], off=(1 - hf) * 32),
                             V(ro[:, i, 1, t, hf * 32:hf * 32 + 1], [0, n], [64, 2], [1, 32]), MUL,
                             [k0, PO.last()] + t_rope + F3))
            k1 = tt(DV, qn.rearrange("p (h d) -> p h d", d=128), qn.rearrange("p (h d) -> p h d", d=128),
                    V(ro[:, i, 0, t, 0:1], [0, n], [1, 128]), MUL, ks)
            k1 = tt(DV, qn, qn, t2[:, 0:n * 128], ADD, [k1])
            return k0, k1
        qn_free = [[], [], [], []]
        q_done, k2_done, v2_done = {}, [], []
        tlist = (0, 1) if last else (0, 1, 2, 3)

        def heads(got, keys, g):
            tl = tiles4 if keys else tlist
            kn = []
            for t, (b, P, tk) in enumerate(got):
                if keys:
                    tk = act(VV[:, t, :], P[:, 256:512], ACT.Copy, [tk] + F2)
                    v2_done.append(tk)
                k0, k1 = norm_heads(P[:, 0:256] if keys else P[:, :], tk, 2 if keys else 4, 1 if keys else 0, t, t, 0)
                let(b, k0)
                kn.append(k1)
                yield
            for h in range(2 if keys else 4):
                b, P, fr = all8.get() if keys or g == 0 else hi4.get()
                PE.wait(*fr, *kn)
                for i, t in enumerate(tl):
                    tk = tp(P[:, i * 128:(i + 1) * 128], sb["QNB"][:, t, h * 128:(h + 1) * 128], IDENT,
                            inc=i == len(tl) - 1)
                o = KT[:, h, :] if keys else QT[:, g * 4 + h, 0:len(tl) * 128]
                k = act(o, P[:, 0:len(tl) * 128], ACT.Copy, [tk] + F2)
                let(b, k)
                if keys:
                    k2_done.append(k)
                else:
                    q_done[g * 4 + h] = k
                for t in tl:
                    qn_free[t] = [tk]
                yield
        g0, g1, g2 = [], [], []
        weave(group_N_gen(f"wkv{l}", 0, tiles4, lo4, hd, g0), conv_split(), 2)
        F3 = fence()
        weave(group_N_gen(f"wq{l}", 0, tlist, hi4, hd, g1), heads(g0, True, 0), 2)
        weave(group_N_gen(f"wq{l}", 1, tlist, lo4, hd, g2), heads(g1, False, 0), 2)
        q_end = heads(g2, False, 1)
        jobs = [(0, h, t) for h in range(8) for t in range(2)]
        if not last:
            jobs += [(1, h, t) for h in range(8) for t in range(2)]

        def attn2(ring):
            AE, AP2, AR = sb["AE"], sb["APT"], sb["AR"]
            drain_gen = q_end
            for _ in drain_gen:
                yield
            F4 = fence()
            e_free, p_free = [F4, F4, F4, F4], [F4, F4]
            ed, pd, ob, xd2 = {}, {}, {}, {}
            n = len(jobs)

            def sc(j):
                s, h, t = jobs[j]
                nk = 512 if s == 0 else 256
                k0 = 0 if s == 0 else 256
                b, P, fr = ring.get()
                c = s * 256 + t * 128
                tk = mm(P[:, 0:nk], QT[:, h, c:c + 128], KT[:, h // 4, k0:k0 + nk], True, True,
                        fr + [q_done[h]] + k2_done, inc=True)
                e, a = j % 4, j % 4
                k = red(AR[:, 0, a:a + 1], P[:, 0:nk], MAX, [tk] + F4, negate=True)
                k = act(AE[:, e, 0:nk], P[:, 0:nk], ACT.Exp, [k] + e_free[e], bias=AR[:, 0, a:a + 1],
                        accum=AR[:, 1, a:a + 1])
                let(b, k)
                xd2[j] = k

            def pb(j):
                s, h, t = jobs[j]
                nk = 512 if s == 0 else 256
                e = a = j % 4
                k = xd2[j]
                k = DV.run(lambda en: en.reciprocal(AR[:, 2, a:a + 1], AR[:, 1, a:a + 1]), [k])
                ed[j] = ts(DV, AE[:, e, 0:nk], AE[:, e, 0:nk], AR[:, 2, a:a + 1], None, MUL, None, [k])

            def tr_(j):
                s, h, t = jobs[j]
                nk = 4 if s == 0 else 2
                b, P, fr = ring.get()
                e, w = j % 4, j % 2
                PE.wait(*fr, ed[j])
                for i in range(nk):
                    tk = tp(P[:, i * 128:(i + 1) * 128], AE[:, e, i * 128:(i + 1) * 128], IDENT, inc=i == nk - 1)
                e_free[e] = [tk]
                k = act(AP2[:, w, 0:nk * 128], P[:, 0:nk * 128], ACT.Copy, [tk] + p_free[w])
                let(b, k)
                pd[j] = k

            def pv_(j):
                s, h, t = jobs[j]
                nk = 4 if s == 0 else 2
                if t == 0:
                    ob[0] = ring.get()
                b, P, fr = ob[0]
                w = j % 2
                PE.wait(*fr, pd[j], *v2_done)
                for i in range(nk):
                    kt = i if s == 0 else 2 + i
                    tk = mm(P[:, t * 128:(t + 1) * 128], VV[:, kt, (h // 4) * 128:(h // 4 + 1) * 128],
                            AP2[:, w, i * 128:(i + 1) * 128], i == 0, i == nk - 1, inc=i == nk - 1)
                p_free[w] = [tk]
                if t == 1:
                    k = act(QT[:, h, s * 256:(s + 1) * 256], P[:, 0:256], ACT.Copy, [tk])
                    let(b, k)
                    o_done.append(k)
            for j in range(n + 4):
                if j < n:
                    sc(j)
                if 0 <= j - 1 < n:
                    pb(j - 1)
                if 0 <= j - 2 < n:
                    tr_(j - 2)
                if 0 <= j - 3 < n:
                    pv_(j - 3)
                yield
        o_done = []

        S = sb["S"]
        bgh = sb["BG"]
        F4 = fence()
        t_bg = ts(DV, bgh[:, 0:24], par("b_gate", l * 24, 24), 0.5, None, MUL, None)
        s_done = {}

        def branch_out(bi, ring, ab):
            for ft in range(8):
                hi, lo, wt = get_w(f"wmg{l}", bi * 8 + ft)
                b, P, fr = ring.get()
                tk = group_T(P, 0, hi, lo, 0, NT, fr + wt, hdone=hd)
                put_w(tk)
                g = sb["GT"][:, ft % 2, 0:NT]
                kg = act(g, P[:, 0:NT], ACT.Tanh, [tk, t_bg, DV.last(), PO.last()] + F4, scale=0.5, bias=bgh[:, bi * 8 + ft:bi * 8 + ft + 1])
                let(b, kg)
                yield
                hi, lo, wt = get_w(f"wbr{l}", bi * 8 + ft)
                b, P, fr = ring.get()
                tk = group_T(P, 0, hi, lo, 0, NT, fr + wt, ABH, ABL, ab)
                put_w(tk)
                if bi == 0:
                    k = stt(S[:, ft, 0:NT], g, 1.0, P[:, 0:NT], ADD, MUL, [tk, kg] + F4)
                else:
                    k = stt(g, g, 1.0, P[:, 0:NT], ADD, MUL, [tk, kg])
                let(b, k)
                if bi:
                    k = tt(PO, S[:, ft, 0:NT], S[:, ft, 0:NT], g, ADD, [k, s_done[ft]])
                s_done[ft] = k
                yield
        mark(f"b2.{l} outA|attn")
        side = attn2(hi4)
        next(side), next(side)
        weave(branch_out(0, lo4, ab), side, 2.6)

        def z_stage(name, value, ring):
            r = {}
            for ft in range(8):
                hi, lo, wt = get_w(name, ft)
                b, P, fr = ring.get()
                tk = group_T(P, 0, hi, lo, 0, NT, fr + wt, hdone=hd)
                put_w(tk)
                i = ft % 2
                z = sb["ZB"][:, i, 0:NT]
                kt_ = act(z, P[:, 0:NT], ACT.Tanh, [tk, DV.last(), PO.last()], scale=0.5)
                kz = stt(z, z, 1.0, P[:, 0:NT], ADD, MUL, [kt_])
                let(b, kz)
                kv = value(ft, z, kz)
                r[ft] = split_ab(ft, z, [kv])
                yield r
        ab = []

        def val_b(ft, z, kz):
            return stt(z, z, 0.5, QT[:, ft, 0:NT], MUL, MUL, [kz] + o_done)

        mark(f"b2.{l} zb")
        for ab in z_stage(f"wzb{l}", val_b, lo4):
            pass
        mark(f"b2.{l} outB")
        drain(branch_out(1, all8, ab))

        def val_c(ft, z, kz):
            b, P, fr = hi4.get()
            PE.wait(*fr, *og_done)
            nt = NT // 128
            for t in range(nt):
                tk = tp(P[:, t * 128:(t + 1) * 128], GV[:, t, ft * 128:(ft + 1) * 128], IDENT, inc=t == nt - 1)
            k = ts(DV, z, z, 0.5, None, MUL, None, [kz])
            k = stt(z, P[:, 0:NT], par("glag", l * 2 + ft % 2), z, MUL, MUL, [tk, k])
            let(b, k)
            return k
        mark(f"b2.{l} zc")
        for ab in z_stage(f"wzc{l}", val_c, lo4):
            pass
        mark(f"b2.{l} gb")
        F5 = fence()
        gb = []

        def gate_rows(ring):
            ks = [tt(DV, sb["GC"][:, s, :], MT[:, l, 16:24, s], par("g_post", l * 8, 8), MUL, F5 + mod_done[l])
                  for s in range(ns)]
            yield
            dg_free = [[], []]
            for s in range(ns):
                for hf in range(2):
                    b, P, fr = ring.get()
                    for j in range(4):
                        kd = ts(DV, sb["DG"][:, j % 2, :], IDENT, sb["GC"][:, s, hf * 4 + j:hf * 4 + j + 1], 16.0,
                                MUL, MUL, [ks[s]] + dg_free[j % 2])
                        tk = mm(P[:, j * 128:(j + 1) * 128], TRI_ONES, sb["DG"][:, j % 2, :], True, True,
                                fr + [kd], inc=True)
                        dg_free[j % 2] = [tk]
                    k = act(sb["GB"][:, s, hf * 512:(hf + 1) * 512], P[:, :], ACT.Copy, [tk] + F5)
                    let(b, k)
                    gb.append(k)
                    yield
        TRI_ONES = sb["TRI"][:, 128:256]
        weave(branch_out(2, lo4, ab), gate_rows(hi4), 1)
        F6 = fence()
        xr = rdma.start(PO, sb["AFX"][:, 0:NT // 128, :],
                        A["xscr"][0, 0:NT, :].rearrange("(t p) d -> p t d", p=128), F6 + sp_done)
        mark(f"b2.{l} wo")
        sd = {}
        tpe = PE.last()
        for kt in range(8):
            a = act(ABH[:, kt, 0:NT], S[:, kt, 0:NT], ACT.Copy, [s_done[kt], tpe], scale=0.5)
            d = stt(ABL[:, kt, 0:NT], S[:, kt, 0:NT], 0.5, ABH[:, kt, 0:NT].bitcast(F32), MUL, SUB, [a])
            sd[kt] = [a, d]
        gs = sb["GSS"]
        nt = len(tlist)
        x_done = []
        first = {}
        for g in range(2):
            res, at = [], 0
            for _ in group_N_gen(f"wo2{l}", g, tlist, (lo4, hi4)[g] if nt == 4 else all8, sd, res, ABH, ABL, by_tile=g == 1):
                while at < len(res):
                    i = at
                    b, P, tk = res[i]
                    at += 1
                    k = act(sb["ZB"][:, g, :], P[:, :], ACT.Square, [tk, AC.last()] + F6,
                            accum=gs[:, g, i:i + 1])
                    k2 = copy(DV, sb["XS"][:, i, g * 512:(g + 1) * 512], P[:, :], [k] + F6)
                    let(b, k2)
                    if g == 0:
                        first[i] = [k, k2]
                        continue
                    xs = sb["XS"][:, i, :]
                    c = tt(DV, sb["SSO"][:, 0, i:i + 1], gs[:, 0, i:i + 1], gs[:, 1, i:i + 1], ADD, [k, k2] + first[i])
                    c = rsqrt(sb["SSO"][:, 1, i:i + 1], sb["SSO"][:, 0, i:i + 1], 1.0 / 1024, 1, [c])
                    c = stt(xs, xs, sb["SSO"][:, 1, i:i + 1], sb["GB"][:, i // 2, :], MUL, MUL, [c] + gb)
                    c = tt(DV, xs, xs, sb["AFX"][:, i, :], ADD, [c, xr])
                    x_done.append([c])
        allx = [x for v in x_done for x in v]
        if not last:
            sp_done = []
            for s in range(2):
                sp_done.append(spill[s].start(PO, A["xscr"][0, s * 256:(s + 1) * 256, :].rearrange("(t p) d -> p t d", p=128),
                                              sb["XS"][:, 2 * s:2 * s + 2, :], allx + [xr]))
        else:
            for t in range(2):
                t_out = odma.start(SP, out[0, t * 128:(t + 1) * 128, :], sb["XS"][:, t, :], x_done[t])
            SP.wait(t_out)
    SP.wait(*sp_done)
    mark("end")
    return used, {"pe": PE, "act": AC, "dve": DV, "pool": PO, "sp": SP}


def build(nc, args, out):
    base = 16512

    class Map:

        def __init__(self):
            self.t = {}

        def put(self, name, off, shape, dt=F32):
            n = int(np.prod(shape[1:])) * (1 if dt == U8 else 4)
            h = nc.alloc_sbuf_tensor_at(name, shape, dt, offset=base + off)
            self.t[name] = h
            return -(-(off + n) // 32) * 32
    m = Map()
    o = m.put("RAW", 0, [128, 5, 1024])
    o = m.put("SPH", o, [128, 4, 1024], F32R)
    o = m.put("SPL", o, [128, 4, 1024], F32R)
    o = m.put("HTH", o, [128, 8, 512], F32R)
    o = m.put("HTL", o, [128, 8, 512], F32R)
    D = o
    o = m.put("IDENT", D, [128, 128])
    o = m.put("PAR", o, [128, NPAR])
    o = m.put("TRI", o, [128, 384])
    o = m.put("MASK", o, [128, 14 * 128], U8)
    o = m.put("MODT", o, [128, 2, 24, 2])
    o = m.put("GP", o, [128, 2, 8, 2])
    o = m.put("CS", o, [128, 2, 16])
    o = m.put("RS", o, [128, 3, 32])
    o = m.put("SS", o, [128, 8])
    o = m.put("GSS", o, [128, 2, 8])
    o = m.put("SSO", o, [128, 2, 4])
    o = m.put("AR", o, [128, 3, 4])
    o = m.put("ONE", o, [128, 1])
    o = m.put("BG", o, [128, 24])
    o = m.put("GC", o, [128, 2, 8])
    o = m.put("ROPE", o, [128, 2, 2, 2, 128])
    o = m.put("GN", o, [128, 2, 128])
    C = o
    q = m.put("XS", C, [128, 4, 1024])
    m.put("QT", C, [128, 8, 512])
    m.put("LA", C, [128, 4, 512])
    m.put("E4", C + 8192, [128, 4, 512])
    m.put("EB", C + 8192, [128, 2, 4, 256])
    m.put("KE", C + 8192, [128, 4, 4, 128])
    m.put("KT", q, [128, 2, 512])
    m.put("VV", q + 4096, [128, 4, 256])
    m.put("BC", q, [128, 2, 4, 256])
    g = q + 8192
    m.put("GQ", g, [128, 4, 512])
    m.put("GK", g + 8192, [128, 4, 512])
    m.put("S", g, [128, 8, 512])
    v = m.put("GV", g + 16384, [128, 4, 1024])
    m.put("GB", g + 16384, [128, 2, 1024])
    m.put("DG", g + 16384 + 8192, [128, 2, 128])
    a = m.put("AF", v, [128, 8, 512])
    m.put("AFX", v, [128, 4, 1024])
    w = m.put("AE", v, [128, 4, 512])
    w = m.put("APT", w, [128, 2, 512])
    m.put("GT", v + 12288, [128, 2, 512])
    Z = a
    m.put("XN2", Z, [128, 4, 1024])
    m.put("HV", Z + 16384, [128, 2, 512])
    m.put("DG2", Z + 20480, [128, 4, 128])
    z = m.put("ATT", Z, [128, 8, 128])
    z = m.put("ATX", z, [128, 8, 128])
    z = m.put("ST", z, [128, 2, 4, 256])
    z = m.put("RT", z, [33, 512])
    z = m.put("SQ2", z, [128, 256])
    z = m.put("WA", z, [128, 2, 3, 512])
    zmax = z
    zw = m.put("WDEC", z, [33, 1024])
    m.put("MB2", zw, [128, 4, 256])
    m.put("MB0", C, [128, 4, 256])
    m.put("MB1", C + 4096, [128, 4, 256])
    m.put("ABH", Z, [128, 8, 512], F32R)
    e = m.put("ABL", Z + 16384, [128, 8, 512], F32R)
    e = m.put("ZB", e, [128, 2, 512])
    m.t["end2"] = max(e, zw + 4096)
    qq = m.put("QNB", v, [128, 4, 512])
    m.put("QT2", v + 8192, [128, 512])
    m.put("SQ3", v + 10240, [128, 512])
    p = m.put("YN", C + 16384, [128, 2, 1024])
    p = m.put("QKN", p, [128, 2, 2, 512])
    p = m.put("VN", p, [128, 2, 1024])
    qkt_at = p
    p = m.put("QKT", p, [128, 16, 256])
    p = m.put("BIAS", p, [128, 12, 384])
    m.put("MASKF", p, [128, 14 * 128])
    p = m.put("E3", p, [128, 4, 384])
    p = m.put("PT3", p, [128, 2, 384])
    p = m.put("XN1", p, [128, 2, 1024])
    p = m.put("DG1", p, [128, 2, 128])
    p = m.put("SQ", p, [128, 2, 512])
    p = m.put("AROW", p, [2, 512])
    p = m.put("QS", p, [128, 2, 16])
    p = m.put("RR", p, [128, 4, 32])
    p = m.put("SM", p, [128, 16])
    p = m.put("LT", p, [128, 64])
    p = m.put("LAMR", p, [128, 512])
    m.put("FT", m.put("FC", qkt_at, [128, 2, 2, 256]), [128, 2, 256])
    p = m.put("AH", p, [128, 3, 256], F32R)
    p = m.put("AL", p, [128, 3, 256], F32R)
    x1 = m.put("OH", C + 16384, [32, 384])
    x1 = m.put("RB", x1, [32, 12])
    x1 = m.put("MROW", x1, [12, 384])
    x1 = m.put("RROW", x1, [12, 384])
    top = max(p, m.t.pop("end2"))
    print("SBUF top", base + top, "of", nc.sbuf_usable_end)
    print("tops", base + p, base + max(e, zw))
    assert base + top <= nc.sbuf_usable_end
    sb = m.t

    names = ["pe", "act", "dve", "pool", "sp"] + [f"raw{i}" for i in range(5)] + \
        ["cst", "cst2", "bias",  "xs", "sp0", "sp1", "gd", "td", "wd", "rdl", "out"]
    sems = {n: nc.alloc_semaphore("s_" + n) for n in names}
    banks = [nc.alloc_psum_tensor(f"pb{i}", [128, 512], F32) for i in range(8)]
    order, _ = program(nc, None, args, sems, sb, banks, out)
    _, E = program(nc, order, args, sems, sb, banks, out)
    print({k: len(e.todo) for k, e in E.items()})

    with nc.Block() as block:
        @block.sync
        def _(eng):
            for f in E["sp"].todo:
                f(eng)

        @block.scalar
        def _(eng):
            for f in E["act"].todo:
                f(eng)

        @block.vector
        def _(eng):
            for f in E["dve"].todo:
                f(eng)

        @block.gpsimd
        def _(eng):
            for f in E["pool"].todo:
                f(eng)

        @block.tensor
        def _(eng):
            for f in E["pe"].todo:
                f(eng)


def shape_constants():
    ident = np.eye(128, dtype=np.float32)
    s, t = np.arange(128)[:, None], np.arange(128)[None, :]
    tri = np.concatenate([(s <= t), np.ones((128, 128)), (s >= t)], axis=1).astype(np.float32) / np.float32(16)
    masks = []
    for d in range(2):
        for h in LEVELS:
            a, b = (s, t) if d == 0 else (t, s)
            masks.append((a // (2 * h) == b // (2 * h)) & (a % (2 * h) < h) & (b % (2 * h) >= h))
    mask = np.concatenate(masks, axis=1).astype(np.float32)
    bucket = np.searchsorted(np.array(BUCKET_STARTS), np.arange(256), side="right") - 1
    onehot = np.zeros((32, 384), np.float32)
    for i in range(256):
        onehot[bucket[255 - i], i] = 1.0
    maskrow = np.zeros((12, 384), np.float32)
    maskrow[:, 256:] = -1e30
    pos = np.arange(256)
    fr = (10000.0 ** (-np.arange(32, dtype=np.float32) * 2.0 / 64)).astype(np.float32)
    ang = np.stack([(pos // 64).astype(np.float32)[:, None] * fr, (pos % 64).astype(np.float32)[:, None] * fr], 1)
    c, sn = np.cos(ang), np.sin(ang)
    Ct = np.stack([c, c], axis=2).reshape(256, 128)
    St = np.stack([-sn, sn], axis=2).reshape(256, 128)
    rope = np.stack([Ct, St]).reshape(2, 2, 128, 128).transpose(2, 0, 1, 3).astype(np.float32)
    return dict(ident=ident, tri=tri, mask=mask, onehot=onehot, maskrow=maskrow, rope=np.ascontiguousarray(rope))


def lay_out(inp):
    i = {k: np.asarray(v) for k, v in inp.items()}
    d = shape_constants()

    def T(w):
        return np.ascontiguousarray(w.reshape(8, 128, -1, 128).transpose(2, 1, 0, 3)).reshape(-1, 128, 1024)

    def N(w):
        k, c = w.shape
        return np.ascontiguousarray(w.reshape(k // 256, 2, 128, c // 512, 512).transpose(3, 0, 2, 1, 4)).reshape(-1, 128, 1024)

    def cols(a):
        return a.reshape(-1, 128).T
    for l in range(2):
        d[f"w_in{l}"] = N(i["w_in"][l])
        d[f"w_out{l}"] = N(i["w_out"][l])
        d[f"w_up{l}"] = T(i["w_up"][l])
        d[f"w_down{l}"] = i["w_down"][l].reshape(FF_TILES, 128, 1024)
        w = i["w_in_2"][l]
        d[f"wa{l}"] = T(w[:, 0:4096])
        d[f"wq{l}"] = N(w[:, 4096:5120])
        d[f"wkv{l}"] = N(w[:, 5120:5632])
        d[f"wzb{l}"] = T(w[:, 5632:6656])
        d[f"wgq{l}"] = T(w[:, 6656:7168])
        d[f"wgk{l}"] = T(w[:, 7168:7680])
        d[f"wgv{l}"] = N(w[:, 7680:8704])
        d[f"wr{l}"] = np.ascontiguousarray(w[:, 8704:8736].reshape(8, 128, 32).transpose(1, 0, 2)).reshape(1, 128, 256)
        d[f"wzc{l}"] = T(w[:, 8736:9760])
        d[f"wmg{l}"] = T(w[:, 9760:12832])
        d[f"wbr{l}"] = np.concatenate([T(i[n][l]) for n in ("w_br_conv_2", "w_br_attn_2", "w_br_gla_2")])
        d[f"wo2{l}"] = N(i["w_out_2"][l])
    d["w_ada"] = np.concatenate([N(i["w_ada_2"][l]) for l in range(2)])
    wdec = np.zeros((2, 33, 1024), np.float32)
    wdec[:, 0:16, 0:512] = i["w_decay_fwd_2"]
    wdec[:, 16:32, 512:1024] = i["w_decay_bwd_2"]
    wdec[:, 32, 0:512] = i["b_decay_fwd_2"]
    wdec[:, 32, 512:1024] = i["b_decay_bwd_2"]
    d["wdec"] = wdec
    qk = i["qk_norm_g"]
    d["par"] = np.ascontiguousarray(np.concatenate([
        cols(i["ln_attn_g"]), cols(i["ln_ffn_g"]), cols(np.concatenate([qk, qk], axis=-1)), cols(i["diff_subln_g"]),
        cols(i["conv_w"]), cols(i["conv_b"]),
        np.stack([i["c_2"][0].reshape(8, 128), i["c_ctx_2"].reshape(8, 128)], axis=1).reshape(16, 128).T,
        cols(i["b_ada_2"]), cols(i["g_pre_2"]), cols(i["g_post_2"]), cols(i["conv_w_2"]), cols(i["gla_norm_g_2"]),
        cols(i["b_gate_2"])], axis=1))
    d["lamr"] = np.ascontiguousarray(np.broadcast_to(i["diff_lambda"].reshape(1, 512), (128, 512)))
    d["qkn"] = np.ascontiguousarray(np.stack([i["q_norm_g_2"], i["k_norm_g_2"]], axis=1).reshape(4, 128))
    d["rel_bias"] = i["rel_bias"]
    d["x"] = i["x"]
    d["ctx"] = i["ctx_2"]
    return d


def kernel(**inputs):
    import concourse.bacc as bacc
    from concourse.bass_utils import run_bass_kernel_spmd

    nc = bacc.Bacc("TRN2", target_bir_lowering=False, num_devices=1)
    arrays, args = {}, {}
    for name, a in lay_out(inputs).items():
        a = np.ascontiguousarray(a)
        arrays["in_" + name] = a
        args[name] = nc.dram_tensor("in_" + name, a.shape, mybir.dt.from_np(a.dtype), kind="ExternalInput").ap()
    args["rscr"] = nc.dram_tensor("rscr", (12, 128, 384), F32, kind="Internal").ap()
    args["xscr"] = nc.dram_tensor("xscr", (1, 512, 1024), F32, kind="Internal").ap()
    out = nc.dram_tensor("out0", (1, 256, 1024), F32, kind="ExternalOutput").ap()
    build(nc, args, out)
    r = run_bass_kernel_spmd(nc, [arrays], core_ids=[0])
    return r.results[0]["out0"]
```

```python
import concourse.bass as bass
from concourse import mybir
import math
import numpy as np

F32 = mybir.dt.float32
F32R = mybir.dt.float32r
U8 = mybir.dt.uint8
I32 = mybir.dt.int32
ALU = mybir.AluOpType
ACT = mybir.ActivationFunctionType
AX = mybir.AxisListType
ADD, SUB, MUL, MAX, MIN = ALU.add, ALU.subtract, ALU.mult, ALU.max, ALU.min

EPS = 1e-6
BUCKET_STARTS = list(range(17)) + [21, 27, 35, 46, 59, 77, 99, 128, 166, 216]
FF_TILES = 22
PCOLS = {}
_at = 0
for _name, _n in (("ln_attn", 16), ("ln_ffn", 16), ("qkg", 8), ("subg", 2), ("cw", 2 * 3 * 44), ("cb", 88),
                  ("c", 16), ("b_ada", 48), ("g_pre", 16), ("g_post", 16), ("cw2", 48), ("glag", 4),
                  ("b_gate", 48)):
    PCOLS[_name] = _at
    _at += _n
NPAR = _at
LEVELS = (64, 32, 16, 8, 4, 2, 1)
RA = [2.0, 1.8]
IC, PC = 3.5, (6, 10)
BO = [(4, 4, 4), (6, 4, 5)]
RB = [(2, 2, 2.8, 4), (1.4, 1, 1.2, 2.6)]
RQ = ((.8, .8, 2), (.8, 1, 3))
GA = [(2, 5, 2, 1, 2), (1, 3, 1, 0, 0)]
SP_ = ((0, 0, 1), (1, 1, 1))
PF = 2
LT, LV = 2, 3


class Engine:

    def __init__(self, name, sem):
        self.name, self.sem, self.count, self.todo, self.seen = name, sem, 0, [], {}

    def wait(self, *tokens):
        for t in tokens:
            if t is None:
                continue
            sem, value = t
            key = id(sem)
            if self.seen.get(key, 0) < value:
                self.seen[key] = value
                self.todo.append(lambda e, s=sem, v=value: e.wait_ge(s, v))

    def run(self, fn, after=(), inc=True):
        self.wait(*after)
        if inc:
            self.count += 1
            self.todo.append(lambda e, f=fn, s=self.sem: f(e).then_inc(s, 1))
            return (self.sem, self.count)
        self.todo.append(fn)
        return None

    def last(self):
        return (self.sem, self.count) if self.count else None


class Dma:

    def __init__(self, sem):
        self.sem, self.count = sem, 0

    def start(self, eng, out, in_, after=()):
        eng.wait(*after)
        self.count += 16
        eng.todo.append(lambda e, o=out, i=in_, s=self.sem: e.dma_start(o, i).then_inc(s, 16))
        return (self.sem, self.count)


def V(ap, *dims, off=0):
    return bass.AP(ap.tensor, ap.offset + off, [list(ap.ap[0])] + [list(d) for d in dims])


def program(nc, order, A, sems, sb, banks, out):
    PE, AC, DV, PO, SP = (Engine(n, sems[n]) for n in ("pe", "act", "dve", "pool", "sp"))
    used = []

    def act(o, i, func, after=(), scale=1.0, bias=None, accum=None):
        kw = {}
        if bias is not None:
            kw["bias"] = bias
        if accum is not None:
            kw["accum_out"] = accum
        return AC.run(lambda e: e.activation(o, i, func, scale=scale, **kw), after)

    def tt(E, o, a, b, op, after=()):
        return E.run(lambda e: e.tensor_tensor(o, a, b, op), after)

    def ts(E, o, a, s1, s2, op0, op1, after=()):
        if op1 is None:
            return E.run(lambda e: e.tensor_scalar(o, a, s1, None, op0), after)
        return E.run(lambda e: e.tensor_scalar(o, a, s1, s2, op0, op1), after)

    def stt(o, a, s, b, op0, op1, after=()):
        return DV.run(lambda e: e.scalar_tensor_tensor(out=o, in0=a, scalar=s, in1=b, op0=op0, op1=op1), after)

    def copy(E, o, i, after=()):
        return E.run(lambda e: e.tensor_copy(o, i), after)

    def red(o, i, op, after=(), negate=None):
        return DV.run(lambda e: e.tensor_reduce(out=o, in_=i, axis=AX.X, op=op, negate=negate), after)

    def mm(o, l, r, start, stop, after=(), inc=False):
        return PE.run(lambda e: e.matmul(o, l, r, start=start, stop=stop), after, inc)

    def tp(o, i, ident, after=(), inc=False):
        return PE.run(lambda e: e.transpose(o, i, ident), after, inc)

    def fence():
        return [e.last() for e in (PE, AC, DV, PO)]

    free = [[] for _ in range(8)]

    let_at = [0] * 8

    class Ring:
        def __init__(self, ids):
            self.ids = ids

        def get(self):
            b = min((b for b in self.ids if free[b] is not None), key=lambda b: let_at[b])
            toks, free[b] = free[b], None
            return b, banks[b], toks

    def let(b, *toks):
        free[b] = list(toks)
        let_at[b] = max(let_at) + 1

    NR, NS = 5, 4
    raw_free = [[] for _ in range(NR)]
    spl_free = [[] for _ in range(NS)]
    raw_dma = [Dma(sems[f"raw{i}"]) for i in range(NR)]
    st = {"load": 0, "split": 0, "get": 0, "nsplit": 0}
    held = set()
    split_on = list(SP_[0])
    loaded, ready, done_raw = {}, {}, set()

    def load_upto(n):
        while order is not None and st["load"] <= n and st["load"] < len(order):
            u = st["load"]
            if u >= NR and u - NR not in done_raw:
                return
            name, idx, cols, kind = order[u]
            s = u % NR
            loaded[u] = raw_dma[s].start(SP, sb["RAW"][:, s, 0:cols], A[name][idx, :, 0:cols], raw_free[s])
            st["load"] += 1

    def split_upto(n):
        while order is not None and st["split"] <= n and st["split"] < len(order):
            u = st["split"]
            load_upto(u + NR - 1)
            if u not in loaded:
                return
            name, idx, cols, kind = order[u]
            s = u % NR
            raw = sb["RAW"][:, s, 0:cols]
            if kind == "raw":
                ready[u] = (raw, None, s, None, [loaded[u]])
            else:
                k = st["nsplit"]
                q = k % NS
                if q in held:
                    return
                held.add(q)
                st["nsplit"] += 1
                hi, lo = sb["SPH"][:, q, 0:cols], sb["SPL"][:, q, 0:cols]
                t1 = act(hi, raw, ACT.Copy, [loaded[u]] + spl_free[q])
                eng = PO if split_on[k % len(split_on)] else DV
                t2 = tt(eng, lo, raw, hi.bitcast(F32), SUB, [loaded[u], t1] + spl_free[q])
                raw_free[s] = [t1, t2]
                done_raw.add(u)
                ready[u] = (hi, lo, None, q, [t1, t2])
            st["split"] += 1

    def get_w(name, idx, cols=1024, kind="split"):
        used.append((name, idx, cols, kind))
        u = st["get"]
        st["get"] += 1
        if order is None:
            if kind == "raw":
                return sb["RAW"][:, 0, 0:cols], None, []
            return sb["SPH"][:, 0, 0:cols], sb["SPL"][:, 0, 0:cols], []
        assert order[u] == (name, idx, cols, kind)
        split_upto(u + NS + 1)
        hi, lo, s, q, toks = ready[u]
        return hi, lo, toks

    def put_w(tok, back=0):
        if order is None:
            return
        u = st["get"] - 1 - back
        _, _, s, q, _ = ready.pop(u)
        if s is not None:
            raw_free[s] = [tok]
            done_raw.add(u)
        else:
            spl_free[q] = [tok]
            held.discard(q)

    xdma, cdma = Dma(sems["xs"]), Dma(sems["cst"])
    pdma = Dma(sems["par"])
    pdma.start(AC, sb["PAR"][:, :], A["par"])
    T_par = pdma.start(AC, sb["IDENT"][:, :], A["ident"])
    xdma.start(SP, sb["XS"][:, 0, :], A["x"][0, 0:128, :])
    T_x = xdma.start(SP, sb["XS"][:, 1, :], A["x"][0, 128:256, :])
    for o, i in ((sb["OH"][0:32, 0:384], "onehot"), (sb["RB"][0:32, 0:12], "rel_bias"),
                 (sb["MROW"][0:12, 0:384], "maskrow"), (sb["LAMR"][:, :], "lamr")):
        T_bias_in = cdma.start(PO, o, A[i])
    kdma = Dma(sems["cst2"])
    kdma.start(PO, sb["TRI"][:, :], A["tri"], [T_x])
    kdma.start(PO, sb["MASKF"][:, :], A["mask"])
    T_const = kdma.start(PO, sb["XS"][:, 2:4, :], A["ctx"][0, :, :].rearrange("(t p) d -> p t d", p=128))
    IDENT = sb["IDENT"][:, :]
    t_one = DV.run(lambda e: e.memset(sb["ONE"][:, :], 1.0))

    def par(name, i=0, n=1):
        c = PCOLS[name] + i
        return sb["PAR"][:, c:c + n]

    def rsqrt(dst, ss, inv, n, after=()):
        w = sb["RS"]
        xh, y, t = w[:, 0, 0:n], w[:, 1, 0:n], w[:, 2, 0:n]
        k = ts(DV, xh, ss, inv, EPS, MUL, ADD, after)
        k = ts(DV, t.bitcast(I32), xh.bitcast(I32), 1, None, ALU.logical_shift_right, None, [k])
        k = ts(DV, y.bitcast(I32), t.bitcast(I32), -1.0, float(0x5f3759df), MUL, ADD, [k])
        for i in range(3):
            k = tt(DV, t, y, y, MUL, [k])
            k = stt(t, t, -0.5, xh, MUL, MUL, [k])
            k = stt(dst if i == 2 else y, t, 1.5, y, ADD, MUL, [k])
        return k

    norm_prev = []

    def norm_stats(tiles, junk, DG, after, on_act=0):
        prev = list(norm_prev)
        t0, nt = tiles[0], len(tiles)
        ks = []
        for i, t in enumerate(tiles):
            x, acc = sb["XS"][:, t, :], sb["SS"][:, t:t + 1]
            if i == on_act:
                ks.append(act(junk[:, i, :], x, ACT.Square, list(after[i]) + prev, accum=acc))
            else:
                DV.wait(*after[i], *prev)
                ks.append(DV.run(lambda e, o=junk[:, i, :], x=x, acc=acc: e.scalar_tensor_tensor(
                    out=o, in0=x, scalar=1.0, in1=x, op0=MUL, op1=MUL, accum_out=acc)))
        k = rsqrt(sb["SS"][:, 4 + t0:4 + t0 + nt], sb["SS"][:, t0:t0 + nt], 1.0 / 1024, nt, ks + prev)
        dg = [ts(DV, DG[:, i, :], IDENT, sb["SS"][:, 4 + t:5 + t], None, MUL, None, [k, T_par])
              for i, t in enumerate(tiles)]
        norm_prev[:] = ks + dg
        return dg

    def norm_products(tiles, DG, dg, ring, gain, after, done):
        for kt in range(8):
            b, P, fr = ring.get()
            for i, t in enumerate(tiles):
                tk = mm(P[:, i * 128:(i + 1) * 128], sb["XS"][:, t, kt * 128:(kt + 1) * 128], DG[:, i, :],
                        True, True, fr + [dg[i]] + list(after[i]), inc=i == len(tiles) - 1)
            done[kt] = done.get(kt, []) + gain(kt, b, P, tk)
            yield
        norm_prev.append(tk)

    def norm_T(tiles, junk, DG, ring, gain, after, done, side=(), ahead=0):
        side = iter(side)
        dg = norm_stats(tiles, junk, DG, after)
        for _ in range(ahead):
            next(side, None)
        for _ in norm_products(tiles, DG, dg, ring, gain, after, done):
            next(side, None)
        drain(side)

    def gain_mod(l, s, HV, mode, free_):
        MT, GP = sb["MODT"], sb["GP"]

        def f(kt, b, P, tk):
            w = HV[:, kt % 2, 0:256]
            o = slice(s * 256, s * 256 + 256)
            G, sh = GP[:, l, kt, s:s + 1], MT[:, l, kt, s:s + 1]
            after = [tk] + free_[kt % 2] + mod_done[l]
            if mode == "act":
                k = act(w, P[:, 0:256], ACT.Identity, after, scale=G, bias=sh)
            else:
                k = ts(DV, w, P[:, 0:256], G, sh, MUL, ADD, after)
            let(b, k)
            a = act(HH[:, kt, o], w, ACT.Copy, [k])
            E = PO if mode == "act" or kt % 2 else DV
            d = tt(E, HL[:, kt, o], w, HH[:, kt, o].bitcast(F32), SUB, [a, k])
            free_[kt % 2] = [a, d]
            return [a, d]
        return f

    HH, HL = sb["HTH"], sb["HTL"]

    def group_T(P, col, hi, lo, n0, n1, after, xh=None, xl=None, hdone=None):
        xh, xl = xh or HH, xl or HL
        wh, wl = (a.rearrange("p (k c) -> p k c", k=8) for a in (hi, lo))
        o = P[:, col:col + n1 - n0]
        PE.wait(*after)
        hdone = hdone or {}
        for kt in range(8):
            PE.wait(*hdone.get(kt, ()))
            mm(o, wh[:, kt, :], xh[:, kt, n0:n1], kt == 0, False)
            mm(o, wh[:, kt, :], xl[:, kt, n0:n1], False, False)
            tk = mm(o, wl[:, kt, :], xh[:, kt, n0:n1], False, kt == 7, inc=kt == 7)
        return tk

    def group_T_half(P, n, hi, lo, after, part, hdone):
        wh, wl = (a.rearrange("p (k c) -> p k c", k=8) for a in (hi, lo))
        PE.wait(*after)
        for kt in range(4 * part, 4 * part + 4):
            PE.wait(*hdone[kt])
            mm(P[:, 0:n], wh[:, kt, :], HH[:, kt, 0:n], kt == 0, False)
            mm(P[:, 0:n], wh[:, kt, :], HL[:, kt, 0:n], False, False)
            tk = mm(P[:, 0:n], wl[:, kt, :], HH[:, kt, 0:n], False, kt == 7, inc=kt == 7)
        return tk

    def group_N_gen(name, g, tiles, ring, hdone, res, xh=None, xl=None, by_tile=False):
        xh, xl = xh or HH, xl or HL
        n = len(tiles)
        got = [ring.get() for _ in tiles]

        def part(i, t, u, hi, lo):
            wh, wl = (a.rearrange("p (k c) -> p k c", k=2) for a in (hi, lo))
            P = got[i][1]
            PE.wait(*got[i][2])
            s = slice(t * 128, (t + 1) * 128)
            for j in range(2):
                kt = 2 * u + j
                PE.wait(*hdone.get(kt, ()))
                mm(P[:, :], xh[:, kt, s], wh[:, j, :], kt == 0, False)
                mm(P[:, :], xl[:, kt, s], wh[:, j, :], False, False)
                tk = mm(P[:, :], xh[:, kt, s], wl[:, j, :], False, kt == 7, inc=j == 1)
            return tk
        if by_tile:
            us = []
            for u in range(4):
                us.append(get_w(name, g * 4 + u))
            for i, t in enumerate(tiles):
                for u, (hi, lo, wt) in enumerate(us):
                    PE.wait(*wt)
                    tk = part(i, t, u, hi, lo)
                    if i == n - 1:
                        put_w(tk, 3 - u)
                if i == n - 1:
                    split_on[:] = (1,)
                    split_upto(st["get"] - 1 + PF)
                    split_on[:] = SP_[0]
                res.append((got[i][0], got[i][1], tk))
                yield
            return
        for u in range(4):
            hi, lo, wt = get_w(name, g * 4 + u)
            PE.wait(*wt)
            toks = [part(i, t, u, hi, lo) for i, t in enumerate(tiles)]
            put_w(toks[-1])
            if u == 3:
                res += [(got[i][0], got[i][1], toks[i]) for i in range(n)]
            yield

    def group_N(*a, **k):
        res = []
        drain(group_N_gen(*a, res, **k))
        return res

    def drain(g):
        for _ in g:
            pass

    def weave(main, side, ratio=1, steps=None):
        live = True
        acc = 0.0
        n = 0
        while steps is None or n < steps:
            n += 1
            try:
                next(main)
            except StopIteration:
                break
            acc += ratio
            while live and acc >= 1:
                try:
                    acc -= next(side) or 1
                except StopIteration:
                    live = False
        if live and steps is None:
            drain(side)

    lo4, hi4 = Ring([0, 1, 2, 3]), Ring([4, 5, 6, 7])
    ada_ring = Ring([7])
    arow = sb["AROW1"]
    low7 = Ring([0, 1, 2, 3, 4, 5, 6])
    all8 = Ring(list(range(8)))

    c, cs = par("c", 0, 16), sb["CS"]
    k = act(cs[:, 0, :], c, ACT.Tanh, [T_par], scale=0.5)
    k = stt(cs[:, 1, :], cs[:, 0, :], 1.0, c, ADD, MUL, [k])
    t_cs = ts(DV, cs[:, 1, :], cs[:, 1, :], 0.5, None, MUL, None, [k])
    mod_done = {0: [], 1: []}

    def ada_steps():
        MT = sb["MODT"]
        for l in range(1):
            for g in range(6):
                b, P, fr = ada_ring.get()
                for u in range(4):
                    w, _, wt = get_w("w_ada", l * 24 + g * 4 + u, kind="raw")
                    PE.wait(t_cs, *fr, *wt)
                    for j in range(2):
                        kt = 2 * u + j
                        tk = mm(P[0:2, :], cs[:, 1, kt * 2:kt * 2 + 2], w[:, j * 512:(j + 1) * 512], kt == 0, kt == 7,
                                inc=j == 1)
                    put_w(tk)
                    if u < 3:
                        yield
                k = act(arow[0:2, :], P[0:2, :], ACT.Copy, [tk, PE.last()])
                yield
                for j in range(4):
                    tk = tp(P[:, 2 * j:2 * j + 2], arow[0:2, j * 128:(j + 1) * 128], IDENT[0:2, 0:2], [k],
                            inc=j == 3)
                k = tt(DV, MT[:, l, 4 * g:4 * g + 4, :], P[:, 0:8].rearrange("p (j s) -> p j s", j=4),
                       V(par("b_ada", l * 24 + 4 * g, 4), [1, 4], [0, 2]), ADD, [tk])
                let(b, k)
                if g == 5:
                    k2 = stt(sb["GP"][:, l, :, :], MT[:, l, 8:16, :], 1.0, V(par("g_pre", l * 8, 8), [1, 8], [0, 2]),
                             ADD, MUL, [k])
                    mod_done[l] = [k, k2]
                yield "group"
    ada = ada_steps()
    ada_dma = [Dma(sems[f"ada{i}"]) for i in range(3)]

    def ada_dve(ring):
        MT, ACC = sb["MODT"], sb["ACC"]
        F = fence()
        acc_free, turn = [F, F], None

        def end(g, toks):
            for s in range(2):
                b, P, fr = ring.get()
                PE.wait(*fr, *toks)
                for j in range(4):
                    tk = tp(P[:, j * 128:(j + 1) * 128], ACC[:, g % 2, s, j * 128:(j + 1) * 128], IDENT, inc=j == 3)
                k = red(V(MT[:, 1, 4 * g:4 * g + 1, s], [2, 4]), P[:, :].rearrange("p (a n) -> p a n", a=4), ADD, [tk])
                let(b, k)
            acc_free[g % 2] = [tk]
            return k
        slot_free = [F, F, F]
        loads = {}

        def load(n):
            if n < 24:
                loads[n] = ada_dma[n % 3].start(AC, sb["ARAW"][:, n % 3, :], A["w_ada"][24 + n, :, :], slot_free[n % 3])
        load(0), load(1)
        yield
        for g in range(6):
            last = [None, None]
            for u in range(4):
                n = 4 * g + u
                load(n + 2)
                w, wt = sb["ARAW"][:, n % 3, :], [loads[n]]
                for j in range(2):
                    for s in range(2):
                        kt = 2 * u + j
                        a, wj, m = ACC[:, g % 2, s, :], w[:, j * 512:(j + 1) * 512], cs[:, 1, kt * 2 + s:kt * 2 + s + 1]
                        if kt == 0:
                            last[s] = ts(DV, a, wj, m, None, MUL, None, wt + acc_free[g % 2])
                        else:
                            last[s] = stt(a, wj, m, a, MUL, ADD, wt + [last[s]])
                slot_free[n % 3] = [last[1]]
                if u == 1 and turn:
                    end(*turn)
                yield
            turn = (g, last)
        k = end(*turn)
        k = tt(DV, MT[:, 1, :, :], MT[:, 1, :, :], V(par("b_ada", 24, 24), [1, 24], [0, 2]), ADD, [k])
        k2 = stt(sb["GP"][:, 1, :, :], MT[:, 1, 8:16, :], 1.0, V(par("g_pre", 8, 8), [1, 8], [0, 2]), ADD, MUL, [k])
        mod_done[1] = [k, k2]
        yield

    def fill_ada(groups):
        for _ in range(groups):
            for end in ada:
                yield
                if end:
                    break

    BIAS = sb["BIAS"]

    def bias_strips():
        b, P, fr = hi4.get()
        tk = mm(P[0:12, 0:384], sb["RB"][0:32, 0:12], sb["OH"][0:32, 0:384], True, True, fr + [T_bias_in], inc=True)
        t1 = tt(DV, sb["RROW"][0:12, :], P[0:12, 0:384], sb["MROW"][0:12, 0:384], ADD, [tk, T_bias_in])
        let(b, t1)
        rd = Dma(sems["bias"])
        tr = rd.start(PO, A["rscr"], V(sb["RROW"][0:12, :], [0, 128], [1, 384]), [t1])
        src = A["rscr"]
        for part in range(3):
            o = 128 if part == 0 else (part - 1) * 128
            t_bias = rd.start(PO, BIAS[:, :, part * 128:(part + 1) * 128],
                              bass.AP(src.tensor, src.offset + 127 + o, [[383, 128], [128 * 384, 12], [1, 128]]), [tr])
        return t_bias

    ASC = 128 ** -0.5
    tdma = Dma(sems["td"])

    spill = [Dma(sems["sp0"]), Dma(sems["sp1"])]

    def load_tables(l, after):
        for i in range(2):
            tdma.start(AC, sb["GN"][:, i, :],
                       bass.AP(A["qkn"].tensor, A["qkn"].offset + (l * 2 + i) * 128, [[0, 128], [1, 128]]), after)
            t = tdma.start(AC, sb["ROPE"][:, i, :, :, :], A["rope"])
        return t

    def tables(t_in):
        k = ts(DV, sb["GN"][:, 0, :], sb["GN"][:, 0, :], ASC, None, MUL, None, [t_in])
        t_rope = []
        for i in range(2):
            g = sb["GN"][:, i, :]
            t_rope.append(tt(DV, sb["ROPE"][:, i, 0, :, :], sb["ROPE"][:, i, 0, :, :],
                             V(g, [0, 2], [1, 128]), MUL, [k]))
            for t in range(2):
                for hf in range(2):
                    o = V(sb["ROPE"][:, i, 1, t, hf * 32:hf * 32 + 1], [64, 2], [1, 32])
                    t_rope.append(tt(DV, o, o, V(sb["GN"][:, i, (1 - hf) * 32:(1 - hf) * 32 + 1], [64, 2], [1, 32]),
                                     MUL, [k]))
        return t_rope

    hd2 = {}
    QKT, VN, YN, QKN = sb["QKT"], sb["VN"], sb["YN"], sb["QKN"]
    x_done = [[T_x], [T_x]]
    for l in range(2):
        lam_init = 0.8 - 0.6 * math.exp(-0.3 * l)
        sm = sb["SM"]
        lr = sb["LAMR"]
        k = []
        for j in range(2):
            a0 = (l * 4 + 2 * j) * 64
            k1 = tt(DV, sb["LT"][:, 0:64], lr[:, a0:a0 + 64], lr[:, a0 + 64:a0 + 128], MUL, [T_bias_in, T_par, DV.last()])
            k2 = red(sm[:, j:j + 1], sb["LT"][:, 0:64], ADD, [k1])
            k.append(act(sm[:, 2 + j:3 + j], sm[:, j:j + 1], ACT.Exp, [k2]))
        k1 = tt(DV, sm[:, 4:5], sm[:, 3:4], sm[:, 2:3], SUB, k)
        t_lam = ts(DV, sm[:, 5:6], sm[:, 4:5], -lam_init, None, ADD, None, [k1])
        ts(DV, sm[:, 6:7], par("qkg", l * 4), 0.125, None, MUL, None, [T_par])
        ts(DV, sm[:, 7:8], par("qkg", l * 4 + 2), 0.125, None, MUL, None)
        t_cols = ts(DV, sm[:, 8:9], par("subg", l), 1.0 - lam_init, None, MUL, None)

        def gain1(name):
            def f(kt, b, P, tk):
                g = par(name, l * 8 + kt)
                a = act(HH[:, kt, 0:256], P[:, 0:256], ACT.Copy, [tk], scale=g)
                d = stt(HL[:, kt, 0:256], P[:, 0:256], g, HH[:, kt, 0:256].bitcast(F32), MUL, SUB, [a])
                let(b, d)
                return [a, d]
            return f
        hd = {}
        norm_T((0, 1), sb["XN1"], sb["DG1"], low7, gain1("ln_attn"), x_done, hd,
               fill_ada(GA[l][0]), GA[l][1])
        if l == 0:
            t_bias = bias_strips()
            t_mask = copy(DV, sb["MASK"][:, :], sb["MASKF"][:, :], [T_const])

        qk_done, v_done = {}, {}
        pend = None
        FQ = fence()

        qkn_free = [[], []]

        def qk_finish(sec, kn, ring):
            for half in range(2):
                b, P, fr = ring.get()
                PE.wait(*fr)
                for f in range(2):
                    for t in range(2):
                        ft = half * 2 + f
                        tk = tp(P[:, (f * 2 + t) * 128:(f * 2 + t + 1) * 128],
                                QKN[:, sec % 2, t, ft * 128:(ft + 1) * 128], IDENT, [kn[t]], inc=f == 1 and t == 1)
                base = {0: 0, 1: 4, 3: 8, 4: 12}[sec] + half * 2
                g = {0: sm[:, 6:7], 1: par("qkg", l * 4 + 1), 3: sm[:, 7:8], 4: par("qkg", l * 4 + 3)}[sec]
                o = QKT[:, base:base + 2, :].rearrange("p a b -> p (a b)")
                t = act(o, P[:, :], ACT.Copy, [tk, t_cols] + FQ, scale=g)
                let(b, t)
                qk_done[(sec, half)] = t
            qkn_free[sec % 2] = [tk]
        sq_free = [[], []]

        def qkv(secs, ring):
            pend = None
            for sec in secs:
                got = []
                for _ in group_N_gen(f"w_in{l}", sec, (0, 1), ring, hd, got):
                    yield
                if pend is not None:
                    qk_finish(*pend, ring)
                    pend = None
                if sec in (2, 5):
                    for t, (b, P, tk) in enumerate(got):
                        k = act(VN[:, t, (sec == 5) * 512:(sec == 5) * 512 + 512], P[:, :], ACT.Copy, [tk])
                        let(b, k)
                        v_done[(sec, t)] = k
                    continue
                ks = []
                for t, (b, P, tk) in enumerate(got):
                    k = act(sb["SQ"][:, t, :], P[:, :], ACT.Square, [tk] + sq_free[t] + FQ)
                    ks.append(red(sb["QS"][:, 0, t * 8:t * 8 + 8],
                                  sb["SQ"][:, t, :].rearrange("p (h d) -> p h d", d=64), ADD, [k]))
                    sq_free[t] = [ks[-1]]
                k = rsqrt(sb["QS"][:, 1, 0:16], sb["QS"][:, 0, 0:16], 1.0 / 64, 16, ks)
                kn = []
                for t, (b, P, tk) in enumerate(got):
                    k2 = tt(DV, QKN[:, sec % 2, t, :].rearrange("p (h d) -> p h d", d=64),
                            P[:, :].rearrange("p (h d) -> p h d", d=64),
                            V(sb["QS"][:, 1, t * 8:t * 8 + 1], [1, 8], [0, 64]), MUL, [k] + qkn_free[sec % 2] + FQ)
                    let(b, k2)
                    kn.append(k2)
                pend = (sec, kn)
        side = qkv((0, 1, 2), all8)
        next(side), next(side)
        if l == 1:
            assert mod_done[0]
            ctx_after = [[T_const]] * 2
            dgc = norm_stats((2, 3), sb["XN1"], sb["DG1"], ctx_after)
            hvf = [list(norm_prev), list(norm_prev)]
        drain(side)

        R = sb["RR"]
        E3, PT = sb["E3"], sb["PT3"]
        FA = fence()
        e_done, e_free, pt_free = {}, [FA] * 4, [FA] * 2
        y_done = []
        sc_ring, tp_ring, pv_ring = Ring([4, 5]), Ring([6]), Ring([7])
        pv = {}

        def scores(u):
            s, fam = u % 8, u // 8
            half, ft = s % 2, s // 2
            hb = s // 2 if fam == 0 else 4 + s
            b, P, fr = sc_ring.get()
            p0 = half * 64
            q = QKT[p0:p0 + 64, fam * 8 + ft, :]
            kk = QKT[p0:p0 + 64, fam * 8 + 4 + ft, :]
            PE.wait(*fr, qk_done[(fam * 3, ft // 2)], qk_done[(fam * 3 + 1, ft // 2)])
            mm(P[:, 0:128], q[:, 0:128], kk[:, 0:128], True, True)
            tk = mm(P[:, 128:384], q[:, 128:256], kk[:, 0:256], True, True, inc=True)
            e = u % 4
            LG = E3[:, e, :]
            k = tt(DV, LG, P[:, 0:384], BIAS[:, hb, :], ADD, [tk, t_bias] + e_free[e])
            let(b, k)
            ka = red(R[:, 0, 2 * u:2 * u + 1], LG[:, 0:128], MAX, [k], negate=True)
            kb = red(R[:, 0, 2 * u + 1:2 * u + 2], LG[:, 128:384], MAX, [k], negate=True)
            act(LG[:, 0:128], LG[:, 0:128], ACT.Exp, [ka], bias=R[:, 0, 2 * u:2 * u + 1],
                accum=R[:, 1, 2 * u:2 * u + 1])
            ke = act(LG[:, 128:384], LG[:, 128:384], ACT.Exp, [kb], bias=R[:, 0, 2 * u + 1:2 * u + 2],
                     accum=R[:, 1, 2 * u + 1:2 * u + 2])
            ex_done[u] = ke

        def probs(u):
            s, fam = u % 8, u // 8
            half, ft = s % 2, s // 2
            LG = E3[:, u % 4, :]
            ke = ex_done[u]
            kr = DV.run(lambda e_: e_.reciprocal(R[:, 2, 2 * u:2 * u + 2], R[:, 1, 2 * u:2 * u + 2]), [ke])
            if fam == 0:
                if half == 0:
                    k = ts(DV, LG[:, 0:128], LG[:, 0:128], R[:, 2, 2 * u:2 * u + 1], None, MUL, None, [kr])
                    k = ts(DV, LG[:, 128:384], LG[:, 128:384], R[:, 2, 2 * u + 1:2 * u + 2], None, MUL, None, [k])
                    e_done[u] = k
                else:
                    kl = tt(DV, R[:, 3, 2 * u:2 * u + 2], R[:, 2, 2 * u:2 * u + 2],
                            V(sm[:, 5:6], [0, 2]), MUL, [kr, t_lam])
                    prev = E3[:, (u - 1) % 4, :]
                    k = stt(LG[:, 0:128], LG[:, 0:128], R[:, 3, 2 * u:2 * u + 1], prev[:, 0:128], MUL, ADD,
                            [kl, e_done[u - 1]])
                    k = stt(LG[:, 128:384], LG[:, 128:384], R[:, 3, 2 * u + 1:2 * u + 2], prev[:, 128:384], MUL, ADD,
                            [k])
                    e_free[(u - 1) % 4] = [k]
                    e_done[u] = k
            else:
                e_done[u] = kr

        def trans(u):
            e = u % 4
            b, P, fr = tp_ring.get()
            PE.wait(*fr, e_done[u])
            for j in range(3):
                tk = tp(P[:, j * 128:(j + 1) * 128], E3[:, e, j * 128:(j + 1) * 128], IDENT, inc=j == 2)
            e_free[e] = [tk]
            w = u % 2 if u >= 8 else u // 2 % 2
            k = act(PT[:, w, :], P[:, 0:384], ACT.Copy, [tk] + pt_free[w])
            let(b, k)
            pt_done[u] = k
        pt_done, ex_done = {}, {}
        sqy_free = []

        def values(u):
            w = u % 2 if u >= 8 else u // 2 % 2
            fam = u // 8
            s = u % 8
            if fam == 0:
                h, dv, per = s // 2, 128, 2
                c0 = h * 128
            else:
                h, dv, per = s, 64, 4
                c0 = 512 + h * 64
            i = h % per
            if i == 0:
                pv[fam] = pv_ring.get()
            b, P, fr = pv[fam]
            PE.wait(*fr, pt_done[u], *v_done.values())
            o = P[:, :].rearrange("p (i t d) -> p i t d", i=per, t=2)
            mm(o[:, i, 0, :], PT[:, w, 0:128], VN[:, 0, c0:c0 + dv], True, True)
            mm(o[:, i, 1, :], PT[:, w, 128:256], VN[:, 0, c0:c0 + dv], True, False)
            tk = mm(o[:, i, 1, :], PT[:, w, 256:384], VN[:, 1, c0:c0 + dv], False, True, inc=True)
            pt_free[w] = [tk]
            if i < per - 1:
                return
            cb = c0 - i * dv
            yo = V(YN[:, 0, cb:cb + 1], [dv, per], [1024, 2], [1, dv])
            if fam == 1:
                r0 = 2 * (u - per + 1)
                k = tt(DV, yo, o, V(R[:, 2, r0:r0 + 1], [2, per], [1, 2], [0, dv]), MUL, [tk])
                let(b, k)
                y_done.append(k)
            else:
                k = act(sb["SQY"][:, :], P[:, :], ACT.Square, [tk] + sqy_free)
                k = red(sb["QSY"][:, 0, 0:4], sb["SQY"][:, :].rearrange("p (g d) -> p g d", d=128), ADD, [k])
                sqy_free[:] = [k]
                k = rsqrt(sb["QSY"][:, 1, 0:4], sb["QSY"][:, 0, 0:4], 1.0 / 128, 4, [k])
                k = tt(DV, yo, o, V(sb["QSY"][:, 1, 0:1], [2, per], [1, 2], [0, dv]), MUL, [k])
                let(b, k)
                y_done.append(k)

        def attn1(us):
            tr_ = [u for u in us if u >= 8 or u % 2 == 1]
            for u in range(us[0], us[-1] + 1 + LV):
                if u in us:
                    scores(u)
                if u - 1 in us:
                    probs(u - 1)
                if u - LT in tr_:
                    trans(u - LT)
                if u - LV in tr_:
                    values(u - LV)
                yield
        yd = {}

        def y_T(kts, ring):
            for kt2 in kts:
                b, P, fr = ring.get()
                PE.wait(*fr, *y_done)
                for f in range(2):
                    for t in range(2):
                        kt = kt2 * 2 + f
                        tk = tp(P[:, (f * 2 + t) * 128:(f * 2 + t + 1) * 128], YN[:, t, kt * 128:(kt + 1) * 128],
                                IDENT, inc=f == 1 and t == 1)
                oh = HH[:, kt2 * 2:kt2 * 2 + 2, 0:256]
                ol = HL[:, kt2 * 2:kt2 * 2 + 2, 0:256]
                Pv = P[:, :].rearrange("p (f n) -> p f n", f=2)
                g = sm[:, 8:9] if kt2 < 2 else 1.0
                a = act(oh, Pv, ACT.Copy, [tk, t_cols], scale=g)
                d = stt(ol, Pv, g, oh.bitcast(F32), MUL, SUB, [a])
                let(b, d)
                yd[2 * kt2] = yd[2 * kt2 + 1] = [a, d]
                yield
        split_on[:] = SP_[1]
        weave(qkv((3, 4, 5), lo4), attn1(range(8)), RQ[l][0])
        got0 = []
        wg0 = group_N_gen(f"w_out{l}", 0, (0, 1), Ring([0, 1]), yd, got0)
        ada_ring = Ring([3])
        if l == 0:
            extra = fill_ada(GA[l][2])
        else:
            extra = norm_products((2, 3), sb["DG1"], dgc, Ring([3]), gain_mod(0, 1, sb["XN1"], "dve", hvf),
                                  ctx_after, hd2)

        def beside():
            for _ in range(RQ[l][2]):
                next(extra, None)
                yield
            for _ in y_T((0, 1), Ring([2])):
                yield
            next(wg0)
            yield
            next(wg0)
            yield
            yield from extra
        weave(beside(), attn1(range(8, 16)), RQ[l][1])
        if l == 1:
            norm_prev += [x for v in hvf for x in v]
        ada_ring = Ring([7])
        split_on[:] = SP_[0]
        drain(y_T((2, 3), hi4))
        drain(wg0)
        xd = [[], []]
        for g in range(2):
            got = got0 if g == 0 else group_N(f"w_out{l}", 1, (0, 1), Ring([2, 3]), yd, by_tile=True)
            for t, (b, P, tk) in enumerate(got):
                xs = sb["XS"][:, t, g * 512:(g + 1) * 512]
                k = tt(DV, xs, P[:, :], xs, ADD, [tk])
                let(b, k)
                xd[t].append(k)

        hd = {}
        norm_T((0, 1), sb["XN1"], sb["DG1"], low7, gain1("ln_ffn"), xd, hd, fill_ada(GA[l][3]), GA[l][4])
        up_ring = Ring([0, 1, 2, 3])
        accs = [(i, banks[i], free[i]) for i in (4, 5, 6, 7)]
        for i in (4, 5, 6, 7):
            free[i] = None
        FF = fence()
        f_free = [FF, FF]
        a_free = [[], [], []]
        a_done = {}

        def ff_up(j):
            b, P, fr = up_ring.get()
            for side in range(2):
                hi, lo, wt = get_w(f"w_up{l}", side * FF_TILES + j)
                tk = group_T(P, side * 256, hi, lo, 0, 256, fr + wt, hdone=hd)
                put_w(tk)
            i = j % 2
            C = sb["FC"]
            outs = []
            for side in range(2):
                ft = side * FF_TILES + j
                w = [par("cw", (l * 3 + q) * 44 + ft) for q in range(3)]
                c = C[:, i, side, :]
                u = P[:, side * 256:(side + 1) * 256]
                outs.append(act(c, u, ACT.Identity, [tk] + f_free[i], scale=w[2], bias=par("cb", l * 44 + ft)))
            for side in range(2):
                ft = side * FF_TILES + j
                w = [par("cw", (l * 3 + q) * 44 + ft) for q in range(3)]
                c = C[:, i, side, :]
                u = P[:, side * 256:(side + 1) * 256]
                k = stt(c[:, 1:256], u[:, 0:255], w[1], c[:, 1:256], MUL, ADD, [outs[1]])
                k = stt(c[:, 2:256], u[:, 0:254], w[0], c[:, 2:256], MUL, ADD, [k])
                outs[side] = k
            let(b, k)
            th = sb["FT"][:, i, :]
            kt_ = act(th, C[:, i, 0, :], ACT.Tanh, [outs[0]], scale=0.5)
            k = stt(th, th, 1.0, C[:, i, 0, :], ADD, MUL, [kt_])
            k = stt(th, th, 0.5, C[:, i, 1, :], MUL, MUL, [k, outs[1]])
            s = j % 3
            kh = act(sb["AH"][:, s, :], th, ACT.Copy, [k] + a_free[s])
            kl = tt(PO, sb["AL"][:, s, :], th, sb["AH"][:, s, :].bitcast(F32), SUB, [kh] + a_free[s])
            f_free[i] = [k, kh, kl]
            a_done[j] = [kh, kl]

        def ff_down(j):
            hi, lo, wt = get_w(f"w_down{l}", j)
            s = j % 3
            PE.wait(*wt, *a_done[j])
            for t in range(2):
                for g in range(2):
                    b, P, fr = accs[t * 2 + g]
                    PE.wait(*fr)
                    xh, xl = sb["AH"][:, s, t * 128:(t + 1) * 128], sb["AL"][:, s, t * 128:(t + 1) * 128]
                    wh, wl = hi[:, g * 512:(g + 1) * 512], lo[:, g * 512:(g + 1) * 512]
                    mm(P[:, :], xh, wh, j == 0, False)
                    mm(P[:, :], xl, wh, False, False)
                    tk = mm(P[:, :], xh, wl, False, j == FF_TILES - 1, inc=True)
            put_w(tk)
            a_free[s] = [tk]
            return tk
        for j in range(FF_TILES + 2):
            if j < FF_TILES:
                ff_up(j)
            if j == 3 and l == 0:
                t_tab = load_tables(0, [T_par])
            if j == 6 and l == 0:
                sp_ctx = spill[1].start(AC, A["xscr"][0, 256:512, :].rearrange("(t p) d -> p t d", p=128),
                                        sb["XS"][:, 2:4, :], [T_const])
            if j == 3 and l == 1:
                t_rope = tables(t_tab)
            if j >= 2:
                tk = ff_down(j - 2)
        x_done = [[], []]
        for t in range(2):
            for g in range(2):
                b, P, _ = accs[t * 2 + g]
                xs = sb["XS"][:, t, g * 512:(g + 1) * 512]
                k = tt(DV, xs, P[:, :], xs, ADD, [tk])
                let(b, k)
                x_done[t].append(k)


    def gla_queries(l, n, hd, after):
        for ft in range(4):
            hi, lo, wt = get_w(f"wgq{l}", ft)
            b, P, fr = all8.get()
            tk = group_T(P, 0, hi, lo, 0, n, fr + wt, hdone=hd)
            put_w(tk)
            k = act(sb["GQ"][:, ft, 0:n], P[:, 0:n], ACT.Copy, [tk] + after, scale=ASC)
            let(b, k)
        return k

    x_done += [[T_const], [T_const]]
    wdma, rdma = Dma(sems["wd"]), Dma(sems["rdl"])
    odma = Dma(sems["out"])
    MT, GP = sb["MODT"], sb["GP"]
    for l in range(2):
        last = l == 1
        NT = 256 if last else 512
        streams = (0,) if last else (1, 0)
        if l:
            hd = hd3
            t_rope = t_rope_next
        F0 = [x for v in x_done for x in v] if l else fence()
        t_wd = wdma.start(AC, sb["WDEC"][:, :], A["wdec"][l, :, :], F0)

        if l == 0:
            hd = hd2
            norm_prev += F0
            hvf = [F0, F0]
            norm_T((0, 1), sb["JUNK"], sb["DG2"], low7, gain_mod(0, 0, sb["HV"], "act", hvf), [F0] * 2, hd,
                   ada)
            sp_done = [sp_ctx, spill[0].start(AC, A["xscr"][0, 0:256, :].rearrange("(t p) d -> p t d", p=128),
                                              sb["XS"][:, 0:2, :], x_done[0] + x_done[1])]
        F1 = fence()

        GQ, GK, GV = sb["GQ"], sb["GK"], sb["GV"]
        tiles4 = (0, 1, 2, 3)
        hi, lo, wt = get_w(f"wr{l}", 0, cols=256)
        b, P, fr = all8.get()
        wh, wl = (a.rearrange("p (k c) -> p k c", k=8) for a in (hi, lo))
        PE.wait(*wt, *fr)
        for kt in range(8):
            PE.wait(*hd[kt])
            mm(P[0:32, :], wh[:, kt, :], HH[:, kt, :], kt == 0, False)
            mm(P[0:32, :], wh[:, kt, :], HL[:, kt, :], False, False)
            tk = mm(P[0:32, :], wl[:, kt, :], HH[:, kt, :], False, kt == 7, inc=kt == 7)
        put_w(tk)
        k_rt = act(sb["RT"][0:32, :], P[0:32, :], ACT.Copy, [tk] + F1)
        let(b, k_rt)
        k1s = DV.run(lambda e: e.memset(sb["RT"][32:33, :], 1.0), F1)
        for ft in range(4):
            hi, lo, wt = get_w(f"wgk{l}", ft)
            b, P, fr = all8.get()
            tk = group_T(P, 0, hi, lo, 0, 512, fr + wt, hdone=hd)
            put_w(tk)
            k = act(GK[:, ft, :], P[:, :], ACT.Copy, [tk] + F1)
            let(b, k)
            gk_done = k
        if l == 0:
            gq_done = gla_queries(0, NT, hd, F1)
        for g in range(2):
            for t, (b, P, tk) in enumerate(group_N(f"wgv{l}", g, tiles4, all8, hd)):
                k = act(GV[:, t, g * 512:(g + 1) * 512], P[:, :], ACT.Copy, [tk] + F1)
                let(b, k)
                gv_done = k

        def gla(ring):
            LA, E4, B, TRI = sb["LA"], sb["E4"], sb["BC"], sb["TRI"]
            attT, attX, ST, KE = sb["ATT"], sb["ATX"], sb["ST"], sb["KE"]
            state_done = []
            for s in (1, 0):
                full = s in streams
                F = fence() + sp_done
                got, ks, la = {}, {}, []
                for i in range(5):
                    if i < 4:
                        b, P, fr = ring.get()
                        c = s * 256 + (i // 2) * 128
                        tk = mm(P[:, :], sb["RT"][0:33, c:c + 128], sb["WDEC"][:, (i % 2) * 512:(i % 2 + 1) * 512],
                                True, True, fr + [k_rt, t_wd, k1s], inc=True)
                        got[i] = (b, P, tk)
                    if i >= 1:
                        b, P, tk = got[i - 1]
                        ka = act(E4[:, i - 1, :], P[:, :], ACT.Abs, [tk] + F)
                        kb = ts(DV, LA[:, i - 1, :], P[:, :], 0.0, None, MIN, None, [ka] + F)
                        let(b, kb)
                        ks[i - 1] = (act(E4[:, i - 1, :], E4[:, i - 1, :], ACT.Exp, [ka], scale=-1.0), kb)
                    yield
                for i in range(4):
                    k = act(E4[:, i, :], E4[:, i, :], ACT.Ln, [ks[i][0], t_one], bias=sb["ONE"][:, 0:1])
                    la.append(tt(DV, LA[:, i, :], LA[:, i, :], E4[:, i, :], SUB, [k, ks[i][1]]))
                yield PC[l]
                bd = []
                for i in range(5):
                    if i < 4:
                        d, hp = i // 2, i % 2
                        b, P, fr = ring.get()
                        PE.wait(*fr, *la)
                        for hh in range(2):
                            h = hp * 2 + hh
                            o = hh * 256
                            sl = slice(h * 128, (h + 1) * 128)
                            if d == 0:
                                mm(P[:, o:o + 256], LA[:, 0, sl], TRI[:, 0:256], True, False)
                                tk = mm(P[:, o + 128:o + 256], LA[:, 2, sl], TRI[:, 0:128], False, True, inc=True)
                            else:
                                mm(P[:, o:o + 256], LA[:, 3, sl], TRI[:, 128:384], True, False)
                                tk = mm(P[:, o:o + 128], LA[:, 1, sl], TRI[:, 256:384], False, True, inc=True)
                        got[i] = (b, P, tk)
                    if i >= 1:
                        d, hp = (i - 1) // 2, (i - 1) % 2
                        b, P, tk = got[i - 1]
                        k = act(B[:, d, hp * 2:hp * 2 + 2, :].rearrange("p h n -> p (h n)"), P[:, :], ACT.Copy, [tk] + F)
                        let(b, k)
                        bd.append(k)
                    yield
                q = GQ[:, :, s * 256:(s + 1) * 256]
                kk = GK[:, :, s * 256:(s + 1) * 256]
                sdone = bd + [gk_done, gq_done, gv_done, la[-1]]
                ad = [None, None]
                xd_ = []
                items = []
                if full:
                    items = [("diag", hp) for hp in range(2)] + [("level", h) for h in LEVELS] + [("level", 128)]
                items += [("edge", d) for d in range(2)]
                n = len(items)
                nbuf = 6 if last else 5
                BUF = [sb[f"BUF{i}"][:, :, :] for i in range(nbuf)]
                buf_free = [list(F) for _ in range(nbuf)]
                bufs, c = {}, (nbuf - 16) % nbuf * full
                for j, (kind, _) in enumerate(items):
                    w = {"diag": 0, "level": 2, "edge": 1}[kind]
                    bufs[j] = [(c + i) % nbuf for i in range(w)]
                    c += w
                e_done, m_done, c_done = {}, {}, {}

                def decay(j):
                    kind, h = items[j]
                    if kind == "diag":
                        return
                    after = sdone + [x for i in bufs[j] for x in buf_free[i]]
                    if kind == "edge":
                        E, bv = BUF[bufs[j][0]], B[:, h, :, :]
                        if s == 0:
                            e_done[j] = [act(E, bv, ACT.Exp, after)]
                        else:
                            end = V(bv, [256, 4], [0, 256], off=255 if h == 0 else 0)
                            k1 = tt(DV, E, end, bv, SUB, after)
                            e_done[j] = [act(E, E, ACT.Exp, [k1])]
                        return
                    K, Q = (BUF[i] for i in bufs[j])
                    nb = 1024 // (2 * h)
                    up = lambda a: V(a, [2 * h, nb], [1, h], off=h)
                    dn = lambda a: V(a, [2 * h, nb], [1, h])
                    b0, b1 = B[:, 0, :, :], B[:, 1, :, :]
                    ref0 = V(b0, [2 * h, nb], [0, h], off=h - 1)
                    ref1 = V(b1, [2 * h, nb], [0, h], off=h)
                    tt(DV, dn(K), ref0, dn(b0), SUB, after)
                    k1 = tt(DV, up(K), ref1, up(b1), SUB)
                    tt(DV, up(Q), up(b0), ref0, SUB)
                    k2 = tt(DV, dn(Q), dn(b1), ref1, SUB)
                    e_done[j] = [act(K, K, ACT.Exp, [k1]), act(Q, Q, ACT.Exp, [k2])]

                def scale(j):
                    kind, h = items[j]
                    if kind == "diag":
                        return
                    if kind == "edge":
                        E = BUF[bufs[j][0]]
                        m_done[j] = [tt(DV, E, q if s == 0 else kk, E, MUL, e_done[j] + sdone)]
                        return
                    K, Q = (BUF[i] for i in bufs[j])
                    k1 = tt(DV, K, kk, K, MUL, [e_done[j][0]] + sdone)
                    k2 = tt(PO, Q, q, Q, MUL, [e_done[j][1]] + sdone)
                    m_done[j] = [k1, k2]

                def product(j):
                    kind, h = items[j]
                    if kind == "edge":
                        return
                    r = []
                    for hp in ((h,) if kind == "diag" else range(2)):
                        b, P, fr = ring.get()
                        PE.wait(*fr, *(sdone if kind == "diag" else m_done[j]))
                        for x in range(4):
                            o = P[:, x * 128:(x + 1) * 128]
                            hd_, t = hp * 2 + x // 2, x % 2
                            sl = slice(t * 128, t * 128 + 128)
                            if kind == "diag":
                                l_, r_ = kk[:, hd_, sl], q[:, hd_, sl]
                            elif h < 128:
                                l_, r_ = BUF[bufs[j][0]][:, hd_, sl], BUF[bufs[j][1]][:, hd_, sl]
                            else:
                                ks_, qs_ = slice(hp * 128, hp * 128 + 128), slice((1 - hp) * 128, (2 - hp) * 128)
                                l_, r_ = BUF[bufs[j][0]][:, x, ks_], BUF[bufs[j][1]][:, x, qs_]
                            tk = mm(o, l_, r_, True, True, inc=x == 3)
                        r.append((b, P, tk, hp))
                    for i in bufs[j]:
                        buf_free[i] = [tk]
                    c_done[j] = r

                def keep(j):
                    kind, h = items[j]
                    for b, P, tk, hp in c_done.get(j, ()):
                        P4 = P[:, :].rearrange("p (a n) -> p a n", a=4)
                        o = attT[:, hp * 4:hp * 4 + 4, :]
                        if kind == "diag":
                            k = ad[hp] = stt(o, P4, 2.0, V(sb["IDENT"][:, 0:1], [0, 4], [1, 128]), MUL, MUL, [tk] + F)
                        elif h < 128:
                            mk = V(sb["MASK"][:, LEVELS.index(h) * 128:LEVELS.index(h) * 128 + 1], [0, 4], [1, 128])
                            k = ad[hp] = DV.run(lambda e, o=o, mk=mk, P4=P4: e.copy_predicated(o, mk, P4),
                                                [tk, ad[hp], t_mask])
                        else:
                            k = act(attX[:, hp * 4:hp * 4 + 4, :], P4, ACT.Copy, [tk] + F)
                            xd_.append(k)
                        let(b, k)

                for j in range(n + 3):
                    if j < n and last:
                        decay(j)
                    if 0 <= j - 3 < n:
                        keep(j - 3)
                    if 0 <= j - 2 < n:
                        product(j - 2)
                    if 0 <= j - 1 < n:
                        scale(j - 1)
                    if j < n and not last:
                        decay(j)
                    yield IC
                dm = [(BUF[bufs[n - 2 + d][0]], m_done[n - 2 + d]) for d in range(2)]
                if s == 1:
                    got = {}
                    for i in range(7):
                        if i < 4:
                            d, hp = i // 2, i % 2
                            M, km = dm[d]
                            b, P, fr = ring.get()
                            PE.wait(*fr, *km)
                            for hh in range(2):
                                for t in range(2):
                                    tk = tp(P[:, (hh * 2 + t) * 128:(hh * 2 + t + 1) * 128],
                                            M[:, hp * 2 + hh, t * 128:(t + 1) * 128], IDENT, inc=hh == 1 and t == 1)
                            k = act(KE[:, i, :, :].rearrange("p a n -> p (a n)"), P[:, :], ACT.Copy,
                                    [tk] + dm[0][1] + dm[1][1])
                            let(b, k)
                            got[i] = k
                        if 1 <= i < 5:
                            d, hp = (i - 1) // 2, (i - 1) % 2
                            b, P, fr = ring.get()
                            PE.wait(*fr, got[i - 1])
                            for hh in range(2):
                                h = hp * 2 + hh
                                for t in range(2):
                                    tk = mm(P[:, hh * 256:(hh + 1) * 256], KE[:, i - 1, hh * 2 + t, :],
                                            GV[:, 2 + t, h * 256:(h + 1) * 256], t == 0, t == 1, inc=t == 1)
                            got[10 + i] = (b, P, tk)
                        if 2 <= i < 6:
                            d, hp = (i - 2) // 2, (i - 2) % 2
                            b, P, tk = got[10 + i - 1]
                            k = act(ST[:, d, hp * 2:hp * 2 + 2, :].rearrange("p a n -> p (a n)"), P[:, :],
                                    ACT.Copy, [tk] + F)
                            let(b, k)
                            state_done.append(k)
                        yield
                if not full:
                    continue
                for h in range(5):
                    if h < 4:
                        b, P, fr = ring.get()
                        PE.wait(*fr, *ad, *xd_)
                        if s == 0:
                            PE.wait(*state_done, *dm[0][1], *dm[1][1])
                        vh = [GV[:, s * 2 + t, h * 256:(h + 1) * 256] for t in range(2)]
                        for t in range(2):
                            o = P[:, t * 256:(t + 1) * 256]
                            mm(o, attT[:, h * 2 + t, :], vh[t], True, False)
                            if s == 0:
                                for d in range(2):
                                    mm(o, dm[d][0][:, h, t * 128:(t + 1) * 128], ST[:, d, h, :], False, False)
                            tk = mm(o, attX[:, (1 - t) * 4 + h, :], vh[1 - t], False, True, inc=True)
                        got[h] = (b, P, tk)
                    if h >= 1:
                        b, P, tk = got[h - 1]
                        k = act(V(GV[:, s * 2, (h - 1) * 256:(h - 1) * 256 + 1], [1024, 2], [1, 256]),
                                P[:, :].rearrange("p (t n) -> p t n", t=2), ACT.Copy, [tk])
                        let(b, k)
                    yield
                gs = sb["GSS"]
                F3 = [DV.last(), k]
                for t in range(2):
                    for h in range(4):
                        k = act(sb["SQ2"][:, :], GV[:, s * 2 + t, h * 256:(h + 1) * 256], ACT.Square,
                                F3 + [AC.last()], accum=gs[:, 0, t * 4 + h:t * 4 + h + 1])
                yield
                k = rsqrt(gs[:, 1, 0:8], gs[:, 0, 0:8], 1.0 / 256, 8, [k])
                for t in range(2):
                    v = V(GV[:, s * 2 + t, 0:1], [256, 4], [1, 256])
                    og_done.append(tt(PO, v, v, V(gs[:, 1, t * 4:t * 4 + 1], [1, 4], [0, 256]), MUL, [k]))
                yield
        og_done = []

        AF = sb["AF"]
        fA = fence()
        wk = {"af": [fA, fA]}
        af_done = []
        ns = 1 if last else 2

        def branch_a(ring):
            for ft in range(8):
                i = ft % 2
                c_sb, u_sb, cv = (sb["WA1" if last else "WA"][:, i, w_, 0:NT] for w_ in range(3))
                pb = {}
                for nm in ("c", "x", "b", "z"):
                    hi, lo, wt = get_w(f"wa{l}", {"b": 0, "c": 8, "x": 16, "z": 24}[nm] + ft)
                    b, P, fr = ring.get()
                    group_T_half(P, NT, hi, lo, fr + wt, 0, hd)
                    yield
                    tk = group_T_half(P, NT, hi, lo, (), 1, hd)
                    put_w(tk)
                    pb[nm] = (b, P[:, 0:NT], tk)
                    if nm == "c":
                        kc = act(c_sb, pb[nm][1], ACT.Copy, [tk] + wk["af"][i])
                        let(b, kc)
                    elif nm == "x":
                        ku = tt(DV, u_sb, P[:, 0:NT], c_sb, MUL, [tk, kc] + wk["af"][i])
                        let(b, ku)
                        w = [par("cw2", (l * 3 + q) * 8 + ft) for q in range(3)]
                        k = act(cv, u_sb, ACT.Copy, [ku] + wk["af"][i], scale=w[1])
                        for s in range(ns):
                            o = s * 256
                            k = stt(cv[:, o + 1:o + 256], u_sb[:, o:o + 255], w[0], cv[:, o + 1:o + 256], MUL, ADD, [k])
                            k = stt(cv[:, o:o + 255], u_sb[:, o + 1:o + 256], w[2], cv[:, o:o + 255], MUL, ADD, [k])
                        kcv = k
                    elif nm == "b":
                        kb = stt(cv, P[:, 0:NT], 0.5, cv, MUL, MUL, [tk, kcv])
                        let(b, kb)
                    else:
                        kt_ = act(c_sb, P[:, 0:NT], ACT.Tanh, [tk, ku], scale=0.5)
                        kz = stt(c_sb, c_sb, 1.0, P[:, 0:NT], ADD, MUL, [kt_])
                        let(b, kz)
                        k = tt(DV, AF[:, ft, 0:NT], c_sb, cv, MUL, [kz, kb] + fA)
                        wk["af"][i] = [k]
                        af_done.append(k)
                    yield
        weave(branch_a(lo4), gla(hi4), RA[l])

        F2 = fence()
        ABH, ABL = sb["ABH"], sb["ABL"]

        def split_ab(kt, v, after, n=NT):
            a = act(ABH[:, kt, 0:n], v, ACT.Copy, after)
            d = tt(PO if kt % 2 else DV, ABL[:, kt, 0:n], v, ABH[:, kt, 0:n].bitcast(F32), SUB, [a] + list(after))
            return [a, d]
        ab = {}

        def conv_split():
            for kt in range(8):
                ab[kt] = split_ab(kt, AF[:, kt, 0:NT], F2)
                yield
        QT, KT, VV = sb["QT"], sb["KT"], sb["VV"]
        ro = sb["ROPE"]

        def sum_heads(P, tk, n, j):
            k = act(sb["SQ3"][:, 0:n * 128], P, ACT.Square, [tk] + sq_free + F3)
            k = red(sb["GSS"][:, 0, j * n:j * n + n], sb["SQ3"][:, 0:n * 128].rearrange("p (h d) -> p h d", d=128),
                    ADD, [k])
            sq_free[:] = [k]
            return k

        def norm_heads(P, n, i, t, slot, kr):
            qn, t2 = sb["QNB"][:, slot, 0:n * 128], sb["QT2"]
            k0 = tt(DV, qn.rearrange("p (h d) -> p h d", d=128), P.rearrange("p (h d) -> p h d", d=128),
                    V(sb["GSS"][:, 1, slot * n:slot * n + 1], [1, n], [0, 128]), MUL, [kr] + qn_free[slot] + F3)
            if t >= 2:
                g = sb["GN"][:, i, :]
                k1 = tt(DV, qn.rearrange("p (h d) -> p h d", d=128), qn.rearrange("p (h d) -> p h d", d=128),
                        V(g, [0, n], [1, 128]), MUL, [k0] + t_rope)
                return k0, k1
            ks = []
            for hf in range(2):
                ks.append(tt(DV, V(t2[:, hf * 32:hf * 32 + 1], [128, n], [64, 2], [1, 32]),
                             V(qn, [128, n], [64, 2], [1, 32], off=(1 - hf) * 32),
                             V(ro[:, i, 1, t, hf * 32:hf * 32 + 1], [0, n], [64, 2], [1, 32]), MUL,
                             [k0] + t_rope + F3))
            k1 = tt(DV, qn.rearrange("p (h d) -> p h d", d=128), qn.rearrange("p (h d) -> p h d", d=128),
                    V(ro[:, i, 0, t, 0:1], [0, n], [1, 128]), MUL, ks)
            k1 = tt(DV, qn, qn, t2[:, 0:n * 128], ADD, [k1])
            return k0, k1
        qn_free = [[], [], [], []]
        sq_free = []
        q_done, k2_done, v2_done = {}, [], []
        tlist = (0, 1) if last else (0, 1, 2, 3)

        def heads(got, keys, g):
            tl = tiles4 if keys else tlist
            kn, ks = [], []
            n = 2 if keys else 4
            for t, (b, P, tk) in enumerate(got):
                if keys:
                    tk = act(VV[:, t, :], P[:, 256:512], ACT.Copy, [tk] + F2)
                    v2_done.append(tk)
                ks.append(sum_heads(P[:, 0:n * 128], tk, n, t))
                yield
            kr = rsqrt(sb["GSS"][:, 1, 0:n * len(got)], sb["GSS"][:, 0, 0:n * len(got)], 1.0 / 128, n * len(got), ks)
            for t, (b, P, _) in enumerate(got):
                k0, k1 = norm_heads(P[:, 0:n * 128], n, 1 if keys else 0, t, t, kr)
                let(b, k0)
                kn.append(k1)
                yield
            for h in range(n):
                b, P, fr = lo4.get()
                PE.wait(*fr, *kn)
                for i, t in enumerate(tl):
                    tk = tp(P[:, i * 128:(i + 1) * 128], sb["QNB"][:, t, h * 128:(h + 1) * 128], IDENT,
                            inc=i == len(tl) - 1)
                o = KT[:, h, :] if keys else QT[:, g * 4 + h, 0:len(tl) * 128]
                k = act(o, P[:, 0:len(tl) * 128], ACT.Copy, [tk] + F2)
                let(b, k)
                if keys:
                    k2_done.append(k)
                else:
                    q_done[g * 4 + h] = k
                for t in tl:
                    qn_free[t] = [tk]
                yield
        g0, g1, g2 = [], [], []
        weave(group_N_gen(f"wkv{l}", 0, tiles4, hi4, hd, g0), conv_split(), 2)
        F3 = fence()

        S = sb["S"]
        bgh = sb["BG"]
        t_bg = ts(DV, bgh[:, 0:24], par("b_gate", l * 24, 24), 0.5, None, MUL, None, F3)
        gt_free = [F3, F3]
        s_done = {}

        def branch_out(bi, ring, ab):
            for ft in range(8):
                hi, lo, wt = get_w(f"wmg{l}", bi * 8 + ft)
                b, P, fr = ring.get()
                tk = group_T(P, 0, hi, lo, 0, NT, fr + wt, hdone=hd)
                put_w(tk)
                g = sb["GT"][:, ft % 2, 0:NT]
                kg = act(g, P[:, 0:NT], ACT.Tanh, [tk, t_bg] + gt_free[ft % 2], scale=0.5,
                         bias=bgh[:, bi * 8 + ft:bi * 8 + ft + 1])
                let(b, kg)
                yield
                hi, lo, wt = get_w(f"wbr{l}", bi * 8 + ft)
                b, P, fr = ring.get()
                tk = group_T(P, 0, hi, lo, 0, NT, fr + wt, ABH, ABL, ab)
                put_w(tk)
                if bi == 0:
                    k = stt(S[:, ft, 0:NT], g, 1.0, P[:, 0:NT], ADD, MUL, [tk, kg] + F3)
                else:
                    k = stt(g, g, 1.0, P[:, 0:NT], ADD, MUL, [tk, kg])
                let(b, k)
                if bi:
                    k = tt(PO, S[:, ft, 0:NT], S[:, ft, 0:NT], g, ADD, [k, s_done[ft]])
                gt_free[ft % 2] = [k]
                s_done[ft] = k
                yield
        out_a = branch_out(0, lo4, ab)
        side = heads(g0, True, 0)
        weave(out_a, side, RB[l][0], BO[l][0])
        while any(free[x[0]] is None for x in g0):
            next(side)
        weave(group_N_gen(f"wq{l}", 0, tlist, hi4, hd, g1), side, 1)
        side = heads(g1, False, 0)
        weave(out_a, side, RB[l][1], BO[l][1])
        while any(free[x[0]] is None for x in g1):
            next(side)
        weave(group_N_gen(f"wq{l}", 1, tlist, hi4, hd, g2), side, 1)
        side = heads(g2, False, 1)
        weave(out_a, side, RB[l][2], BO[l][2])
        q_end = side
        jobs = [(0, h, t) for h in range(8) for t in range(2)]
        if not last:
            jobs += [(1, h, t) for h in range(8) for t in range(2)]

        def attn2(ring):
            AE, AP2, AR = sb["AE"], sb["APT"], sb["AR"]
            drain_gen = q_end
            for _ in drain_gen:
                yield
            F4 = fence()
            e_free, p_free = [F4, F4, F4, F4], [F4, F4]
            ed, pd, ob, xd2 = {}, {}, {}, {}
            n = len(jobs)

            def sc(j):
                s, h, t = jobs[j]
                nk = 512 if s == 0 else 256
                k0 = 0 if s == 0 else 256
                b, P, fr = ring.get()
                c = s * 256 + t * 128
                tk = mm(P[:, 0:nk], QT[:, h, c:c + 128], KT[:, h // 4, k0:k0 + nk], True, True,
                        fr + [q_done[h]] + k2_done, inc=True)
                e, a = j % 4, j % 4
                k = red(AR[:, 0, a:a + 1], P[:, 0:nk], MAX, [tk] + F4, negate=True)
                k = act(AE[:, e, 0:nk], P[:, 0:nk], ACT.Exp, [k] + e_free[e], bias=AR[:, 0, a:a + 1],
                        accum=AR[:, 1, a:a + 1])
                let(b, k)
                xd2[j] = k

            def pb(j):
                s, h, t = jobs[j]
                nk = 512 if s == 0 else 256
                e = a = j % 4
                k = xd2[j]
                k = DV.run(lambda en: en.reciprocal(AR[:, 2, a:a + 1], AR[:, 1, a:a + 1]), [k])
                ed[j] = ts(DV, AE[:, e, 0:nk], AE[:, e, 0:nk], AR[:, 2, a:a + 1], None, MUL, None, [k])

            def tr_(j):
                s, h, t = jobs[j]
                nk = 4 if s == 0 else 2
                b, P, fr = ring.get()
                e, w = j % 4, j % 2
                PE.wait(*fr, ed[j])
                for i in range(nk):
                    tk = tp(P[:, i * 128:(i + 1) * 128], AE[:, e, i * 128:(i + 1) * 128], IDENT, inc=i == nk - 1)
                e_free[e] = [tk]
                k = act(AP2[:, w, 0:nk * 128], P[:, 0:nk * 128], ACT.Copy, [tk] + p_free[w])
                let(b, k)
                pd[j] = k

            def pv_(j):
                s, h, t = jobs[j]
                nk = 4 if s == 0 else 2
                if t == 0:
                    ob[0] = ring.get()
                b, P, fr = ob[0]
                w = j % 2
                PE.wait(*fr, pd[j], *v2_done)
                for i in range(nk):
                    kt = i if s == 0 else 2 + i
                    tk = mm(P[:, t * 128:(t + 1) * 128], VV[:, kt, (h // 4) * 128:(h // 4 + 1) * 128],
                            AP2[:, w, i * 128:(i + 1) * 128], i == 0, i == nk - 1, inc=i == nk - 1)
                p_free[w] = [tk]
                if t == 1:
                    k = act(QT[:, h, s * 256:(s + 1) * 256], P[:, 0:256], ACT.Copy, [tk])
                    let(b, k)
                    o_done.append(k)
            for j in range(n + 4):
                if j < n:
                    sc(j)
                if 0 <= j - 1 < n:
                    pb(j - 1)
                if 0 <= j - 2 < n:
                    tr_(j - 2)
                if 0 <= j - 3 < n:
                    pv_(j - 3)
                yield
        o_done = []

        weave(out_a, attn2(hi4), RB[l][3])

        def z_stage(name, value, ring):
            r = {}
            F = fence()
            zb_free = [F, F]
            for ft in range(8):
                hi, lo, wt = get_w(name, ft)
                b, P, fr = ring.get()
                tk = group_T(P, 0, hi, lo, 0, NT, fr + wt, hdone=hd)
                put_w(tk)
                i = ft % 2
                z = sb["ZB"][:, i, 0:NT]
                kt_ = act(z, P[:, 0:NT], ACT.Tanh, [tk] + zb_free[i], scale=0.5)
                kz = stt(z, z, 1.0, P[:, 0:NT], ADD, MUL, [kt_])
                let(b, kz)
                kv = value(ft, z, kz)
                r[ft] = zb_free[i] = split_ab(ft, z, [kv])
                yield r
        ab = []

        def val_b(ft, z, kz):
            return stt(z, z, 0.5, QT[:, ft, 0:NT], MUL, MUL, [kz] + o_done)

        for ab in z_stage(f"wzb{l}", val_b, lo4):
            pass
        if not last:
            t_tab = load_tables(1, fence())
        more = iter(()) if last else ada_dve(hi4)
        weave(branch_out(1, lo4, ab), more, 1, 17)

        def val_c(ft, z, kz):
            b, P, fr = hi4.get()
            PE.wait(*fr, *og_done)
            nt = NT // 128
            for t in range(nt):
                tk = tp(P[:, t * 128:(t + 1) * 128], GV[:, t, ft * 128:(ft + 1) * 128], IDENT, inc=t == nt - 1)
            k = ts(DV, z, z, 0.5, None, MUL, None, [kz])
            k = stt(z, P[:, 0:NT], par("glag", l * 2 + ft % 2), z, MUL, MUL, [tk, k])
            let(b, k)
            return k
        for ab in z_stage(f"wzc{l}", val_c, lo4):
            pass
        if not last:
            t_rope_next = tables(t_tab)
        F5 = fence()
        gb = []

        def gate_rows(ring):
            ks = [tt(DV, sb["GC"][:, s, :], MT[:, l, 16:24, s], par("g_post", l * 8, 8), MUL, F5 + mod_done[l])
                  for s in range(ns)]
            yield
            dg_free = []
            for s in range(ns):
                for hf in range(2):
                    kd = [ts(DV, sb["DG"][:, j, :], IDENT, sb["GC"][:, s, hf * 4 + j:hf * 4 + j + 1], 16.0,
                             MUL, MUL, [ks[s]] + dg_free) for j in range(4)]
                    yield
                    b, P, fr = ring.get()
                    for j in range(4):
                        tk = mm(P[:, j * 128:(j + 1) * 128], TRI_ONES, sb["DG"][:, j, :], True, True,
                                fr + [kd[j]], inc=j == 3)
                    dg_free = [tk]
                    k = act(sb["GB"][:, s, hf * 512:(hf + 1) * 512], P[:, :], ACT.Copy, [tk] + F5)
                    let(b, k)
                    gb.append(k)
                    yield
        def both(a, b):
            while True:
                x, y = next(a, 0), next(b, 0)
                if x == 0 and y == 0:
                    return
                yield
        TRI_ONES = sb["TRI"][:, 128:256]
        weave(branch_out(2, lo4, ab), both(gate_rows(hi4), more), 1)
        F6 = fence()
        xr = rdma.start(PO, sb["AFX"][:, 0:NT // 128, :],
                        A["xscr"][0, 0:NT, :].rearrange("(t p) d -> p t d", p=128), F6 + sp_done)
        sd = {}
        tpe = PE.last()
        for kt in range(8):
            a = act(ABH[:, kt, 0:NT], S[:, kt, 0:NT], ACT.Copy, [s_done[kt], tpe], scale=0.5)
            d = stt(ABL[:, kt, 0:NT], S[:, kt, 0:NT], 0.5, ABH[:, kt, 0:NT].bitcast(F32), MUL, SUB, [a])
            sd[kt] = [a, d]
        gs = sb["GSS"]
        nt = len(tlist)
        x_done = []
        first, dgs = {}, {}
        s_free = F6 + [x for v in sd.values() for x in v]
        norm_prev += s_free
        for g in range(2):
            res, at = [], 0
            for _ in group_N_gen(f"wo2{l}", g, tlist, (lo4, hi4)[g] if nt == 4 else all8, sd, res, ABH, ABL, by_tile=g == 1):
                while at < len(res):
                    i = at
                    b, P, tk = res[i]
                    at += 1
                    k = act(sb["ZB"][:, g, :], P[:, :], ACT.Square, [tk, AC.last()] + F6,
                            accum=gs[:, g, i:i + 1])
                    if g == 0:
                        k2 = copy(DV, sb["XS"][:, i, 0:512], P[:, :], [k] + F6)
                        let(b, k2)
                        first[i] = [k, k2]
                        continue
                    xs = sb["XS"][:, i, :]
                    c = tt(DV, sb["SSO"][:, 0, i:i + 1], gs[:, 0, i:i + 1], gs[:, 1, i:i + 1], ADD, [k] + first[i])
                    c = rsqrt(sb["SSO"][:, 1, i:i + 1], sb["SSO"][:, 0, i:i + 1], 1.0 / 1024, 1, [c])
                    c1 = stt(xs[:, 512:1024], P[:, :], sb["SSO"][:, 1, i:i + 1], sb["GB"][:, i // 2, 512:1024],
                             MUL, MUL, [c] + gb + F6)
                    let(b, c1)
                    c2 = stt(xs[:, 0:512], xs[:, 0:512], sb["SSO"][:, 1, i:i + 1], sb["GB"][:, i // 2, 0:512],
                             MUL, MUL, [c])
                    c = tt(DV, xs, xs, sb["AFX"][:, i, :], ADD, [c1, c2, xr])
                    x_done.append([c])
                    if i % 2 and not last:
                        s_ = i // 2
                        dgs[s_] = norm_stats((i - 1, i), sb["JUNK"], sb["DG2"][:, 2 * s_:2 * s_ + 2, :], x_done[-2:], 1)
        allx = [x for v in x_done for x in v]
        if not last:
            hd3 = {}
            for s in range(2):
                hvf = [list(s_free), list(s_free)]
                drain(norm_products((2 * s, 2 * s + 1), sb["DG2"][:, 2 * s:2 * s + 2, :], dgs[s], all8,
                                    gain_mod(1, s, sb["HV" if s == 0 else "HV1"], ("act", "dve")[s], hvf),
                                    x_done[2 * s:2 * s + 2], hd3))
                if s == 0:
                    gq_done = gla_queries(1, 256, hd3, list(norm_prev))
        if not last:
            sp_done = []
            for s in range(2):
                sp_done.append(spill[s].start(AC, A["xscr"][0, s * 256:(s + 1) * 256, :].rearrange("(t p) d -> p t d", p=128),
                                              sb["XS"][:, 2 * s:2 * s + 2, :], allx + [xr]))
        else:
            for t in range(2):
                t_out = odma.start(SP, out[0, t * 128:(t + 1) * 128, :], sb["XS"][:, t, :], x_done[t])
            SP.wait(t_out)
    SP.wait(*sp_done)
    return used, {"pe": PE, "act": AC, "dve": DV, "pool": PO, "sp": SP}


def build(nc, args, out):
    base = 16512

    class Map:

        def __init__(self):
            self.t = {}

        def put(self, name, off, shape, dt=F32):
            n = int(np.prod(shape[1:])) * (1 if dt == U8 else 4)
            h = nc.alloc_sbuf_tensor_at(name, shape, dt, offset=base + off)
            self.t[name] = h
            return -(-(off + n) // 32) * 32
    m = Map()
    o = m.put("RAW", 0, [128, 5, 1024])
    o = m.put("SPH", o, [128, 4, 1024], F32R)
    o = m.put("SPL", o, [128, 4, 1024], F32R)
    o = m.put("HTH", o, [128, 8, 512], F32R)
    o = m.put("HTL", o, [128, 8, 512], F32R)
    D = o
    o = m.put("IDENT", D, [128, 128])
    o = m.put("PAR", o, [128, NPAR])
    o = m.put("TRI", o, [128, 384])
    o = m.put("MASK", o, [128, 7 * 128], U8)
    o = m.put("MODT", o, [128, 2, 24, 2])
    o = m.put("GP", o, [128, 2, 8, 2])
    o = m.put("CS", o, [128, 2, 16])
    o = m.put("RS", o, [128, 3, 32])
    o = m.put("SS", o, [128, 8])
    o = m.put("GSS", o, [128, 2, 16])
    o = m.put("SSO", o, [128, 2, 4])
    o = m.put("AR", o, [128, 3, 4])
    o = m.put("ONE", o, [128, 1])
    o = m.put("BG", o, [128, 24])
    o = m.put("GC", o, [128, 2, 8])
    o = m.put("ROPE", o, [128, 2, 2, 2, 128])
    o = m.put("GN", o, [128, 2, 128])
    C = o
    q = m.put("XS", C, [128, 4, 1024])
    m.put("QT", C, [128, 8, 512])
    m.put("ARAW", C, [128, 3, 1024])
    m.put("LA", C, [128, 4, 512])
    m.put("E4", C + 8192, [128, 4, 512])
    m.put("KE", C + 8192, [128, 4, 4, 128])
    m.put("KT", q, [128, 2, 512])
    m.put("ACC", q, [128, 2, 2, 512])
    m.put("VV", q + 4096, [128, 4, 256])
    m.put("BC", q, [128, 2, 4, 256])
    g = q + 8192
    m.put("GQ", g, [128, 4, 512])
    m.put("GK", g + 8192, [128, 4, 512])
    m.put("S", g, [128, 8, 512])
    v = m.put("GV", g + 16384, [128, 4, 1024])
    m.put("GB", g + 16384, [128, 2, 1024])
    m.put("DG", g + 16384 + 8192, [128, 4, 128])
    a = m.put("AF", v, [128, 8, 512])
    m.put("AFX", v, [128, 4, 1024])
    w = m.put("AE", v, [128, 4, 512])
    w = m.put("APT", w, [128, 2, 512])
    m.put("GT", v + 12288, [128, 2, 512])
    Z = a
    n = m.put("JUNK", g, [128, 2, 1024])
    n = m.put("HV", n, [128, 2, 256])
    n = m.put("HV1", n, [128, 2, 256])
    m.put("DG2", n, [128, 4, 128])
    z = m.put("ATT", Z, [128, 8, 128])
    z = m.put("ATX", z, [128, 8, 128])
    z = m.put("ST", z, [128, 2, 4, 256])
    z = m.put("RT", z, [33, 512])
    z = m.put("SQ2", z, [128, 256])
    m.put("BUF5", m.put("WA1", z, [128, 2, 3, 256]), [128, 4, 256])
    z = m.put("WA", z, [128, 2, 3, 512])
    zmax = z
    zw = m.put("WDEC", z, [33, 1024])
    for i in range(4):
        m.put(f"BUF{i}", C + 4096 * i, [128, 4, 256])
    m.put("BUF4", zw, [128, 4, 256])
    m.put("ABH", Z, [128, 8, 512], F32R)
    e = m.put("ABL", Z + 16384, [128, 8, 512], F32R)
    e = m.put("ZB", e, [128, 2, 512])
    m.t["end2"] = max(e, zw + 4096)
    qq = m.put("QNB", v, [128, 4, 512])
    m.put("QT2", v + 8192, [128, 512])
    m.put("SQ3", v + 10240, [128, 512])
    p = m.put("YN", C + 16384, [128, 2, 1024])
    p = m.put("QKN", p, [128, 2, 2, 512])
    p = m.put("VN", p, [128, 2, 1024])
    qkt_at = p
    p = m.put("QKT", p, [128, 16, 256])
    p = m.put("BIAS", p, [128, 12, 384])
    m.put("MASKF", p, [128, 7 * 128])
    p = m.put("E3", p, [128, 4, 384])
    p = m.put("PT3", p, [128, 2, 384])
    p = m.put("XN1", p, [128, 2, 1024])
    p = m.put("DG1", p, [128, 2, 128])
    p = m.put("SQ", p, [128, 2, 512])
    p = m.put("AROW1", p, [2, 512])
    p = m.put("SQY", p, [128, 512])
    p = m.put("QSY", p, [128, 2, 4])
    p = m.put("QS", p, [128, 2, 16])
    p = m.put("RR", p, [128, 4, 32])
    p = m.put("SM", p, [128, 16])
    p = m.put("LT", p, [128, 64])
    p = m.put("LAMR", p, [128, 512])
    m.put("FT", m.put("FC", qkt_at, [128, 2, 2, 256]), [128, 2, 256])
    p = m.put("AH", p, [128, 3, 256], F32R)
    p = m.put("AL", p, [128, 3, 256], F32R)
    x1 = m.put("OH", C + 16384, [32, 384])
    x1 = m.put("RB", x1, [32, 12])
    x1 = m.put("MROW", x1, [12, 384])
    x1 = m.put("RROW", x1, [12, 384])
    top = max(p, m.t.pop("end2"))
    assert base + top <= nc.sbuf_usable_end
    sb = m.t

    names = ["pe", "act", "dve", "pool", "sp"] + [f"raw{i}" for i in range(5)] + \
        ["ada0", "ada1", "ada2", "cst", "cst2", "par", "bias",  "xs", "sp0", "sp1", "gd", "td", "wd", "rdl", "out"]
    sems = {n: nc.alloc_semaphore("s_" + n) for n in names}
    banks = [nc.alloc_psum_tensor(f"pb{i}", [128, 512], F32) for i in range(8)]
    order, _ = program(nc, None, args, sems, sb, banks, out)
    _, E = program(nc, order, args, sems, sb, banks, out)

    with nc.Block() as block:
        @block.sync
        def _(eng):
            for f in E["sp"].todo:
                f(eng)

        @block.scalar
        def _(eng):
            for f in E["act"].todo:
                f(eng)

        @block.vector
        def _(eng):
            for f in E["dve"].todo:
                f(eng)

        @block.gpsimd
        def _(eng):
            for f in E["pool"].todo:
                f(eng)

        @block.tensor
        def _(eng):
            for f in E["pe"].todo:
                f(eng)


def shape_constants():
    ident = np.eye(128, dtype=np.float32)
    s, t = np.arange(128)[:, None], np.arange(128)[None, :]
    tri = np.concatenate([(s <= t), np.ones((128, 128)), (s >= t)], axis=1).astype(np.float32) / np.float32(16)
    masks = []
    for h in LEVELS:
        masks.append((s // (2 * h) == t // (2 * h)) & (s // h != t // h))
    mask = np.concatenate(masks, axis=1).astype(np.float32)
    bucket = np.searchsorted(np.array(BUCKET_STARTS), np.arange(256), side="right") - 1
    onehot = np.zeros((32, 384), np.float32)
    for i in range(256):
        onehot[bucket[255 - i], i] = 1.0
    maskrow = np.zeros((12, 384), np.float32)
    maskrow[:, 256:] = -1e30
    pos = np.arange(256)
    fr = (10000.0 ** (-np.arange(32, dtype=np.float32) * 2.0 / 64)).astype(np.float32)
    ang = np.stack([(pos // 64).astype(np.float32)[:, None] * fr, (pos % 64).astype(np.float32)[:, None] * fr], 1)
    c, sn = np.cos(ang), np.sin(ang)
    Ct = np.stack([c, c], axis=2).reshape(256, 128)
    St = np.stack([-sn, sn], axis=2).reshape(256, 128)
    rope = np.stack([Ct, St]).reshape(2, 2, 128, 128).transpose(2, 0, 1, 3).astype(np.float32)
    return dict(ident=ident, tri=tri, mask=mask, onehot=onehot, maskrow=maskrow, rope=np.ascontiguousarray(rope))


def lay_out(inp):
    i = {k: np.asarray(v) for k, v in inp.items()}
    d = shape_constants()

    def T(w):
        return np.ascontiguousarray(w.reshape(8, 128, -1, 128).transpose(2, 1, 0, 3)).reshape(-1, 128, 1024)

    def N(w):
        k, c = w.shape
        return np.ascontiguousarray(w.reshape(k // 256, 2, 128, c // 512, 512).transpose(3, 0, 2, 1, 4)).reshape(-1, 128, 1024)

    def cols(a):
        return a.reshape(-1, 128).T
    for l in range(2):
        d[f"w_in{l}"] = N(i["w_in"][l])
        d[f"w_out{l}"] = N(i["w_out"][l])
        d[f"w_up{l}"] = T(i["w_up"][l])
        d[f"w_down{l}"] = i["w_down"][l].reshape(FF_TILES, 128, 1024)
        w = i["w_in_2"][l]
        d[f"wa{l}"] = T(w[:, 0:4096])
        d[f"wq{l}"] = N(w[:, 4096:5120])
        d[f"wkv{l}"] = N(w[:, 5120:5632])
        d[f"wzb{l}"] = T(w[:, 5632:6656])
        d[f"wgq{l}"] = T(w[:, 6656:7168])
        d[f"wgk{l}"] = T(w[:, 7168:7680])
        d[f"wgv{l}"] = N(w[:, 7680:8704])
        d[f"wr{l}"] = np.ascontiguousarray(w[:, 8704:8736].reshape(8, 128, 32).transpose(1, 0, 2)).reshape(1, 128, 256)
        d[f"wzc{l}"] = T(w[:, 8736:9760])
        d[f"wmg{l}"] = T(w[:, 9760:12832])
        d[f"wbr{l}"] = np.concatenate([T(i[n][l]) for n in ("w_br_conv_2", "w_br_attn_2", "w_br_gla_2")])
        d[f"wo2{l}"] = N(i["w_out_2"][l])
    d["w_ada"] = np.concatenate([N(i["w_ada_2"][l]) for l in range(2)])
    wdec = np.zeros((2, 33, 1024), np.float32)
    wdec[:, 0:16, 0:512] = i["w_decay_fwd_2"]
    wdec[:, 16:32, 512:1024] = i["w_decay_bwd_2"]
    wdec[:, 32, 0:512] = i["b_decay_fwd_2"]
    wdec[:, 32, 512:1024] = i["b_decay_bwd_2"]
    d["wdec"] = wdec
    qk = i["qk_norm_g"]
    d["par"] = np.ascontiguousarray(np.concatenate([
        cols(i["ln_attn_g"]), cols(i["ln_ffn_g"]), cols(np.concatenate([qk, qk], axis=-1)), cols(i["diff_subln_g"]),
        cols(i["conv_w"]), cols(i["conv_b"]),
        np.stack([i["c_2"][0].reshape(8, 128), i["c_ctx_2"].reshape(8, 128)], axis=1).reshape(16, 128).T,
        cols(i["b_ada_2"]), cols(i["g_pre_2"]), cols(i["g_post_2"]), cols(i["conv_w_2"]), cols(i["gla_norm_g_2"]),
        cols(i["b_gate_2"])], axis=1))
    d["lamr"] = np.ascontiguousarray(np.broadcast_to(i["diff_lambda"].reshape(1, 512), (128, 512)))
    d["qkn"] = np.ascontiguousarray(np.stack([i["q_norm_g_2"], i["k_norm_g_2"]], axis=1).reshape(4, 128))
    d["rel_bias"] = i["rel_bias"]
    d["x"] = i["x"]
    d["ctx"] = i["ctx_2"]
    return d


def kernel(**inputs):
    import concourse.bacc as bacc
    from concourse.bass_utils import run_bass_kernel_spmd

    nc = bacc.Bacc("TRN2", target_bir_lowering=False, num_devices=1)
    arrays, args = {}, {}
    for name, a in lay_out(inputs).items():
        a = np.ascontiguousarray(a)
        arrays["in_" + name] = a
        args[name] = nc.dram_tensor("in_" + name, a.shape, mybir.dt.from_np(a.dtype), kind="ExternalInput").ap()
    args["rscr"] = nc.dram_tensor("rscr", (12, 128, 384), F32, kind="Internal").ap()
    args["xscr"] = nc.dram_tensor("xscr", (1, 512, 1024), F32, kind="Internal").ap()
    out = nc.dram_tensor("out0", (1, 256, 1024), F32, kind="ExternalOutput").ap()
    build(nc, args, out)
    r = run_bass_kernel_spmd(nc, [arrays], core_ids=[0])
    return r.results[0]["out0"]
```
